# Optimizing a Trainium2 kernel written in Bass

```python
import jax, jax.numpy as jnp
from jax import lax
import numpy as np

D_MODEL = 1024
BATCH = 1
SEQ = 1024
DEPTH = 2

HEAD_DIM = 64
RET_HEADS = 8
NSA_HEADS = 8
NSA_KV_GROUPS = 2
NSA_GROUP_SIZE = NSA_HEADS // NSA_KV_GROUPS
RET_W = RET_HEADS * HEAD_DIM
NSA_W = NSA_HEADS * HEAD_DIM
NSA_KV_W = NSA_KV_GROUPS * HEAD_DIM
N_BRANCHES = 3
EVEN_IN_W = 4 * RET_W + NSA_W + 2 * N_BRANCHES * NSA_KV_W + NSA_HEADS * N_BRANCHES
RET_CHUNK = 128
CMP_STRIDE = 16
CMP_BLOCK = 2 * CMP_STRIDE
CMP_HIDDEN = 128
SEL_BLOCK = 64
TOP_N = 8
WINDOW = 256
NSA_QBLOCK = 64
CONV_WIDTH = 3
N_GROUPS = 4
EXPERTS_PER_GROUP = 8
N_EXPERTS = N_GROUPS * EXPERTS_PER_GROUP
TOP_K_IN_GROUP = 2
D_EXPERT = 256
MOE_ROW_BLOCK = 256
N_EVEN = (DEPTH + 1) // 2
N_ODD = DEPTH // 2
RMS_EPS = 1e-6
NEG_INF = -1e30
F32 = jnp.float32

kernel_name = "hybrid_retention_nsa_shortconv_hmoe"

def rms_norm(x, g):
    xf = x.astype(F32)
    y = xf * lax.rsqrt(jnp.mean(xf * xf, axis=-1, keepdims=True) + RMS_EPS)
    return (y * g.astype(F32)).astype(x.dtype)

def masked_softmax(scores, mask):
    s = jnp.where(mask, scores.astype(F32), NEG_INF)
    m = jnp.max(s, axis=-1, keepdims=True)
    p = jnp.where(mask, jnp.exp(s - m), 0.0)
    return p / jnp.maximum(jnp.sum(p, axis=-1, keepdims=True), 1e-30)

def alibi_slopes(n_heads):
    return 2.0 ** (-8.0 * jnp.arange(1, n_heads + 1, dtype=F32) / n_heads)

def retention(q, k, v):
    b, h, s, d = q.shape
    nc = s // RET_CHUNK
    log_g = jnp.log(1.0 - 2.0 ** (-5.0 - jnp.arange(h, dtype=F32)))
    pos = jnp.arange(RET_CHUNK, dtype=F32)
    diff = pos[:, None] - pos[None, :]
    decay = jnp.where(diff >= 0, jnp.exp(log_g[:, None, None] * jnp.maximum(diff, 0.0)), 0.0)
    q_c = q.reshape(b, h, nc, RET_CHUNK, d)
    k_c = k.reshape(b, h, nc, RET_CHUNK, d) * (d ** -0.5)
    v_c = v.reshape(b, h, nc, RET_CHUNK, d)
    scores = jnp.einsum('bhcid,bhcjd->bhcij', q_c, k_c) * decay[None, :, None]
    y_intra = jnp.einsum('bhcij,bhcje->bhcie', scores, v_c)
    k_decay = jnp.exp(log_g[:, None] * (RET_CHUNK - 1 - pos))[None, :, None, :, None]
    q_decay = jnp.exp(log_g[:, None] * (pos + 1.0))[None, :, None, :, None]
    chunk_kv = jnp.einsum('bhcjd,bhcje->cbhde', k_c * k_decay, v_c)
    chunk_decay = jnp.exp(log_g * RET_CHUNK)[None, :, None, None]

    def step(state, kv):
        return chunk_decay * state + kv, state

    _, prev_states = lax.scan(step, jnp.zeros((b, h, d, d), chunk_kv.dtype), chunk_kv)
    y_inter = jnp.einsum('bhcid,cbhde->bhcie', q_c * q_decay, prev_states)
    return (y_intra + y_inter).reshape(b, h, s, d)

def compress_blocks(x, pe, w1, w2):
    b, g, s, d = x.shape
    chunks = x.reshape(b, g, s // CMP_STRIDE, CMP_STRIDE, d)
    blocks = jnp.concatenate([chunks[:, :, :-1], chunks[:, :, 1:]], axis=3) + pe
    flat = blocks.reshape(b, g, blocks.shape[2], CMP_BLOCK * d)
    return jax.nn.gelu(flat @ w1) @ w2

def native_sparse_attention(q, kc, vc, ks, vs, kw, vw, gates, cmp_pe, w_cmp1, w_cmp2,
                            q_norm_g, k_norm_g):
    b, s = q.shape[:2]
    G, R, d = NSA_KV_GROUPS, NSA_GROUP_SIZE, HEAD_DIM
    QB = NSA_QBLOCK
    scale = d ** -0.5
    slopes = alibi_slopes(NSA_HEADS).reshape(G, R)[None, :, :, None, None]
    q = rms_norm(q, q_norm_g).transpose(0, 2, 1, 3).reshape(b, G, R, s, d)
    kc, vc, ks, vs, kw, vw = [t.transpose(0, 2, 1, 3) for t in (kc, vc, ks, vs, kw, vw)]
    t_pos = jnp.arange(s)

    k_cmp = rms_norm(compress_blocks(kc, cmp_pe[0], w_cmp1[0], w_cmp2[0]), k_norm_g[0])
    v_cmp = compress_blocks(vc, cmp_pe[1], w_cmp1[1], w_cmp2[1])
    n_cmp = k_cmp.shape[2]
    cmp_start = jnp.arange(n_cmp) * CMP_STRIDE
    dist_cmp = t_pos[:, None] - (cmp_start + CMP_BLOCK - 1)[None, :]
    sc = jnp.einsum('bgrqd,bgnd->bgrqn', q, k_cmp) * scale - slopes * dist_cmp.astype(F32)
    p_cmp = masked_softmax(sc, dist_cmp >= 0)
    o_cmp = jnp.einsum('bgrqn,bgnd->bgrqd', p_cmp.astype(v_cmp.dtype), v_cmp)

    n_sel = s // SEL_BLOCK
    top_n = min(TOP_N, n_sel)
    sel_ids = jnp.arange(n_sel)
    sel_start = sel_ids * SEL_BLOCK
    overlap = ((cmp_start[:, None] < sel_start[None, :] + SEL_BLOCK)
               & (cmp_start[:, None] + CMP_BLOCK > sel_start[None, :])).astype(F32)
    imp = jnp.einsum('bgrqn,nj->bgqj', p_cmp, overlap)
    q_blk = t_pos // SEL_BLOCK
    valid = sel_start[None, :] <= t_pos[:, None]
    forced = ((sel_ids[None, :] == 0) | (sel_ids[None, :] == q_blk[:, None])
              | (sel_ids[None, :] == q_blk[:, None] - 1))
    imp = jnp.where(forced, imp + 1e3, jnp.where(valid, imp, -1e3))
    _, sel_idx = lax.top_k(imp, top_n)

    ks_blocks = rms_norm(ks, k_norm_g[1]).reshape(b, G, n_sel, SEL_BLOCK, d)
    vs_blocks = vs.reshape(b, G, n_sel, SEL_BLOCK, d)
    pad = ((0, 0), (0, 0), (WINDOW, 0), (0, 0))
    kw_pad = jnp.pad(rms_norm(kw, k_norm_g[2]), pad)
    vw_pad = jnp.pad(vw, pad)
    nq = s // QB
    q_blocks = q.reshape(b, G, R, nq, QB, d).transpose(3, 0, 1, 2, 4, 5)
    idx_blocks = sel_idx.reshape(b, G, nq, QB, top_n).transpose(2, 0, 1, 3, 4)
    b_ar = jnp.arange(b)[:, None, None, None]
    g_ar = jnp.arange(G)[None, :, None, None]
    sel_off = jnp.arange(SEL_BLOCK)
    win_off = jnp.arange(WINDOW + QB)

    def sparse_block(args):
        qb, idx, i = args
        t = i * QB + jnp.arange(QB)
        k_sel = ks_blocks[b_ar, g_ar, idx]
        v_sel = vs_blocks[b_ar, g_ar, idx]
        s_pos = idx[..., None] * SEL_BLOCK + sel_off
        d_sel = (t[:, None, None] - s_pos)[:, :, None]
        sc_s = (jnp.einsum('bgrqd,bgqnkd->bgrqnk', qb, k_sel) * scale
                - slopes[..., None] * d_sel.astype(F32))
        m_sel = top_n * SEL_BLOCK
        p_s = masked_softmax(sc_s.reshape(b, G, R, QB, m_sel), (d_sel >= 0).reshape(b, G, 1, QB, m_sel))
        o_s = jnp.einsum('bgrqm,bgqmd->bgrqd', p_s.astype(v_sel.dtype), v_sel.reshape(b, G, QB, m_sel, d))
        k_win = lax.dynamic_slice_in_dim(kw_pad, i * QB, WINDOW + QB, axis=2)
        v_win = lax.dynamic_slice_in_dim(vw_pad, i * QB, WINDOW + QB, axis=2)
        w_pos = i * QB - WINDOW + win_off
        d_win = t[:, None] - w_pos[None, :]
        mask = (d_win >= 0) & (d_win < WINDOW) & (w_pos[None, :] >= 0)
        sc_w = jnp.einsum('bgrqd,bgkd->bgrqk', qb, k_win) * scale - slopes * d_win.astype(F32)
        p_w = masked_softmax(sc_w, mask)
        o_w = jnp.einsum('bgrqk,bgkd->bgrqd', p_w.astype(v_win.dtype), v_win)
        return o_s, o_w

    o_sel, o_win = lax.map(sparse_block, (q_blocks, idx_blocks, jnp.arange(nq)))
    o_sel = o_sel.transpose(1, 2, 3, 0, 4, 5).reshape(b, G, R, s, d)
    o_win = o_win.transpose(1, 2, 3, 0, 4, 5).reshape(b, G, R, s, d)

    gt = jax.nn.sigmoid(gates).transpose(0, 2, 1, 3).reshape(b, G, R, s, N_BRANCHES)
    o = gt[..., 0:1] * o_cmp + gt[..., 1:2] * o_sel + gt[..., 2:3] * o_win
    return o.transpose(0, 3, 1, 2, 4).reshape(b, s, NSA_W)

def even_mixer(xn, w_in, cmp_pe, w_cmp1, w_cmp2, q_norm_g, k_norm_g, ret_norm_g, w_out):
    b, s, _ = xn.shape
    sizes = [RET_W] * 4 + [NSA_W] + [NSA_KV_W] * (2 * N_BRANCHES) + [NSA_HEADS * N_BRANCHES]
    cuts = [int(c) for c in np.cumsum(sizes)[:-1]]
    rq, rk, rv, rg, nq_, kc, vc, ks, vs, kw, vw, ng = jnp.split(xn @ w_in, cuts, axis=-1)
    heads = lambda t, h: t.reshape(b, s, h, HEAD_DIM)
    y_ret = retention(*[heads(t, RET_HEADS).transpose(0, 2, 1, 3) for t in (rq, rk, rv)])
    y_ret = rms_norm(y_ret, ret_norm_g).transpose(0, 2, 1, 3).reshape(b, s, RET_W) * jax.nn.silu(rg)
    y_nsa = native_sparse_attention(
        heads(nq_, NSA_HEADS), *[heads(t, NSA_KV_GROUPS) for t in (kc, vc, ks, vs, kw, vw)],
        ng.reshape(b, s, NSA_HEADS, N_BRANCHES), cmp_pe, w_cmp1, w_cmp2, q_norm_g, k_norm_g)
    return jnp.concatenate([y_ret, y_nsa], axis=-1) @ w_out

def odd_mixer(xn, w_in, conv_w, conv_b, w_out):
    gate_b, gate_c, h = jnp.split(xn @ w_in, 3, axis=-1)
    u = gate_c * h
    y = lax.conv_general_dilated(u, conv_w[:, None, :], window_strides=(1,),
                                 padding=[(CONV_WIDTH - 1, 0)],
                                 dimension_numbers=('NWC', 'WIO', 'NWC'),
                                 feature_group_count=u.shape[-1]) + conv_b
    return (gate_b * y) @ w_out

def hierarchical_moe(xn, wg_group, bg_group, wg_expert, bg_expert, w_gate, w_up, w_down):
    b, s, d = xn.shape
    n_tok = b * s
    x_tok = xn.reshape(n_tok, d)
    xf = x_tok.astype(F32)
    grp_prob = jax.nn.softmax(xf @ wg_group.astype(F32) + bg_group.astype(F32), axis=-1)
    grp_p, grp_idx = lax.top_k(grp_prob, 1)
    e_logits = (xf @ wg_expert.astype(F32) + bg_expert.astype(F32)).reshape(n_tok, N_GROUPS, EXPERTS_PER_GROUP)
    in_grp = jnp.take_along_axis(e_logits, grp_idx[:, :, None], axis=1)[:, 0]
    top_p, top_local = lax.top_k(jax.nn.softmax(in_grp, axis=-1), TOP_K_IN_GROUP)
    gate = grp_p * top_p / jnp.sum(top_p, axis=-1, keepdims=True)
    expert_id = grp_idx * EXPERTS_PER_GROUP + top_local

    n_slot = n_tok * TOP_K_IN_GROUP
    flat_e = expert_id.reshape(-1)
    order = jnp.argsort(flat_e)
    e_sorted = flat_e[order]
    tok_sorted = (jnp.arange(n_slot) // TOP_K_IN_GROUP)[order]
    gate_sorted = gate.reshape(-1)[order]
    counts = jax.ops.segment_sum(jnp.ones_like(flat_e), flat_e, num_segments=N_EXPERTS)
    padded = (counts + MOE_ROW_BLOCK - 1) // MOE_ROW_BLOCK * MOE_ROW_BLOCK
    start = jnp.cumsum(counts) - counts
    pend = jnp.cumsum(padded)
    dest = (pend - padded)[e_sorted] + (jnp.arange(n_slot) - start[e_sorted])
    n_blocks = -(-n_slot // MOE_ROW_BLOCK) + N_EXPERTS
    buf = jnp.zeros((n_blocks * MOE_ROW_BLOCK, d), xn.dtype).at[dest].set(x_tok[tok_sorted])
    block_expert = jnp.minimum(
        jnp.searchsorted(pend, jnp.arange(n_blocks) * MOE_ROW_BLOCK, side='right'), N_EXPERTS - 1)

    def expert_block(args):
        xb, e = args
        return (jax.nn.silu(xb @ w_gate[e]) * (xb @ w_up[e])) @ w_down[e]

    y_buf = lax.map(expert_block, (buf.reshape(n_blocks, MOE_ROW_BLOCK, d), block_expert)).reshape(-1, d)
    y = jnp.zeros_like(x_tok).at[tok_sorted].add(y_buf[dest] * gate_sorted[:, None].astype(y_buf.dtype))
    return y.reshape(b, s, d)

def setup_inputs(seed: int = 0) -> dict:
    key = jax.random.key(seed)
    k = jax.random.split(key, 24)
    nrm = lambda kk, shape, sc: jax.random.normal(kk, shape, F32) * sc
    d = HEAD_DIM
    return {
        "x": nrm(k[0], (BATCH, SEQ, D_MODEL), 1.0),
        "mix_norm_g": 1.0 + nrm(k[1], (DEPTH, D_MODEL), 0.02),
        "ffn_norm_g": 1.0 + nrm(k[2], (DEPTH, D_MODEL), 0.02),
        "ev_w_in": nrm(k[3], (N_EVEN, D_MODEL, EVEN_IN_W), D_MODEL ** -0.5),
        "ev_cmp_pe": nrm(k[4], (N_EVEN, 2, CMP_BLOCK, d), 0.1),
        "ev_w_cmp1": nrm(k[5], (N_EVEN, 2, CMP_BLOCK * d, CMP_HIDDEN), (CMP_BLOCK * d) ** -0.5),
        "ev_w_cmp2": nrm(k[6], (N_EVEN, 2, CMP_HIDDEN, d), CMP_HIDDEN ** -0.5),
        "ev_q_norm_g": 1.0 + nrm(k[7], (N_EVEN, d), 0.02),
        "ev_k_norm_g": 1.0 + nrm(k[8], (N_EVEN, N_BRANCHES, d), 0.02),
        "ev_ret_norm_g": 1.0 + nrm(k[9], (N_EVEN, d), 0.02),
        "ev_w_out": nrm(k[10], (N_EVEN, RET_W + NSA_W, D_MODEL), (RET_W + NSA_W) ** -0.5),
        "od_w_in": nrm(k[11], (N_ODD, D_MODEL, 3 * D_MODEL), D_MODEL ** -0.5),
        "od_conv_w": nrm(k[12], (N_ODD, CONV_WIDTH, D_MODEL), CONV_WIDTH ** -0.5),
        "od_conv_b": nrm(k[13], (N_ODD, D_MODEL), 0.01),
        "od_w_out": nrm(k[14], (N_ODD, D_MODEL, D_MODEL), D_MODEL ** -0.5),
        "moe_wg_group": nrm(k[15], (DEPTH, D_MODEL, N_GROUPS), D_MODEL ** -0.5),
        "moe_bg_group": nrm(k[16], (DEPTH, N_GROUPS), 0.01),
        "moe_wg_expert": nrm(k[17], (DEPTH, D_MODEL, N_EXPERTS), D_MODEL ** -0.5),
        "moe_bg_expert": nrm(k[18], (DEPTH, N_EXPERTS), 0.01),
        "moe_w_gate": nrm(k[19], (DEPTH, N_EXPERTS, D_MODEL, D_EXPERT), D_MODEL ** -0.5),
        "moe_w_up": nrm(k[20], (DEPTH, N_EXPERTS, D_MODEL, D_EXPERT), D_MODEL ** -0.5),
        "moe_w_down": nrm(k[21], (DEPTH, N_EXPERTS, D_EXPERT, D_MODEL), D_EXPERT ** -0.5),
    }

def reference(x, mix_norm_g, ffn_norm_g, ev_w_in, ev_cmp_pe, ev_w_cmp1, ev_w_cmp2,
              ev_q_norm_g, ev_k_norm_g, ev_ret_norm_g, ev_w_out, od_w_in, od_conv_w,
              od_conv_b, od_w_out, moe_wg_group, moe_bg_group, moe_wg_expert,
              moe_bg_expert, moe_w_gate, moe_w_up, moe_w_down):
    h = x
    for layer in range(DEPTH):
        i = layer // 2
        xn = rms_norm(h, mix_norm_g[layer])
        if layer % 2 == 0:
            h = h + even_mixer(xn, ev_w_in[i], ev_cmp_pe[i], ev_w_cmp1[i], ev_w_cmp2[i],
                               ev_q_norm_g[i], ev_k_norm_g[i], ev_ret_norm_g[i], ev_w_out[i])
        else:
            h = h + odd_mixer(xn, od_w_in[i], od_conv_w[i], od_conv_b[i], od_w_out[i])
        xn = rms_norm(h, ffn_norm_g[layer])
        h = h + hierarchical_moe(xn, moe_wg_group[layer], moe_bg_group[layer],
                                 moe_wg_expert[layer], moe_bg_expert[layer],
                                 moe_w_gate[layer], moe_w_up[layer], moe_w_down[layer])
    return h


_drawn_inputs = setup_inputs


def setup_inputs(seed=0):
    import zlib

    import numpy as np

    out = dict(_drawn_inputs(seed))
    spreads = {}
    factors = {'ev_q_norm_g': 3.473, 'ev_k_norm_g': 3.525, 'od_conv_b': 3.837, 'moe_bg_group': 3.819}
    for name, (base, spread) in spreads.items():
        noise = np.random.default_rng([zlib.crc32(name.encode()), seed]).standard_normal(out[name].shape)
        drawn = base * np.exp(spread * noise) if base else spread * noise
        out[name] = __import__('jax').numpy.asarray(drawn.astype(out[name].dtype))
    for name, factor in factors.items():
        out[name] = (out[name] * factor).astype(out[name].dtype)
    return out
```

```python
import numpy as np
import concourse.bass as bass
from concourse import mybir
from contextlib import ExitStack

F32 = mybir.dt.float32
F32R = mybir.dt.float32r
BF16 = mybir.dt.bfloat16
I32 = mybir.dt.int32
ALU = mybir.AluOpType
ACT = mybir.ActivationFunctionType
X = mybir.AxisListType.X
ds = bass.ds

P = 128
S = 1024
D = 1024
NT = S // P
KT = D // P
HD = 64
RH = 8
NH = 8
G = 2
R = NH // G
RET_W = RH * HD
NSA_W = NH * HD
KV_W = G * HD
N_BRANCH = 3
IN_W = 4 * RET_W + NSA_W + 6 * KV_W + NH * N_BRANCH
C_NQ = 4 * RET_W
C_KC = C_NQ + NSA_W
C_VC, C_KS, C_VS, C_KW, C_VW, C_NG = (C_KC + KV_W * n for n in range(1, 7))
CMP_STRIDE = 16
CMP_HID = 128
NC_ = S // CMP_STRIDE
SEL = 64
NS = S // SEL
WINDOW = 256
NG = 4
EPG = 8
NE = NG * EPG
DE = 256
EPS = 1e-6
NEG = -1e30
COLS = 512


class Pool_:

    def __init__(self, nc, name):
        self.nc, self.name, self.ctx, self.used = nc, name, ExitStack(), []

    def __enter__(self):
        return self

    def __exit__(self, *a):
        if self.used and a[0] is None:
            self.nc.clear_and_free_semaphores(self.used)
            self.nc.all_engine_barrier()
        return self.ctx.__exit__(*a)

    def sb(self, name, shape, dt=F32):
        return self.ctx.enter_context(self.nc.sbuf_tensor(f"{self.name}_{name}", shape, dt))

    def ps(self, name, shape, dt=F32):
        return self.ctx.enter_context(self.nc.psum_tensor(f"{self.name}_{name}", shape, dt))

    def sem(self, name):
        self.used.append(self.nc.alloc_semaphore(f"{self.name}_{name}"))
        return self.used[-1]

    def sems(self, name, n=2):
        return [self.sem(f"{name}{j}") for j in range(n)]


def row_of(vec, n=P):
    return bass.AP(tensor=vec.tensor, offset=vec.offset, ap=[[0, n]] + [list(x) for x in vec.ap])


def norm_transpose(nc, name, src, ident, xT_hi, xT_lo=None, gain=None, xn_dram=None, mix=None):
    with Pool_(nc, name) as m:
        xin = m.sb("xin", [P, 2, D])
        ps_t = m.ps("ps_t", [P, 2, KT, P])
        loaded, mixed, stored = m.sems("loaded"), m.sems("mixed"), m.sems("stored")
        summed, root_ready, normed = m.sems("summed"), m.sems("root_ready"), m.sems("normed")
        transposed, hi_ready, lo_ready = m.sems("transposed"), m.sems("hi_ready"), m.sems("lo_ready")
        gain_loaded = m.sem("gain_loaded")
        apart = m.sem("apart")
        if gain is not None:
            gains = m.sb("gains", [P, D])
            xn = m.sb("xn", [P, 2, D])
            sq = m.sb("sq", [P, 2, D])
            ssq = m.sb("ssq", [P, 2])
            root = m.sb("root", [P, 2])
            rstd = m.sb("rstd", [P, 2])
            eps = m.sb("eps", [P, 1])
            eps_ready = m.sem("eps_ready")
        if mix is not None:
            slots, gates, mix_out = mix
            ya = m.sb("ya", [P, 2, 2, D])
        rows = xn if gain is not None else xin
        n_stores = (mix is not None) + (xn_dram is not None)

        with nc.Block() as block:
            @block.sync
            def _(sp):
                if gain is not None:
                    sp.dma_start(gains[:], row_of(gain)).then_inc(gain_loaded, 16)
                with sp.Fori(0, NT // 2) as i:
                    for u in range(2):
                        first, second = sp.snap((2 * i + u) * P), sp.snap((2 * i + u) * P + S)
                        stores = sp.snap(i * (16 * n_stores)) if mix is not None else None
                        sp.wait_ge(transposed[u], i)
                        if mix is not None:
                            sp.sem_inc(apart, 1)
                            sp.wait_ge(stored[u], stores)
                        sp.dma_start(xin[:, u, :], src[ds(first, P), :]).then_inc(loaded[u], 16)
                        if mix is not None:
                            for c, row in enumerate((first, second)):
                                sp.dma_start(ya[:, u, c, :], slots[ds(row, P), :]
                                             ).then_inc(loaded[u], 16)
                    for u in range(2):
                        first = sp.snap((2 * i + u) * P)
                        if mix is not None:
                            sp.wait_ge(mixed[u], i + 1)
                            sp.dma_start(mix_out[ds(first, P), :], xin[:, u, :]).then_inc(stored[u], 16)
                        if xn_dram is not None:
                            sp.wait_ge(normed[u], i + 1)
                            sp.dma_start(xn_dram[ds(first, P), :], xn[:, u, :]).then_inc(stored[u], 16)
                if n_stores:
                    for u in range(2):
                        sp.wait_ge(stored[u], 16 * n_stores * (NT // 2))

            @block.scalar
            def _(act):
                if gain is not None:
                    act.wait_ge(eps_ready, 1)
                with act.Fori(0, NT // 2) as i:
                    if gain is not None:
                        for u in range(2):
                            if mix is None:
                                act.wait_ge(loaded[u], 16 * i + 16)
                            else:
                                act.wait_ge(mixed[u], i + 1)
                            act.activation(sq[:, u, :], xin[:, u, :], ACT.Square,
                                           accum_out=ssq[:, u:u + 1]).then_inc(summed[u], 1)
                            act.wait_ge(summed[u], i + 1)
                            act.wait_ge(normed[u], i)
                            act.activation(root[:, u:u + 1], ssq[:, u:u + 1], ACT.Sqrt, bias=eps[:],
                                           scale=1.0 / D).then_inc(root_ready[u], 1)
                    for u in range(2):
                        act.wait_ge(transposed[u], i + 1)
                        act.activation(xT_hi[:, :, ds((2 * i + u) * P, P)], ps_t[:, u, :, :],
                                       ACT.Copy).then_inc(hi_ready[u], 1)

            @block.vector
            def _(dve):
                if gain is not None:
                    dve.memset(eps[:], EPS).then_inc(eps_ready, 1)
                    dve.wait_ge(gain_loaded, 16)
                with dve.Fori(0, NT // 2) as i:
                    for u in range(2):
                        if mix is not None:
                            dve.wait_ge(loaded[u], 48 * i + 48)
                            for c in range(2):
                                last = dve.scalar_tensor_tensor(
                                    xin[:, u, :], ya[:, u, c, :], gates[:, ds(2 * i + (u + c * NT), 1)],
                                    xin[:, u, :], ALU.mult, ALU.add)
                                if c == 1:
                                    last.then_inc(mixed[u], 1)
                                dve.drain()
                    for u in range(2):
                        if gain is not None:
                            dve.wait_ge(root_ready[u], i + 1)
                            dve.reciprocal(rstd[:, u:u + 1], root[:, u:u + 1])
                            dve.drain()
                            dve.wait_ge(transposed[u], i)
                            if xn_dram is not None:
                                dve.wait_ge(stored[u], 16 * n_stores * i)
                            dve.scalar_tensor_tensor(xn[:, u, :], xin[:, u, :], rstd[:, u:u + 1], gains[:],
                                                     ALU.mult, ALU.mult).then_inc(normed[u], 1)
                    for u in range(2):
                        if xT_lo is not None:
                            dve.wait_ge(hi_ready[u], i + 1)
                            at = ds((2 * i + u) * P, P)
                            dve.tensor_tensor(xT_lo[:, :, at], ps_t[:, u, :, :], xT_hi[:, :, at].bitcast(F32),
                                              ALU.subtract).then_inc(lo_ready[u], 1)

            @block.tensor
            def _(pe):
                with pe.Fori(0, NT // 2) as i:
                    for u in range(2):
                        pe.wait_ge(*((normed[u], i + 1) if gain is not None else (loaded[u], 16 * i + 16)))
                        pe.wait_ge(*((lo_ready[u], i) if xT_lo is not None else (hi_ready[u], i)))
                        for k in range(KT):
                            last = pe.transpose(ps_t[:, u, k, :], rows[:, u, k * P:(k + 1) * P], ident[:])
                        last.then_inc(transposed[u], 1)


def project(nc, name, xT_hi, xT_lo, w, width, out, residual=None):
    full = width // COLS
    with Pool_(nc, name) as m:
        raw = m.sb("raw", [P, 2, KT, COLS])
        w_hi = m.sb("w_hi", [P, 2, KT, COLS], F32R)
        w_lo = m.sb("w_lo", [P, 2, KT, COLS], F32R)
        stage = m.sb("stage", [P, 4, COLS])
        ps = m.ps("ps", [P, NT, COLS])
        raw_loaded = m.sems("raw_loaded", 4)
        hi_ready, lo_ready = m.sems("hi_ready"), m.sems("lo_ready")
        product_ready = m.sems("product_ready", NT - 1)
        last_product = m.sems("last_product")
        tile_out = m.sems("tile_out", NT)
        stage_stored = m.sems("stage_stored", 4)
        res_loaded = m.sems("res_loaded", 4)
        if residual is not None:
            res = m.sb("res", [P, 4, COLS])
        w_k = w.rearrange("(k p) n -> p k n", p=P)

        n_blocks = -(-width // COLS)
        wide = [min(COLS, width - b * COLS) for b in range(n_blocks)]
        HALF = KT // 2

        with nc.Block() as block:
            @block.sync
            def _(sp):
                for b, n in enumerate(wide):
                    if b >= 2:
                        sp.wait_ge(lo_ready[b % 2], 2 * (b // 2))
                    for c in range(2):
                        at = slice(c * HALF, (c + 1) * HALF)
                        sp.dma_start(raw[:, b % 2, at, 0:n], w_k[:, at, b * COLS:b * COLS + n]
                                     ).then_inc(raw_loaded[2 * (b % 2) + c], 16)
                for s in range(4):
                    sp.wait_ge(stage_stored[s], 16 * n_blocks * (NT // 4))

            if residual is not None:
                @block.gpsimd
                def _(pool):
                    for b, n in enumerate(wide):
                        for t in range(NT):
                            if (b, t) >= (0, 4):
                                pool.wait_ge(tile_out[(t + 4) % NT], b + (t >= 4))
                            pool.dma_start(res[:, t % 4, 0:n], residual[t * P:(t + 1) * P, b * COLS:b * COLS + n]
                                           ).then_inc(res_loaded[t % 4], 16)

            @block.scalar
            def _(act):
                def high(b):
                    for c in range(2):
                        at, n = slice(c * HALF, (c + 1) * HALF), wide[b]
                        act.wait_ge(raw_loaded[2 * (b % 2) + c], 16 * (b // 2 + 1))
                        if b >= 2:
                            act.wait_ge(last_product[b % 2], b // 2)
                        act.activation(w_hi[:, b % 2, at, 0:n], raw[:, b % 2, at, 0:n], ACT.Copy
                                       ).then_inc(hi_ready[b % 2], 1)

                high(0)
                for b, n in enumerate(wide):
                    if b + 1 < n_blocks:
                        high(b + 1)
                    for t in range(NT):
                        act.wait_ge(tile_out[t], b + 1)
                        act.dma_start(out[t * P:(t + 1) * P, b * COLS:b * COLS + n], stage[:, t % 4, 0:n]
                                      ).then_inc(stage_stored[t % 4], 16)

            @block.vector
            def _(dve):
                def low(b):
                    for c in range(2):
                        at, n = slice(c * HALF, (c + 1) * HALF), wide[b]
                        dve.wait_ge(hi_ready[b % 2], 2 * (b // 2) + c + 1)
                        dve.tensor_tensor(w_lo[:, b % 2, at, 0:n], raw[:, b % 2, at, 0:n],
                                          w_hi[:, b % 2, at, 0:n].bitcast(F32), ALU.subtract
                                          ).then_inc(lo_ready[b % 2], 1)

                low(0)
                for b, n in enumerate(wide):
                    for t in range(NT):
                        if t == 2 and b + 1 < n_blocks:
                            low(b + 1)
                        if t < NT - 1:
                            dve.wait_ge(product_ready[t], b + 1)
                        else:
                            dve.wait_ge(last_product[b % 2], b // 2 + 1)
                        if (b, t) >= (0, 4):
                            dve.wait_ge(stage_stored[t % 4], 16 * (2 * b + t // 4))
                        if residual is None:
                            last = dve.tensor_copy(stage[:, t % 4, 0:n], ps[:, t, 0:n])
                        else:
                            dve.wait_ge(res_loaded[t % 4], 16 * (2 * b + t // 4 + 1))
                            last = dve.tensor_tensor(stage[:, t % 4, 0:n], ps[:, t, 0:n], res[:, t % 4, 0:n], ALU.add)
                        last.then_inc(tile_out[t], 1)

            @block.tensor
            def _(pe):
                def body(u, i, n):
                    for t in range(NT):
                        pe.wait_ge(tile_out[t], 2 * i + u)
                        at = slice(t * P, (t + 1) * P)
                        for k in range(KT):
                            if t == 0 and k % HALF == 0:
                                pe.wait_ge(lo_ready[u], 2 * i + k // HALF + 1)
                            for j, (a, w_part) in enumerate(((xT_hi, w_hi), (xT_hi, w_lo), (xT_lo, w_hi))):
                                last = pe.matmul(ps[:, t, 0:n], a[:, k, at], w_part[:, u, k, 0:n],
                                                 start=(k == 0 and j == 0), stop=(k == KT - 1 and j == 2))
                        last.then_inc(product_ready[t] if t < NT - 1 else last_product[u], 1)

                with pe.Fori(0, full // 2) as i:
                    for u in range(2):
                        body(u, i, COLS)
                for b in range(full // 2 * 2, n_blocks):
                    body(b % 2, b // 2, wide[b])

CAP = S
NOWHERE = 4 * S


def route(nc, name, xT, w_group, b_group, w_expert, b_expert, table, gates, most, cst):
    NL = NG + NE
    with Pool_(nc, name) as m:
        w = m.sb("w", [P, KT, NL])
        bias = m.sb("bias", [P, NL])
        lg = m.sb("lg", [P, NT, NL])
        t4, e4, v4 = (m.sb(n, [P, NT, NG]) for n in ("t4", "e4", "v4"))
        em, v32 = (m.sb(n, [P, NT, NE]) for n in ("em", "v32"))
        chosen = m.sb("chosen", [P, 2, NT, NE])
        both = m.sb("both", [P, NT, NE])
        small = m.sb("small", [P, 8, NT])
        run = m.sb("run", [P, NT + 1, NE])
        pos = m.sb("pos", [P, NT, NE])
        dest_f = m.sb("dest_f", [P, 2, NT])
        dest = m.sb("dest", [P, 2, NT], I32)
        codes = m.sb("codes", [P, 2, NT, 2], I32)
        nowhere = m.sb("nowhere", [P, NE * CAP * 2 // P], I32)
        most_f = m.sb("most_f", [P, 1])
        ps_l = m.ps("ps_l", [P, NT, 64])
        ps_c = m.ps("ps_c", [P, 2, NT, NE])
        loaded, logits, shifted, exps = m.sem("loaded"), m.sem("logits"), m.sem("shifted"), m.sem("exps")
        chosen_ready, counted, dest_ready = m.sem("chosen_ready"), m.sem("counted"), m.sem("dest_ready")
        filled, cleared, scattered = m.sem("filled"), m.sem("cleared"), m.sem("scattered")
        top, gsum, best, second, e2, den, inv = (small[:, j, :] for j in range(7))

        with nc.Block() as block:
            @block.sync
            def _(sp):
                sp.dma_start(w[:, :, 0:NG], w_group.rearrange("(k p) n -> p k n", p=P)).then_inc(loaded, 16)
                sp.dma_start(w[:, :, NG:NL], w_expert.rearrange("(k p) n -> p k n", p=P)).then_inc(loaded, 16)
                sp.dma_start(bias[:, 0:NG], row_of(b_group)).then_inc(loaded, 16)
                sp.dma_start(bias[:, NG:NL], row_of(b_expert)).then_inc(loaded, 16)
                sp.wait_ge(filled, 1)
                sp.dma_start(table.rearrange("(p r) c -> p (r c)", p=P), nowhere[:]).then_inc(cleared, 16)

            @block.gpsimd
            def _(pool):
                pool.memset(nowhere[:], NOWHERE).then_inc(filled, 1)
                pool.iota(codes[:, :, :, 0], pattern=[[0, 2], [P, NT]], base=0, channel_multiplier=1)
                pool.iota(codes[:, :, :, 1], pattern=[[S, 2], [P, NT]], base=0, channel_multiplier=1)
                pool.drain()
                pool.wait_ge(cleared, 16)
                pool.wait_ge(dest_ready, 1)
                for c in range(2):
                    for t in range(NT):
                        pool.indirect_dma_start(
                            out=table, out_offset=bass.IndirectOffsetOnAxis(ap=dest[:, c, t:t + 1], axis=0),
                            in_=codes[:, c, t, :], in_offset=None).then_inc(scattered, 16)
                pool.wait_ge(scattered, 16 * 2 * NT)

            @block.tensor
            def _(pe):
                pe.wait_ge(loaded, 64)
                for t in range(NT):
                    for k in range(KT):
                        last = pe.matmul(ps_l[:, t, 0:NL], xT[:, k, t * P:(t + 1) * P], w[:, k, :],
                                         start=(k == 0), stop=(k == KT - 1))
                last.then_inc(logits, 1)
                pe.wait_ge(chosen_ready, 1)
                pe.matmul(ps_c[:, 0, :, :], cst.before[:], both[:], start=True, stop=True)
                pe.matmul(ps_c[:, 1, :, :], cst.ones[:], both[:], start=True, stop=True).then_inc(counted, 1)

            @block.scalar
            def _(act):
                act.wait_ge(shifted, 1)
                act.activation(e4[:], t4[:], ACT.Exp).then_inc(exps, 1)
                act.wait_ge(shifted, 2)
                act.activation(e2, den, ACT.Exp).then_inc(exps, 1)

            @block.vector
            def _(dve):
                def one_hot(out, values, maximum, iota, v, n):
                    wide = [P, NT, n]
                    dve.tensor_tensor(v[:], values, maximum.unsqueeze(2).to_broadcast(wide), ALU.is_equal)
                    dve.drain()
                    dve.scalar_tensor_tensor(v[:], v[:], -64.0, iota.unsqueeze(1).to_broadcast(wide), ALU.mult, ALU.add)
                    dve.drain()
                    dve.tensor_reduce(inv, v[:], X, ALU.min)
                    dve.drain()
                    dve.tensor_tensor(out, v[:], inv.unsqueeze(2).to_broadcast(wide), ALU.is_equal)
                    dve.drain()

                dve.wait_ge(loaded, 64)
                dve.wait_ge(logits, 1)
                dve.tensor_tensor(lg[:], ps_l[:, :, 0:NL], bias[:].unsqueeze(1).to_broadcast([P, NT, NL]), ALU.add)
                dve.drain()
                dve.tensor_reduce(top, lg[:, :, 0:NG], X, ALU.max)
                dve.drain()
                dve.tensor_tensor(t4[:], lg[:, :, 0:NG], top.unsqueeze(2).to_broadcast([P, NT, NG]), ALU.subtract
                                  ).then_inc(shifted, 1)
                one_hot(v4[:], lg[:, :, 0:NG], top, cst.iota[:, 0:NG], v4, NG)
                dve.tensor_scalar(v4[:], v4[:], -1.0, -NEG, ALU.add, ALU.mult)
                dve.drain()
                dve.tensor_tensor(em[:].rearrange("p t (g e) -> p t g e", g=NG),
                                  lg[:, :, NG:NL].rearrange("p t (g e) -> p t g e", g=NG),
                                  v4[:].unsqueeze(3).to_broadcast([P, NT, NG, EPG]), ALU.add)
                dve.drain()
                dve.tensor_reduce(best, em[:], X, ALU.max)
                dve.drain()
                one_hot(chosen[:, 0, :, :], em[:], best, cst.iota[:, 0:NE], v32, NE)
                dve.scalar_tensor_tensor(em[:], chosen[:, 0, :, :], 2 * NEG, em[:], ALU.mult, ALU.add)
                dve.drain()
                dve.tensor_reduce(second, em[:], X, ALU.max)
                dve.drain()
                dve.tensor_tensor(den, second, best, ALU.subtract).then_inc(shifted, 1)
                one_hot(chosen[:, 1, :, :], em[:], second, cst.iota[:, 0:NE], v32, NE)
                dve.tensor_tensor(both[:], chosen[:, 0, :, :], chosen[:, 1, :, :], ALU.add).then_inc(chosen_ready, 1)
                dve.wait_ge(exps, 2)
                dve.tensor_reduce(gsum, e4[:], X, ALU.add)
                dve.drain()
                dve.scalar_tensor_tensor(inv, e2, 1.0, gsum, ALU.add, ALU.mult)
                dve.drain()
                dve.reciprocal(gates[:, 0:NT], inv)
                dve.drain()
                dve.tensor_tensor(gates[:, NT:2 * NT], e2, gates[:, 0:NT], ALU.mult)
                dve.memset(run[:, 0, :], 0.0)
                dve.wait_ge(counted, 1)
                for t in range(NT):
                    dve.drain()
                    dve.tensor_tensor(run[:, t + 1, :], run[:, t, :], ps_c[:, 1, t, :], ALU.add)
                dve.drain()
                dve.tensor_tensor(pos[:], ps_c[:, 0, :, :], run[:, 0:NT, :], ALU.add)
                dve.tensor_reduce(most_f[:], run[:, NT, :], X, ALU.max)
                dve.drain()
                dve.scalar_tensor_tensor(pos[:], cst.iota[:, 0:NE].unsqueeze(1).to_broadcast([P, NT, NE]),
                                         float(CAP), pos[:], ALU.mult, ALU.add)
                dve.tensor_copy(most[:], most_f[:])
                dve.drain()
                for c in range(2):
                    dve.tensor_tensor(v32[:], chosen[:, c, :, :], pos[:], ALU.mult)
                    dve.drain()
                    dve.tensor_reduce(dest_f[:, c, :], v32[:], X, ALU.add)
                    dve.drain()
                dve.tensor_copy(dest[:], dest_f[:]).then_inc(dest_ready, 1)


def experts(nc, name, xn_dram, w_gate, w_up, w_down, table, slots, most, ident):
    U, B = 8, 4
    STEPS = NE // U
    with Pool_(nc, name) as m:
        w_gu = m.sb("w_gu", [P, B, KT, 2 * DE])
        w_d = m.sb("w_d", [P, B, DE // P, D])
        idx = m.sb("idx", [P, U, 2], I32)
        xg = m.sb("xg", [P, B, D])
        xgT = m.sb("xgT", [P, B, KT, P])
        silu = m.sb("silu", [P, B, DE])
        hid = m.sb("hid", [P, B, DE])
        hidT = m.sb("hidT", [P, B, DE // P, P])
        y = m.sb("y", [P, B, D])
        ps_x = m.ps("ps_x", [P, KT, P])
        ps_h = m.ps("ps_h", [P, 2, 2 * DE])
        ps_t = m.ps("ps_t", [P, 2, 2 * P])
        ps_y = m.ps("ps_y", [P, D])
        gu_loaded, down_loaded, idx_loaded = m.sems("gu_loaded", B), m.sems("down_loaded", B), m.sems("idx_loaded", U)
        gathered, x_turned, xT_ready = m.sems("gathered", B), m.sems("x_turned", B), m.sems("xT_ready", B)
        h_ready, silu_ready, hid_ready = m.sems("h_ready", B), m.sems("silu_ready", B), m.sems("hid_ready", B)
        h_turned, hT_ready = m.sems("h_turned", B), m.sems("hT_ready", B)
        y_done, y_out, scattered = m.sems("y_done", B), m.sems("y_out", B), m.sems("scattered", U)
        cleared = m.sem("cleared")
        apart = m.sem("apart")

        def waves(eng, body):
            full = eng.value_load(most[0:1, 0:1], min_val=0, max_val=CAP)
            with eng.Fori(0, CAP // P) as w:
                with eng.If(full > w * P):
                    body(w)

        def steps(eng, w, body):
            with eng.Fori(0, STEPS) as i:
                body(w * STEPS + i)

        def uses(n, u):
            return n * (U // B) + u // B

        with nc.Block() as block:
            @block.sync
            def _(sp):
                def wave(w):
                    with sp.Fori(0, STEPS) as i:
                        n = w * STEPS + i
                        for u in range(U):
                            k = sp.snap(uses(n, u))
                            row, expert = sp.snap((i * U + u) * CAP + w * P), sp.snap(i * U + u)
                            sp.wait_ge(scattered[u], 16 * n)
                            sp.dma_start(idx[:, u, :], table[ds(row, P), :]).then_inc(idx_loaded[u], 16)
                            sp.wait_ge(h_ready[u % B], k)
                            for j, src in enumerate((w_gate, w_up)):
                                sp.dma_start(w_gu[:, u % B, :, j * DE:(j + 1) * DE],
                                             src[ds(expert, 1), :, :].rearrange("a (k p) n -> p (a k) n", p=P)
                                             ).then_inc(gu_loaded[u % B], 16)
                            sp.wait_ge(y_done[u % B], k)
                            sp.dma_start(w_d[:, u % B, :, :],
                                         w_down[ds(expert, 1), :, :].rearrange("a (k p) n -> p (a k) n", p=P)
                                         ).then_inc(down_loaded[u % B], 16)
                waves(sp, wave)

            @block.gpsimd
            def _(pool):
                last_token, last_slot = pool.to_reg(S - 1), pool.to_reg(2 * S - 1)
                pool.wait_ge(cleared, 1)

                def gather(n, u):
                    pool.wait_ge(idx_loaded[u], 16 * n + 16)
                    pool.wait_ge(x_turned[u % B], uses(n, u))
                    pool.sem_inc(apart, 1)
                    pool.indirect_dma_start(
                        out=xg[:, u % B, :], out_offset=None, in_=xn_dram,
                        in_offset=bass.IndirectOffsetOnAxis(ap=idx[:, u, 0:1], axis=0),
                        bounds_check=last_token, oob_is_err=False).then_inc(gathered[u % B], 16)

                def scatter(n, u):
                    pool.wait_ge(y_out[u % B], uses(n, u) + 1)
                    pool.sem_inc(apart, 1)
                    pool.indirect_dma_start(
                        out=slots, out_offset=bass.IndirectOffsetOnAxis(ap=idx[:, u, 1:2], axis=0),
                        in_=y[:, u % B, :], in_offset=None,
                        bounds_check=last_slot, oob_is_err=False).then_inc(scattered[u], 16)

                def body(n, more):
                    for u in range(U):
                        if u + B < U:
                            gather(n, u + B)
                        elif more:
                            gather(n + 1, u + B - U)
                        scatter(n, u)

                def wave(w):
                    first = w * STEPS
                    for u in range(B):
                        gather(first, u)
                    with pool.Fori(0, STEPS - 1) as i:
                        body(w * STEPS + i, True)
                    body(first + (STEPS - 1), False)
                    for u in range(U):
                        pool.wait_ge(scattered[u], w * (16 * STEPS) + 16 * STEPS)
                    pool.sem_inc(apart, 1)
                waves(pool, wave)

            @block.tensor
            def _(pe):
                def turn_x(n, u):
                    pe.wait_ge(gathered[u % B], 16 * uses(n, u) + 16)
                    pe.wait_ge(xT_ready[(u - 1) % B], uses(n, u) + (u % B > 0))
                    for k in range(KT):
                        last = pe.transpose(ps_x[:, k, :], xg[:, u % B, k * P:(k + 1) * P], ident[:])
                    last.then_inc(x_turned[u % B], 1)

                def gate_up(n, u):
                    pe.wait_ge(xT_ready[u % B], uses(n, u) + 1)
                    pe.wait_ge(gu_loaded[u % B], 32 * uses(n, u) + 32)
                    pe.wait_ge(hid_ready[(u + 2) % B], uses(n, u) + (u % B >= 2))
                    for k in range(KT):
                        last = pe.matmul(ps_h[:, u % 2, :], xgT[:, u % B, k, :], w_gu[:, u % B, k, :],
                                         start=(k == 0), stop=(k == KT - 1))
                    last.then_inc(h_ready[u % B], 1)

                def turn_h(n, u):
                    pe.wait_ge(hid_ready[u % B], uses(n, u) + 1)
                    pe.wait_ge(hT_ready[(u + 2) % B], uses(n, u) + (u % B >= 2))
                    for k in range(DE // P):
                        last = pe.transpose(ps_t[:, u % 2, k * P:(k + 1) * P], hid[:, u % B, k * P:(k + 1) * P], ident[:])
                    last.then_inc(h_turned[u % B], 1)

                def down(n, u):
                    pe.wait_ge(hT_ready[u % B], uses(n, u) + 1)
                    pe.wait_ge(down_loaded[u % B], 16 * uses(n, u) + 16)
                    pe.wait_ge(y_out[(u - 1) % B], uses(n, u) + (u % B > 0))
                    for half in range(D // COLS):
                        for k in range(DE // P):
                            last = pe.matmul(ps_y[:, half * COLS:(half + 1) * COLS], hidT[:, u % B, k, :],
                                             w_d[:, u % B, k, half * COLS:(half + 1) * COLS],
                                             start=(k == 0), stop=(k == DE // P - 1))
                    last.then_inc(y_done[u % B], 1)

                def body(n):
                    turn_x(n, 0)
                    for u in range(U):
                        gate_up(n, u)
                        if u + 1 < U:
                            turn_x(n, u + 1)
                        if u:
                            turn_h(n, u - 1)
                            down(n, u - 1)
                    turn_h(n, U - 1)
                    down(n, U - 1)
                waves(pe, lambda w: steps(pe, w, body))

            @block.scalar
            def _(act):
                def x_out(n, u):
                    act.wait_ge(x_turned[u % B], uses(n, u) + 1)
                    act.wait_ge(h_ready[u % B], uses(n, u))
                    act.activation(xgT[:, u % B, :, :], ps_x[:], ACT.Copy).then_inc(xT_ready[u % B], 1)

                def gate(n, u):
                    act.wait_ge(h_ready[u % B], uses(n, u) + 1)
                    act.wait_ge(hid_ready[u % B], uses(n, u))
                    act.activation(silu[:, u % B, :], ps_h[:, u % 2, 0:DE], ACT.Silu).then_inc(silu_ready[u % B], 1)

                def body(n):
                    x_out(n, 0)
                    for u in range(U):
                        gate(n, u)
                        if u + 1 < U:
                            x_out(n, u + 1)
                waves(act, lambda w: steps(act, w, body))

            @block.vector
            def _(dve):
                dve.memset(xg[:], 0.0).then_inc(cleared, 1)

                def product(n, u):
                    dve.wait_ge(silu_ready[u % B], uses(n, u) + 1)
                    dve.wait_ge(h_turned[u % B], uses(n, u))
                    dve.tensor_tensor(hid[:, u % B, :], silu[:, u % B, :], ps_h[:, u % 2, DE:2 * DE], ALU.mult
                                      ).then_inc(hid_ready[u % B], 1)

                def h_out(n, u):
                    dve.wait_ge(h_turned[u % B], uses(n, u) + 1)
                    dve.wait_ge(y_done[u % B], uses(n, u))
                    dve.tensor_copy(hidT[:, u % B, :, :], ps_t[:, u % 2, :]).then_inc(hT_ready[u % B], 1)

                def rows_out(n, u):
                    dve.wait_ge(y_done[u % B], uses(n, u) + 1)
                    dve.wait_ge(scattered[(u + B) % U], 16 * (n + (u >= B)))
                    dve.tensor_copy(y[:, u % B, :], ps_y[:]).then_inc(y_out[u % B], 1)

                def body(n):
                    product(n, 0)
                    for u in range(1, U):
                        h_out(n, u - 1)
                        product(n, u)
                        rows_out(n, u - 1)
                    h_out(n, U - 1)
                    rows_out(n, U - 1)
                waves(dve, lambda w: steps(dve, w, body))


def constants(nc, cst, block):
    @block.gpsimd
    def _(pool):
        pool.memset(cst.ident[:], 0.0)
        pool.memset(cst.ones[:], 1.0)
        pool.iota(cst.iota_i[:], pattern=[[1, 64]], base=0, channel_multiplier=0)
        pool.drain()
        pool.affine_select(out=cst.ident[:], in_=cst.ident[:], compare_op=ALU.not_equal, fill=1.0, base=0,
                           pattern=[[-1, P]], channel_multiplier=1)
        pool.affine_select(out=cst.before[:], in_=cst.ones[:], compare_op=ALU.is_gt, fill=0.0, base=0,
                           pattern=[[1, P]], channel_multiplier=-1)
        pool.tensor_copy(cst.iota[:], cst.iota_i[:])
        pool.drain()


def gated_conv(nc, name, xT_hi, xT_lo, w, conv_w, conv_b, zT_hi, zT_lo):
    PARTS = (1, 2, 0)
    with Pool_(nc, name) as m:
        raw = m.sb("raw", [P, 3, KT, P])
        w_hi = m.sb("w_hi", [P, 3, KT, P], F32R)
        w_lo = m.sb("w_lo", [P, 3, KT, P], F32R)
        taps = m.sb("taps", [P, KT, 3])
        bias = m.sb("bias", [P, KT])
        c_sb = m.sb("c_sb", [P, S])
        u_sb = m.sb("u_sb", [P, S + 2])
        y_sb = m.sb("y_sb", [P, S])
        z_sb = m.sb("z_sb", [P, S])
        ps = m.ps("ps", [P, 3, S])
        raw_loaded, hi_ready, lo_ready = m.sems("raw_loaded", 3), m.sems("hi_ready", 3), m.sems("lo_ready", 3)
        product, taps_loaded = m.sems("product", 3), m.sem("taps_loaded")
        apart = m.sem("apart")
        c_out, u_ready, z_ready, z_hi, z_lo = (m.sem(n) for n in ("c_out", "u_ready", "z_ready", "z_hi", "z_lo"))
        w_k = w.rearrange("(k p) n -> p k n", p=P)

        with nc.Block() as block:
            @block.sync
            def _(sp):
                for j in range(3):
                    sp.dma_start(taps[:, :, j], conv_w[j, :].rearrange("(c p) -> p c", p=P),
                                 allow_slow_non_contiguous=True).then_inc(taps_loaded, 16)
                sp.dma_start(bias[:], conv_b.rearrange("(c p) -> p c", p=P),
                                 allow_slow_non_contiguous=True).then_inc(taps_loaded, 16)
                with sp.Fori(0, KT) as i:
                    for j in range(3):
                        col = sp.snap(i * P + PARTS[j] * D)
                        sp.wait_ge(lo_ready[j], i)
                        sp.sem_inc(apart, 1)
                        sp.dma_start(raw[:, j, :, :], w_k[:, :, ds(col, P)]).then_inc(raw_loaded[j], 16)

            @block.scalar
            def _(act):
                def high(i, j):
                    act.wait_ge(raw_loaded[j], 16 * i + 16)
                    act.wait_ge(product[j], i)
                    act.activation(w_hi[:, j, :, :], raw[:, j, :, :], ACT.Copy).then_inc(hi_ready[j], 1)

                with act.Fori(0, KT) as i:
                    for j in range(3):
                        high(i, j)
                    act.wait_ge(product[0], i + 1)
                    act.wait_ge(u_ready, i)
                    act.activation(c_sb[:], ps[:, 0, :], ACT.Copy).then_inc(c_out, 1)
                    act.wait_ge(z_ready, i + 1)
                    act.activation(zT_hi[:, ds(i, 1), :], z_sb[:].unsqueeze(1), ACT.Copy).then_inc(z_hi, 1)

            @block.vector
            def _(dve):
                dve.memset(u_sb[:, 0:2], 0.0)
                dve.wait_ge(taps_loaded, 64)
                with dve.Fori(0, KT) as i:
                    for j in range(3):
                        dve.wait_ge(hi_ready[j], i + 1)
                        dve.tensor_tensor(w_lo[:, j, :, :], raw[:, j, :, :], w_hi[:, j, :, :].bitcast(F32),
                                          ALU.subtract).then_inc(lo_ready[j], 1)
                    dve.wait_ge(c_out, i + 1)
                    dve.wait_ge(product[1], i + 1)
                    dve.tensor_tensor(u_sb[:, 2:S + 2], c_sb[:], ps[:, 1, :], ALU.mult).then_inc(u_ready, 1)
                    dve.drain()
                    dve.tensor_scalar(y_sb[:], u_sb[:, 2:S + 2], taps[:, ds(i, 1), 2], bias[:, ds(i, 1)], ALU.mult, ALU.add)
                    dve.drain()
                    for j in (1, 0):
                        dve.scalar_tensor_tensor(y_sb[:], u_sb[:, j:S + j], taps[:, ds(i, 1), j], y_sb[:], ALU.mult, ALU.add)
                        dve.drain()
                    dve.wait_ge(product[2], i + 1)
                    dve.wait_ge(z_hi, i)
                    dve.tensor_tensor(z_sb[:], y_sb[:], ps[:, 2, :], ALU.mult).then_inc(z_ready, 1)
                    dve.wait_ge(z_hi, i + 1)
                    dve.tensor_tensor(zT_lo[:, ds(i, 1), :], z_sb[:].unsqueeze(1), zT_hi[:, ds(i, 1), :].bitcast(F32),
                                      ALU.subtract).then_inc(z_lo, 1)

            @block.tensor
            def _(pe):
                with pe.Fori(0, KT) as i:
                    for j in range(3):
                        pe.wait_ge(lo_ready[j], i + 1)
                        pe.wait_ge((c_out, u_ready, z_ready)[j], i)
                        for half in range(S // COLS):
                            at = slice(half * COLS, (half + 1) * COLS)
                            for k in range(KT):
                                for q, (w_part, x_part) in enumerate(((w_hi, xT_hi), (w_hi, xT_lo), (w_lo, xT_hi))):
                                    last = pe.matmul(ps[:, j, at], w_part[:, j, k, :], x_part[:, k, at],
                                                     start=(k == 0 and q == 0), stop=(k == KT - 1 and q == 2))
                        last.then_inc(product[j], 1)


def retention(nc, name, proj, ret_gain, ident, con, y_out):
    PAIRS = RH // 2
    with Pool_(nc, name) as m:
        decay = m.sb("decay", [P, 2, PAIRS, P])
        q_decay = m.sb("q_decay", [P, PAIRS, P])
        k_decay = m.sb("k_decay", [P, RH])
        c_decay = m.sb("c_decay", [P, PAIRS])
        gain = m.sb("gain", [P, HD])
        qkv = m.sb("qkv", [P, 2, 3 * RET_W])
        gate = m.sb("gate", [P, NT, RET_W])
        qkT = m.sb("qkT", [P, 2, PAIRS, P])
        qdT = m.sb("qdT", [P, PAIRS, P])
        kd = m.sb("kd", [P, RET_W])
        scores = m.sb("scores", [P, 2, PAIRS, P])
        state = m.sb("state", [P, PAIRS, HD])
        y = m.sb("y", [P, NT, RET_W])
        sq = m.sb("sq", [P, NT, RET_W])
        ssq = m.sb("ssq", [P, NT, RH])
        eps = m.sb("eps", [P, 1])
        ps_t = m.ps("ps_t", [P, 2, PAIRS, P])
        ps_s = m.ps("ps_s", [P, 2, PAIRS, P])
        ps_y = m.ps("ps_y", [P, 2, COLS])
        ps_kv = m.ps("ps_kv", [P, PAIRS, HD])
        const_loaded, qkv_loaded, gate_loaded = m.sem("const_loaded"), m.sems("qkv_loaded"), m.sem("gate_loaded")
        turned, T_ready, qd_ready, kd_ready = (m.sem(n) for n in ("turned", "T_ready", "qd_ready", "kd_ready"))
        scored, decayed, y_taken = (m.sem(n) for n in ("scored", "decayed", "y_taken"))
        y_ready = m.sems("y_ready")
        kv_ready, state_ready = m.sem("kv_ready"), m.sem("state_ready")
        squared, summed, rooted, silus, done, stored = (
            m.sem(n) for n in ("squared", "summed", "rooted", "silus", "done", "stored"))

        with nc.Block() as block:
            @block.sync
            def _(sp):
                with sp.Fori(0, NT // 2) as i:
                    for u in range(2):
                        row = sp.snap((2 * i + u) * P)
                        sp.wait_ge(y_ready[u], i)
                        sp.dma_start(qkv[:, u, :], proj[ds(row, P), 0:3 * RET_W]).then_inc(qkv_loaded[u], 16)
                sp.wait_ge(done, 1)
                sp.dma_start(y_out.rearrange("(t p) n -> p t n", p=P)[:, :, 0:RET_W], y[:]).then_inc(stored, 16)
                sp.wait_ge(stored, 16)

            @block.scalar
            def _(act):
                for dst, src in ((decay[:], con["decay"].rearrange("p (a b c) -> p a b c", a=2, b=PAIRS)),
                                 (q_decay[:], con["q_decay"].rearrange("p (a b) -> p a b", a=PAIRS)),
                                 (k_decay[:], con["k_decay"]), (c_decay[:], con["c_decay"]),
                                 (gain[:], row_of(ret_gain))):
                    act.dma_start(dst, src).then_inc(const_loaded, 16)
                act.dma_start(gate[:], proj.rearrange("(t p) n -> p t n", p=P)[:, :, 3 * RET_W:4 * RET_W]
                              ).then_inc(gate_loaded, 16)
                with act.Fori(0, NT // 2) as i:
                    for u in range(2):
                        c = 2 * i + u
                        act.wait_ge(turned, c + 1)
                        act.wait_ge(y_ready[1 - u], i + u)
                        act.activation(qkT[:], ps_t[:], ACT.Copy).then_inc(T_ready, 1)
                        act.wait_ge(y_ready[u], i + 1)
                        act.activation(y[:, ds(c, 1), :].rearrange("p t (b a d) -> p (t a) b d", a=2, d=HD),
                                       ps_y[:, :, 0:PAIRS * HD].rearrange("p a (b d) -> p a b d", d=HD),
                                       ACT.Copy).then_inc(y_taken, 1)
                act.wait_ge(y_taken, NT)
                act.activation(sq[:], y[:], ACT.Square).then_inc(squared, 1)
                act.wait_ge(gate_loaded, 16)
                act.activation(gate[:], gate[:], ACT.Silu).then_inc(silus, 1)
                act.wait_ge(summed, 1)
                act.activation(ssq[:], ssq[:], ACT.Sqrt, bias=eps[:], scale=1.0 / HD).then_inc(rooted, 1)

            @block.vector
            def _(dve):
                dve.memset(state[:], 0.0).then_inc(state_ready, 1)
                dve.memset(eps[:], EPS)
                dve.wait_ge(const_loaded, 80)
                with dve.Fori(0, NT // 2) as i:
                    for u in range(2):
                        c = 2 * i + u
                        dve.wait_ge(qkv_loaded[u], 16 * i + 16)
                        dve.wait_ge(kv_ready, c)
                        dve.tensor_tensor(kd[:].rearrange("p (h d) -> p h d", d=HD),
                                          qkv[:, u, RET_W:2 * RET_W].rearrange("p (h d) -> p h d", d=HD),
                                          k_decay[:].unsqueeze(2).to_broadcast([P, RH, HD]), ALU.mult
                                          ).then_inc(kd_ready, 1)
                        dve.wait_ge(T_ready, c + 1)
                        dve.wait_ge(y_ready[1 - u], i + u)
                        dve.tensor_tensor(qdT[:], qkT[:, 0, :, :], q_decay[:], ALU.mult).then_inc(qd_ready, 1)
                        dve.wait_ge(scored, c + 1)
                        dve.tensor_tensor(scores[:], ps_s[:], decay[:], ALU.mult).then_inc(decayed, 1)
                        dve.wait_ge(kv_ready, c + 1)
                        dve.wait_ge(y_ready[u], i + 1)
                        dve.tensor_tensor(state[:], state[:], c_decay[:].unsqueeze(2).to_broadcast([P, PAIRS, HD]),
                                          ALU.mult)
                        dve.drain()
                        dve.tensor_tensor(state[:], state[:], ps_kv[:], ALU.add).then_inc(state_ready, 1)
                        dve.drain()
                heads = [P, NT * RH, HD]
                y_h = y[:].rearrange("p t (h d) -> p (t h) d", d=HD)
                ssq_h = ssq[:].rearrange("p t h -> p (t h)")
                dve.wait_ge(squared, 1)
                dve.tensor_reduce(ssq_h, sq[:].rearrange("p t (h d) -> p (t h) d", d=HD), X, ALU.add
                                  ).then_inc(summed, 1)
                dve.wait_ge(silus, 1)
                dve.wait_ge(rooted, 1)
                dve.reciprocal(ssq_h, ssq_h)
                dve.drain()
                dve.tensor_tensor(y_h, y_h, ssq_h.unsqueeze(2).to_broadcast(heads), ALU.mult)
                dve.drain()
                dve.tensor_tensor(y_h, y_h, gain[:].unsqueeze(1).to_broadcast(heads), ALU.mult)
                dve.drain()
                dve.tensor_tensor(y[:], y[:], gate[:], ALU.mult).then_inc(done, 1)

            @block.tensor
            def _(pe):
                with pe.Fori(0, NT // 2) as i:
                    for u in range(2):
                        c = 2 * i + u
                        pe.wait_ge(qkv_loaded[u], 16 * i + 16)
                        pe.wait_ge(T_ready, c)
                        for a in range(2):
                            for b in range(PAIRS):
                                last = pe.transpose(ps_t[:, a, b, :], qkv[:, u, a * RET_W + b * P:a * RET_W + (b + 1) * P],
                                                    ident[:])
                        last.then_inc(turned, 1)
                        pe.wait_ge(kd_ready, c + 1)
                        pe.wait_ge(state_ready, c + 1)
                        for a in range(2):
                            for b in range(PAIRS):
                                h = 2 * b + a
                                last = pe.matmul(ps_kv[a * HD:(a + 1) * HD, b, :], kd[:, h * HD:(h + 1) * HD],
                                                 qkv[:, u, 2 * RET_W + h * HD:2 * RET_W + (h + 1) * HD],
                                                 start=True, stop=True)
                        last.then_inc(kv_ready, 1)
                        pe.wait_ge(T_ready, c + 1)
                        pe.wait_ge(decayed, c)
                        for a in range(2):
                            at = slice(a * HD, (a + 1) * HD)
                            for b in range(PAIRS):
                                last = pe.matmul(ps_s[:, a, b, :], qkT[at, 1, b, :], qkT[at, 0, b, :],
                                                 start=True, stop=True)
                        last.then_inc(scored, 1)
                        pe.wait_ge(qd_ready, c + 1)
                        pe.wait_ge(y_taken, c)
                        pe.wait_ge(decayed, c + 1)
                        for a in range(2):
                            at = slice(a * HD, (a + 1) * HD)
                            for b in range(PAIRS):
                                h = 2 * b + a
                                pe.matmul(ps_y[:, a, b * HD:(b + 1) * HD], scores[:, a, b, :],
                                          qkv[:, u, 2 * RET_W + h * HD:2 * RET_W + (h + 1) * HD], start=True, stop=False)
                                last = pe.matmul(ps_y[:, a, b * HD:(b + 1) * HD], qdT[at, b, :], state[at, b, :],
                                                 start=False, stop=True)
                        last.then_inc(y_ready[u], 1)


def shape_constants():
    f = np.float32
    con = {}
    log_g = np.log(f(1) - f(2) ** (f(-5) - np.arange(RH, dtype=f)))
    pos = np.arange(P, dtype=f)
    diff = pos[:, None] - pos[None, :]
    dec = np.where(diff >= 0, np.exp(log_g[:, None, None] * np.maximum(diff, 0)), 0) * f(HD ** -0.5)
    by = [[2 * b + a for b in range(RH // 2)] for a in range(2)]
    con["decay"] = dec.transpose(0, 2, 1)[by].transpose(2, 0, 1, 3).reshape(P, -1)
    q_dec = np.exp(log_g[:, None] * (pos + 1))
    con["q_decay"] = np.repeat(q_dec[by], HD, axis=0).reshape(P, -1)
    con["k_decay"] = (np.exp(log_g[:, None] * (P - 1 - pos)) * f(HD ** -0.5)).T
    con["c_decay"] = np.repeat(np.exp(log_g * P)[by], HD, axis=0)
    return {k: np.ascontiguousarray(v, dtype=f) for k, v in con.items()}

QR = HD + NS + 1


def sparse_prepare(nc, name, m, proj, q_gain, k_gains, pe, w1, w2, cst, con, keep):
    with Pool_(nc, name) as m:
        nq = m.sb("nq", [P, NT, NSA_W])
        kv = m.sb("kv", [P, NT, 2 * KV_W])
        kvc = m.sb("kvc", [P, 2, NT, KV_W])
        kvc2 = m.sb("kvc2", [P, 2, NT, G, 2, HD])
        sq = m.sb("sq", [P, NT, NSA_W])
        ssq = m.sb("ssq", [P, NT * 12])
        eps = m.sb("eps", [P, 1])
        gains = m.sb("gains", [P, 4, HD])
        loaded, ready = m.sem("loaded"), m.sem("ready")
        squares, sums, roots, stage = m.sem("squares"), m.sem("sums"), m.sem("roots"), m.sem("stage")
        tiled = proj.rearrange("(t p) n -> p t n", p=P)
        NQ = NT * NH
        NK = NT * 4

        with nc.Block() as block:
            @block.sync
            def _(sp):
                sp.dma_start(nq[:], tiled[:, :, C_NQ:C_KC]).then_inc(loaded, 16)
                for j, (a, b) in enumerate(((C_KS, C_VS), (C_KW, C_VW))):
                    sp.dma_start(kv[:, :, j * KV_W:(j + 1) * KV_W], tiled[:, :, a:b]).then_inc(loaded, 16)
                for j, (a, b) in enumerate(((C_KC, C_VC), (C_VC, C_KS))):
                    sp.dma_start(kvc[:, j, :, :], tiled[:, :, a:b]).then_inc(loaded, 16)
                for j, (a, b) in enumerate(((C_VS, C_KW), (C_VW, C_NG))):
                    sp.dma_start(keep.v[:, :, j, :], tiled[:, :, a:b]).then_inc(loaded, 16)
                sp.dma_start(keep.gate[:], tiled[:, :, C_NG:IN_W]).then_inc(loaded, 16)
                for dst, src in ((gains[:, 0, :], row_of(q_gain)), (gains[:, 1:4, :], row_of(k_gains))):
                    sp.dma_start(dst, src).then_inc(loaded, 16)
                for b in range(2):
                    for g in range(G):
                        sp.dma_start(keep.kT[HD:QR, b, g, :], con["key_rows"]).then_inc(loaded, 16)
                for g in range(G):
                    sp.dma_start(keep.kcT[HD:QR, g, :], con["cmp_rows"]).then_inc(loaded, 16)
                sp.dma_start(keep.q_rows[:], con["q_rows"].rearrange("p (t h j) -> p t h j", t=NT, h=NH)).then_inc(loaded, 16)
                sp.dma_start(keep.forced[:], con["forced"].rearrange("p (t j) -> p t j", t=NT)).then_inc(loaded, 16)
                sp.dma_start(keep.masks_f[:], con["masks"]).then_inc(loaded, 16)
                sp.dma_start(keep.picks_f[:], con["picks"]).then_inc(loaded, 16)
                sp.wait_ge(loaded, 16 * 20)

        with nc.Block() as block:
            @block.scalar
            def _(act):
                act.activation(sq[:], nq[:], ACT.Square).then_inc(squares, 1)
                act.wait_ge(sums, 1)
                act.activation(sq[:, :, 0:2 * KV_W], kv[:], ACT.Square).then_inc(squares, 1)
                act.wait_ge(sums, 2)
                act.activation(ssq[:], ssq[:], ACT.Sqrt, bias=eps[:], scale=1.0 / HD).then_inc(roots, 1)

            @block.gpsimd
            def _(pool):
                pool.tensor_copy(keep.masks[:], keep.masks_f[:])
                pool.tensor_copy(keep.picks[:], keep.picks_f[:])
                pool.tensor_copy(keep.ident_b[:], cst.ident[:])
                pool.tensor_copy(keep.qa[:, :, :, HD:QR], keep.q_rows[:])
                for j in range(2):
                    for a in range(2):
                        pool.tensor_copy(kvc2[:, j, :, :, a, :], kvc[:, j, :, :].rearrange("p t (g d) -> p t g d", d=HD))
                pool.drain()

            @block.vector
            def _(dve):
                dve.memset(eps[:], EPS)
                dve.wait_ge(squares, 1)
                dve.tensor_reduce(ssq[:, 0:NQ], sq[:].rearrange("p t (h d) -> p (t h) d", d=HD), X, ALU.add
                                  ).then_inc(sums, 1)
                dve.wait_ge(squares, 2)
                dve.tensor_reduce(ssq[:, NQ:NQ + NK], sq[:, :, 0:2 * KV_W].rearrange("p t (h d) -> p t h d", d=HD), X,
                                  ALU.add).then_inc(sums, 1)
                dve.wait_ge(roots, 1)
                dve.reciprocal(ssq[:], ssq[:])
                dve.drain()
                q_r = ssq[:, 0:NQ].rearrange("p (t h) -> p t h", t=NT)
                dve.tensor_scalar(q_r, q_r, HD ** -0.5, None, ALU.mult)
                dve.drain()
                nq_h = nq[:].rearrange("p t (h d) -> p t h d", d=HD)
                dve.tensor_tensor(nq_h, nq_h, q_r.unsqueeze(3).to_broadcast([P, NT, NH, HD]), ALU.mult)
                kv_h = kv[:].rearrange("p t (h d) -> p (t h) d", d=HD)
                dve.tensor_tensor(kv_h, kv_h, ssq[:, NQ:NQ + NK].unsqueeze(2).to_broadcast([P, NK, HD]), ALU.mult)
                dve.drain()
                dve.tensor_tensor(keep.qa[:, :, :, 0:HD], nq_h,
                                  gains[:, 0, :].unsqueeze(1).unsqueeze(1).to_broadcast([P, NT, NH, HD]), ALU.mult)
                for b in range(2):
                    part = kv[:, :, b * KV_W:(b + 1) * KV_W].rearrange("p t (g d) -> p t g d", d=HD)
                    dve.tensor_tensor(part, part, gains[:, 2 + b, :].unsqueeze(1).unsqueeze(1).to_broadcast([P, NT, G, HD]),
                                      ALU.mult)
                dve.drain()

        with Pool_(nc, name + "T") as s:
            ps = s.ps("ps", [P, 8, 4, P])
            turned, taken = s.sems("turned", 8), s.sems("taken", 8)
            jobs = [(QR, keep.qa[:, t, h, :], keep.qT[0:QR, t * NH + h, :]) for t in range(NT) for h in range(NH)]
            jobs += [(HD, kv[:, t, b * KV_W + g * HD:b * KV_W + (g + 1) * HD], (b, g, t))
                     for b in range(2) for g in range(G) for t in range(NT)]

            with nc.Block() as block:
                @block.tensor
                def _(pe):
                    for n, (rows, src, dst) in enumerate(jobs):
                        bank = n // 4
                        if n % 4 == 0 and bank >= 8:
                            pe.wait_ge(taken[bank % 8], bank // 8)
                        last = pe.transpose(ps[0:rows, bank % 8, n % 4, :], src, cst.ident[:])
                        if n % 4 == 3:
                            last.then_inc(turned[bank % 8], 1)

                def take(eng, copy, which):
                    for bank in range(len(jobs) // 4):
                        if bank % 2 != which:
                            continue
                        rows, _, dst = jobs[4 * bank]
                        if isinstance(dst, tuple):
                            b, g, t = dst
                            out = keep.kT[0:HD, b, g, t * P:(t + 4) * P].rearrange("p (a b) -> p a b", a=4)
                        else:
                            out = keep.qT[0:QR, 4 * bank:4 * bank + 4, :]
                        eng.wait_ge(turned[bank % 8], bank // 8 + 1)
                        copy(out, ps[0:rows, bank % 8, :, :]).then_inc(taken[bank % 8], 1)

                @block.scalar
                def _(act):
                    take(act, lambda o, i: act.activation(o, i, ACT.Copy), 0)

                @block.vector
                def _(dve):
                    take(dve, lambda o, i: dve.tensor_copy(o, i), 1)

        with Pool_(nc, name + "C") as s:
            L = CMP_STRIDE
            xb = sq[:].rearrange("p t w -> p (t w)")[:, 0:L * G * NC_].rearrange("p (l g n) -> p l g n", l=L, g=G)
            peT = s.sb("peT", [P, 2, L])
            w1s = nq[:].rearrange("p t w -> p (t w)").rearrange("p (j l n) -> p j l n", j=2, l=L)
            w2s = s.sb("w2s", [P, 2, HD])
            hid = s.sb("hid", [P, G, 2, NC_])
            kc = s.sb("kc", [NC_, G, HD])
            ksq = s.sb("ksq", [NC_, G, HD])
            kss = s.sb("kss", [NC_, G])
            ps_x = s.ps("ps_x", [P, G, S])
            ps_h = s.ps("ps_h", [P, G, NC_])
            ps_k = s.ps("ps_k", [P, G, HD])
            ps_t = s.ps("ps_t", [HD, G, NC_])
            w_loaded, x_turned, xb_ready, h_done, hid_ready = (
                s.sem(n) for n in ("w_loaded", "x_turned", "xb_ready", "h_done", "hid_ready"))
            k_done, k_sq, k_sum, k_root, k_ready, k_turned, v_done, v_taken = (
                s.sem(n) for n in ("k_done", "k_sq", "k_sum", "k_root", "k_ready", "k_turned", "v_done", "v_taken"))

            with nc.Block() as block:
                @block.sync
                def _(sp):
                    for j in range(2):
                        for a in range(2):
                            rows = slice(a * HD, (a + 1) * HD)
                            sp.dma_start(peT[rows, j, :], pe[j, a * L:(a + 1) * L, :].rearrange("l d -> d l"),
                                         allow_slow_non_contiguous=True).then_inc(w_loaded, 16)
                            sp.dma_start(w1s[rows, j, :, :],
                                         w1[j, a * L * HD:(a + 1) * L * HD, :].rearrange("(l d) n -> d l n", d=HD)
                                         ).then_inc(w_loaded, 16)
                    sp.dma_start(w2s[:], w2.rearrange("j p d -> p j d")).then_inc(w_loaded, 16)

                @block.tensor
                def _(pe_):
                    for j in range(2):
                        if j:
                            pe_.wait_ge(xb_ready, 1)
                        for g in range(G):
                            for t in range(NT):
                                last = pe_.transpose(ps_x[:, g, t * P:(t + 1) * P],
                                                     kvc2[:, j, t, g, :, :].rearrange("p a d -> p (a d)"), cst.ident[:])
                        last.then_inc(x_turned, 1)
                        pe_.wait_ge(xb_ready, j + 1)
                        pe_.wait_ge(w_loaded, 16 * 9)
                        for l in range(L):
                            last = pe_.matmul(ps_h[:], w1s[:, j, l, :], xb[:, l, :, :], start=(l == 0), stop=(l == L - 1))
                        last.then_inc(h_done, 1)
                        pe_.wait_ge(hid_ready, j + 1)
                        if j == 0:
                            for g in range(G):
                                last = pe_.matmul(ps_k[0:NC_, g, :], hid[:, g, 0, :], w2s[:, 0, :], start=True, stop=True)
                            last.then_inc(k_done, 1)
                            pe_.wait_ge(k_ready, 1)
                            for g in range(G):
                                last = pe_.transpose(ps_t[:, g, :], kc[:, g, :], cst.ident[0:NC_, 0:NC_])
                            last.then_inc(k_turned, 1)
                        else:
                            for g in range(G):
                                last = pe_.matmul(ps_k[:, g, :], hid[:, g, :, :].rearrange("p a n -> p (a n)"), w2s[:, 1, :], start=True, stop=True)
                            last.then_inc(v_done, 1)

                @block.scalar
                def _(act):
                    for j in range(2):
                        act.wait_ge(h_done, j + 1)
                        act.activation(hid[:], ps_h[:].unsqueeze(2).to_broadcast([P, G, 2, NC_]), ACT.Gelu_apprx_tanh).then_inc(hid_ready, 1)
                        if j == 0:
                            act.wait_ge(k_done, 1)
                            act.activation(ksq[:], ps_k[0:NC_, :, :], ACT.Square).then_inc(k_sq, 1)
                            act.wait_ge(k_sum, 1)
                            act.activation(kss[:], kss[:], ACT.Sqrt, bias=eps[0:NC_, :], scale=1.0 / HD).then_inc(k_root, 1)

                @block.vector
                def _(dve):
                    dve.memset(xb, 0.0)
                    dve.memset(keep.v_cmp[:], 0.0)
                    dve.drain()
                    dve.wait_ge(w_loaded, 16 * 9)
                    for j in range(2):
                        dve.wait_ge(x_turned, j + 1)
                        if j:
                            dve.wait_ge(h_done, 1)
                        for a in range(2):
                            rows, n = slice(a * HD, (a + 1) * HD), NC_ - a
                            for g in range(G):
                                last = dve.tensor_tensor(
                                    xb[rows, :, g, 0:n],
                                    ps_x[rows, g, a * L:S].rearrange("p (n l) -> p l n", l=L),
                                    peT[rows, j, :].unsqueeze(2).to_broadcast([HD, L, n]), ALU.add)
                        last.then_inc(xb_ready, 1)
                        if j == 0:
                            dve.wait_ge(k_sq, 1)
                            dve.tensor_reduce(kss[:], ksq[:], X, ALU.add).then_inc(k_sum, 1)
                            dve.wait_ge(k_root, 1)
                            dve.reciprocal(kss[:], kss[:])
                            dve.drain()
                            dve.tensor_tensor(kc[:], ps_k[0:NC_, :, :], kss[:].unsqueeze(2).to_broadcast([NC_, G, HD]), ALU.mult)
                            dve.drain()
                            dve.tensor_tensor(kc[:], kc[:], gains[0:NC_, 1, :].unsqueeze(1).to_broadcast([NC_, G, HD]), ALU.mult
                                              ).then_inc(k_ready, 1)
                            dve.wait_ge(k_turned, 1)
                            dve.tensor_copy(keep.kcT[0:HD, :, :], ps_t[:]).then_inc(v_taken, 1)
                        else:
                            dve.wait_ge(v_done, 1)
                            for a in range(2):
                                rows = slice(a * HD, (a + 1) * HD)
                                dve.tensor_copy(keep.v_cmp[rows, :, a * HD:(a + 1) * HD], ps_k[rows, :, :])
                            dve.drain()

    with Pool_(nc, name + "S") as s:
        BATCH = NT // 2
        pc = s.sb("pc", [P, NT, NH, NC_])
        mx = s.sb("mx", [P, NT * NH])
        hs = s.sb("hs", [P, NT, G, NC_])
        imp = s.sb("imp", [P, NT, G, NS])
        best = s.sb("best", [P, NT * G, 8])
        left = s.sb("left", [P, NT * G, NS])
        bias_q = s.sb("bias_q", [P, NT, G * NS], BF16)
        scored, shifted, exped, prob_ready, picked = (
            s.sem(n) for n in ("scored", "shifted", "exped", "prob_ready", "picked"))
        with Pool_(nc, name + "S1") as b1:
            ps = b1.ps("ps", [P, NT, NH, NC_])
            with nc.Block() as block:
                @block.tensor
                def _(pe_):
                    for t in range(NT):
                        c_mask = keep.masks[:, 2 * P + t * NC_:2 * P + (t + 1) * NC_]
                        for h in range(NH):
                            pe_.matmul(ps[:, t, h, :], keep.ident_b[:], c_mask, start=True, stop=False)
                            last = pe_.matmul(ps[:, t, h, :], keep.qT[0:QR, t * NH + h, :], keep.kcT[0:QR, h // R, :],
                                              start=False, stop=True)
                        if t % BATCH == BATCH - 1:
                            last.then_inc(scored, 1)

                @block.scalar
                def _(act):
                    for b in range(2):
                        at = slice(b * BATCH, (b + 1) * BATCH)
                        act.wait_ge(shifted, b + 1)
                        act.activation(pc[:, at, :, :], pc[:, at, :, :], ACT.Exp).then_inc(exped, 1)

                @block.vector
                def _(dve):
                    n = BATCH * NH

                    def shift(b):
                        at = slice(b * BATCH, (b + 1) * BATCH)
                        m_b = mx[:, b * n:(b + 1) * n]
                        src = ps[:, at, :, :].rearrange("p t h n -> p (t h) n")
                        dve.wait_ge(scored, b + 1)
                        dve.tensor_reduce(m_b, src, X, ALU.max)
                        dve.drain()
                        dve.tensor_scalar(m_b, m_b, -1e20, None, ALU.max)
                        dve.drain()
                        dve.tensor_tensor(pc[:, at, :, :].rearrange("p t h n -> p (t h) n"), src,
                                          m_b.unsqueeze(2).to_broadcast([P, n, NC_]), ALU.subtract).then_inc(shifted, 1)

                    def select(b):
                        at = slice(b * BATCH, (b + 1) * BATCH)
                        m_b = mx[:, b * n:(b + 1) * n]
                        p_b = pc[:, at, :, :].rearrange("p t h n -> p (t h) n")
                        dve.wait_ge(exped, b + 1)
                        dve.tensor_reduce(m_b, p_b, X, ALU.add)
                        dve.drain()
                        dve.tensor_scalar(m_b, m_b, 1e-30, None, ALU.max)
                        dve.drain()
                        dve.reciprocal(m_b, m_b)
                        dve.drain()
                        dve.tensor_tensor(p_b, p_b, m_b.unsqueeze(2).to_broadcast([P, n, NC_]), ALU.mult
                                          ).then_inc(prob_ready, 1)
                        dve.drain()
                        dve.tensor_reduce(hs[:, at, :, :].rearrange("p t g n -> p (t g) n"),
                                          pc[:, at, :, :].rearrange("p t (g r) n -> p (t g) n r", g=G), X, ALU.add)
                        dve.drain()
                        h_b = hs[:, at, :, :].rearrange("p t g n -> p (t g) n")
                        i_b = imp[:, at, :, :].rearrange("p t g j -> p (t g) j")
                        dve.tensor_reduce(i_b, h_b.rearrange("p a (j i) -> p a j i", i=4), X, ALU.add)
                        dve.drain()
                        dve.tensor_tensor(i_b[:, :, 1:NS], i_b[:, :, 1:NS], h_b[:, :, 3:NC_ - 1:4], ALU.add)
                        dve.drain()
                        dve.tensor_tensor(imp[:, at, :, :], imp[:, at, :, :],
                                          keep.forced[:, at, :].unsqueeze(2).to_broadcast([P, BATCH, G, NS]), ALU.add)
                        dve.drain()
                        pairs = range(b * BATCH * G, (b + 1) * BATCH * G)
                        flat = imp[:].rearrange("p t g j -> p (t g) j")
                        for a in pairs:
                            dve.max(best[:, a, :], flat[:, a, :])
                        dve.drain()
                        for a in pairs:
                            dve.match_replace(left[:, a, :], best[:, a, :], flat[:, a, :], -3e38)
                        dve.drain()
                        dve.tensor_scalar(bias_q[:, at, :].rearrange("p t j -> p (t j)"),
                                          left[:, pairs[0]:pairs[-1] + 1, :].rearrange("p a j -> p (a j)"),
                                          -3e38, NEG, ALU.not_equal, ALU.mult).then_inc(picked, 1)

                    shift(0)
                    shift(1)
                    select(0)
                    select(1)
                    dve.drain()

        with Pool_(nc, name + "S2") as b2:
            pT = b2.sb("pT", [P, 2, NH // 2, P])
            ps_sel = b2.ps("ps_sel", [G * NS, NT, P], BF16)
            ps_p = b2.ps("ps_p", [P, 2, NH // 2, P])
            ps_o = b2.ps("ps_o", [P, 2, NSA_W])
            sel_turned, p_turned, pT_ready = b2.sem("sel_turned"), b2.sems("p_turned"), b2.sems("pT_ready")
            o_done, o_taken = b2.sems("o_done"), b2.sems("o_taken")
            g_exp, g_gate = b2.sem("g_exp"), b2.sem("g_gate")
            with nc.Block() as block:
                @block.tensor
                def _(pe_):
                    for t in range(NT):
                        last = pe_.transpose(ps_sel[:, t, :], bias_q[:, t, :], keep.ident_b[:])
                    last.then_inc(sel_turned, 1)

                    def turn(t):
                        u = t % 2
                        if t >= 2:
                            pe_.wait_ge(pT_ready[u], t // 2)
                        for a in range(NH // 2):
                            last = pe_.transpose(ps_p[:, u, a, :], pc[:, t, 2 * a:2 * a + 2, :], cst.ident[:])
                        last.then_inc(p_turned[u], 1)

                    turn(0)
                    for t in range(NT):
                        u = t % 2
                        if t + 1 < NT:
                            turn(t + 1)
                        pe_.wait_ge(pT_ready[u], t // 2 + 1)
                        if t >= 2:
                            pe_.wait_ge(o_taken[u], t // 2)
                        for a in range(NH // 2):
                            last = pe_.matmul(ps_o[:, u, a * P:(a + 1) * P], pT[:, u, a, :], keep.v_cmp[:, 2 * a // R, :],
                                              start=True, stop=True)
                        last.then_inc(o_done[u], 1)

                @block.scalar
                def _(act):
                    act.activation(keep.gate[:], keep.gate[:], ACT.Exp, scale=-1.0).then_inc(g_exp, 1)
                    for t in range(NT):
                        act.wait_ge(p_turned[t % 2], t // 2 + 1)
                        if t >= 2:
                            act.wait_ge(o_done[t % 2], t // 2)
                        act.activation(pT[:, t % 2, :, :], ps_p[:, t % 2, :, :], ACT.Copy).then_inc(pT_ready[t % 2], 1)

                @block.vector
                def _(dve):
                    dve.wait_ge(g_exp, 1)
                    dve.tensor_scalar(keep.gate[:], keep.gate[:], 1.0, None, ALU.add)
                    dve.drain()
                    dve.reciprocal(keep.gate[:], keep.gate[:])
                    dve.wait_ge(sel_turned, 1)
                    dve.tensor_copy(keep.selT[:], ps_sel[:])
                    dve.drain()
                    for t in range(NT):
                        dve.wait_ge(o_done[t % 2], t // 2 + 1)
                        g_cmp = keep.gate[:, t, :].rearrange("p (h b) -> p h b", b=N_BRANCH)[:, :, 0]
                        dve.tensor_tensor(keep.o[:, t, :].rearrange("p (h d) -> p h d", d=HD),
                                          ps_o[:, t % 2, :].rearrange("p (h d) -> p h d", d=HD),
                                          g_cmp.unsqueeze(2).to_broadcast([P, NH, HD]), ALU.mult).then_inc(o_taken[t % 2], 1)
                    dve.drain()


def sparse_attend(nc, name, cst, keep, y_out):
    FAR = WINDOW // P
    SELB, WINB = 0, 1
    units = []
    for t in range(NT):
        for h in range(NH):
            units.append((t, h, SELB, 0, t + 1))
            first = max(0, t - FAR)
            units.append((t, h, WINB, first, t + 1 - first))
    PIECE = COLS // P
    pieces = [[(a, min(PIECE, n - a)) for a in range(0, n, PIECE)] for *_, n in units]
    with Pool_(nc, name) as m:
        prob = m.sb("prob", [P, 2, S])
        probT = m.sb("probT", [P, 2, NT, P])
        low = m.sb("low", [P, 4])
        mass = m.sb("mass", [P, 2, 2, NH])
        coef = m.sb("coef", [P, 2, NH])
        mixed = m.sb("mixed", [P, 2, NH, HD])
        ps_s = m.ps("ps_s", [P, 2, S])
        ps_t = m.ps("ps_t", [P, 2, COLS])
        ps_o = m.ps("ps_o", [P, 2, NSA_W])
        scored, lowest, exped, turned, turned_out, valued = (
            m.sem(n) for n in ("scored", "lowest", "exped", "turned", "turned_out", "valued"))
        o_free, tile_done, stored = m.sem("o_free"), m.sem("tile_done"), m.sem("stored")
        n_pieces = [0]
        for p in pieces:
            n_pieces.append(n_pieces[-1] + len(p))

        with nc.Block() as block:
            @block.tensor
            def _(pe):
                def score(n):
                    t, h, b, first, tiles = units[n]
                    s, g = n % 2, h // R
                    if n >= 2:
                        pe.wait_ge(exped, n - 1)
                    for a, k in pieces[n]:
                        keys = slice((first + a) * P, (first + a + k) * P)
                        out = ps_s[:, s, a * P:(a + k) * P]
                        masks = []
                        if first + a + k == t + 1:
                            masks.append((k - 1, keep.masks[:, 0:P]))
                        if b == WINB and first == t - FAR and a == 0:
                            masks.append((0, keep.masks[:, P:2 * P]))
                        for j, (at, mask) in enumerate(masks):
                            pe.matmul(ps_s[:, s, (a + at) * P:(a + at + 1) * P], keep.ident_b[:], mask,
                                      start=(j == 0), stop=False, skip_group_check=True)
                        if b == SELB:
                            pe.matmul(out, keep.selT[:, t, :], keep.picks[:, g * S + keys.start:g * S + keys.stop],
                                      start=not masks, stop=False, skip_group_check=True)
                        last = pe.matmul(out, keep.qT[0:QR, t * NH + h, :], keep.kT[0:QR, b, g, keys],
                                         start=(b == WINB and not masks), stop=True, skip_group_check=True)
                    last.then_inc(scored, 1)

                def turn(n):
                    pe.wait_ge(exped, n + 1)
                    for j, (a, k) in enumerate(pieces[n]):
                        q = n_pieces[n] + j
                        if q >= 2:
                            pe.wait_ge(turned_out, q - 1)
                        for i in range(k):
                            last = pe.transpose(ps_t[:, q % 2, i * P:(i + 1) * P],
                                                prob[:, n % 2, (a + i) * P:(a + i + 1) * P], cst.ident[:])
                        last.then_inc(turned, 1)

                def value(n):
                    t, h, b, first, tiles = units[n]
                    pe.wait_ge(turned_out, n_pieces[n + 1])
                    if h == 0 and b == 0 and t:
                        pe.wait_ge(o_free, t)
                    g = h // R
                    for i in range(tiles):
                        last = pe.matmul(ps_o[:, b, h * HD:(h + 1) * HD], probT[:, n % 2, i, :],
                                         keep.v[:, first + i, b, g * HD:(g + 1) * HD], start=(i == 0), stop=(i == tiles - 1))
                    last.then_inc(valued, 1)

                score(0)
                for n in range(len(units)):
                    if n + 1 < len(units):
                        score(n + 1)
                    if n:
                        value(n - 1)
                    turn(n)
                value(len(units) - 1)

            def take(eng, copy, n, j):
                a, k = pieces[n][j]
                q = n_pieces[n] + j
                eng.wait_ge(turned, q + 1)
                if n >= 2:
                    eng.wait_ge(valued, n - 1)
                eng.wait_ge(turned_out, q)
                copy(probT[:, n % 2, a:a + k, :], ps_t[:, q % 2, 0:k * P]).then_inc(turned_out, 1)

            @block.scalar
            def _(act):
                def exps(n):
                    t, h, b, first, tiles = units[n]
                    act.wait_ge(lowest, n + 1)
                    if n >= 2:
                        act.wait_ge(turned, n_pieces[n - 1])
                    if h == 0 and b == 0 and t >= 2:
                        act.wait_ge(o_free, t - 1)
                    act.activation(prob[:, n % 2, 0:tiles * P], ps_s[:, n % 2, 0:tiles * P], ACT.Exp,
                                   bias=low[:, n % 4:n % 4 + 1], accum_out=mass[:, t % 2, b, h:h + 1]).then_inc(exped, 1)

                for n in range(len(units)):
                    exps(n)

            @block.vector
            def _(dve):
                def maximum(n):
                    tiles = units[n][-1]
                    dve.wait_ge(scored, n + 1)
                    if n >= 4:
                        dve.wait_ge(exped, n - 3)
                    dve.tensor_reduce(low[:, n % 4:n % 4 + 1], ps_s[:, n % 2, 0:tiles * P], X, ALU.max, negate=True
                                      ).then_inc(lowest, 1)

                def mix(t):
                    dve.wait_ge(valued, 2 * NH * (t + 1))
                    gate = keep.gate[:, t, :].rearrange("p (h b) -> p b h", b=N_BRANCH)[:, 1:3, :]
                    dve.reciprocal(coef[:], mass[:, t % 2, :, :])
                    dve.drain()
                    dve.tensor_tensor(coef[:], coef[:], gate, ALU.mult)
                    dve.drain()
                    dve.tensor_tensor(mixed[:], ps_o[:].rearrange("p b (h d) -> p b h d", d=HD),
                                      coef[:].unsqueeze(3).to_broadcast([P, 2, NH, HD]), ALU.mult).then_inc(o_free, 1)
                    dve.drain()
                    for b in range(2):
                        last = dve.tensor_tensor(keep.o[:, t, :], keep.o[:, t, :],
                                                 mixed[:, b, :, :].rearrange("p h d -> p (h d)"), ALU.add)
                        if b:
                            last.then_inc(tile_done, 1)
                        dve.drain()

                maximum(0)
                for n in range(len(units)):
                    if n + 1 < len(units):
                        maximum(n + 1)
                    for j in range(len(pieces[n])):
                        take(dve, lambda o, i: dve.tensor_copy(o, i), n, j)
                    t = units[n][0]
                    if t and n == 2 * NH * t:
                        mix(t - 1)
                mix(NT - 1)

            @block.sync
            def _(sp):
                for t in range(NT):
                    sp.wait_ge(tile_done, t + 1)
                    sp.dma_start(y_out[t * P:(t + 1) * P, RET_W:RET_W + NSA_W], keep.o[:, t, :]).then_inc(stored, 16)
                sp.wait_ge(stored, 16 * NT)


def sparse_constants(con):
    f = np.float32
    slopes = f(2) ** (f(-8) * np.arange(1, NH + 1, dtype=f) / f(NH))
    tok = np.arange(S).reshape(NT, P).T
    j = np.arange(NS)
    away = (SEL * j[None, None, :] - tok[:, :, None]).astype(f)
    rows = np.concatenate([slopes[None, None, :, None] * away[:, :, None, :],
                           np.broadcast_to(slopes[None, None, :, None], (P, NT, NH, 1))], axis=3)
    con["q_rows"] = rows.reshape(P, -1)

    def key_rows(at):
        return np.concatenate([(at[None, :] // SEL == j[:, None]), (at % SEL)[None, :] * (at < S)[None, :]], axis=0)
    con["key_rows"] = key_rows(np.arange(S))
    con["cmp_rows"] = key_rows(np.arange(NC_) * CMP_STRIDE + 2 * CMP_STRIDE - 1)
    q_block = tok[:, :, None] // SEL
    forced = (j == 0) | (j == q_block) | (j == q_block - 1)
    con["forced"] = np.where(forced, 1e3, np.where(SEL * j <= tok[:, :, None], 0.0, -1e3)).reshape(P, -1)
    p = np.arange(P)
    causal = np.where(p[None, :] <= p[:, None], 0.0, NEG)
    far = np.where(p[None, :] > p[:, None], 0.0, NEG)
    cmp_end = np.arange(NC_) * CMP_STRIDE + 2 * CMP_STRIDE - 1
    c_mask = np.where(cmp_end[None, None, :] <= tok[:, :, None], 0.0, NEG).reshape(P, -1)
    con["masks"] = np.concatenate([causal, far, c_mask], axis=1)
    picks = np.zeros((G, NS, G, S))
    for g in range(G):
        picks[g, :, g, :] = np.arange(S)[None, :] // SEL == j[:, None]
    con["picks"] = picks.reshape(G * NS, G * S)
    return {k: np.ascontiguousarray(v, dtype=f) for k, v in con.items()}


class Kept:

    def __init__(self, m):
        self.v = m.sb("v", [P, NT, 2, KV_W])
        self.gate = m.sb("gate", [P, NT, NH * N_BRANCH])
        self.kT = m.sb("kT", [QR, 2, G, S])
        self.kcT = m.sb("kcT", [QR, G, NC_])
        self.qT = m.sb("qT", [QR, NT * NH, P])
        self.forced = m.sb("forced", [P, NT, NS])
        self.masks = m.sb("masks", [P, 2 * P + NT * NC_], BF16)
        self.picks = m.sb("picks", [G * NS, G * S], BF16)
        self.ident_b = m.sb("ident_b", [P, P], BF16)
        self.v_cmp = m.sb("v_cmp", [P, G, 2 * HD])
        self.selT = m.sb("selT", [G * NS, NT, P], BF16)
        self.o = m.sb("o", [P, NT, NSA_W])


def sparse_attention(nc, name, proj, q_gain, k_gains, pe, w1, w2, cst, con, y_out):
    with Pool_(nc, name) as m:
        keep = Kept(m)
        with Pool_(nc, name + "_first") as first:
            keep.qa = first.sb("qa", [P, NT, NH, QR])
            keep.q_rows = first.sb("q_rows", [P, NT, NH, NS + 1])
            keep.masks_f = first.sb("masks_f", [P, 2 * P + NT * NC_])
            keep.picks_f = first.sb("picks_f", [G * NS, G * S])
            sparse_prepare(nc, name + "p", m, proj, q_gain, k_gains, pe, w1, w2, cst, con, keep)
        sparse_attend(nc, name + "a", cst, keep, y_out)


def trunk(nc, a, con, out):
    ctx = ExitStack()
    with ctx:
        def dram(name, shape, dt=F32):
            return nc.dram_tensor(name, shape, dt).ap()

        proj = dram("proj", [S, IN_W])
        mixer = dram("mixer", [S, D])
        stream = [dram(f"stream{j}", [S, D]) for j in range(3)]
        xn = dram("xn", [S, D])
        table = dram("table", [NE * CAP, 2], I32)
        slots = dram("slots", [2 * S, D])

        with Pool_(nc, "all") as top:
            cst = Constants(top)
            gates = top.sb("gates", [P, 2 * NT])
            most = top.sb("most", [P, 1], I32)
            with nc.Block() as block:
                constants(nc, cst, block)

            def moe(layer, src):
                with Pool_(nc, f"moe{layer}") as m:
                    xT = m.sb("xT", [P, KT, S])
                    norm_transpose(nc, f"fn{layer}", src, cst.ident, xT, gain=a["ffn_norm_g"][layer, :], xn_dram=xn)
                    route(nc, f"rt{layer}", xT, a["moe_wg_group"][layer, :, :], a["moe_bg_group"][layer, :],
                          a["moe_wg_expert"][layer, :, :], a["moe_bg_expert"][layer, :], table, gates, most, cst)
                experts(nc, f"ex{layer}", xn, a["moe_w_gate"][layer, :, :, :], a["moe_w_up"][layer, :, :, :],
                        a["moe_w_down"][layer, :, :, :], table, slots, most, cst.ident)

            with Pool_(nc, "in") as m:
                xT_hi, xT_lo = m.sb("xT_hi", [P, KT, S], F32R), m.sb("xT_lo", [P, KT, S], F32R)
                norm_transpose(nc, "mn0", a["x"][0, :, :], cst.ident, xT_hi, xT_lo, gain=a["mix_norm_g"][0, :])
                project(nc, "in0", xT_hi, xT_lo, a["ev_w_in"][0, :, :], IN_W, proj)
            retention(nc, "ret", proj, a["ev_ret_norm_g"][0, :], cst.ident, con, mixer)
            sparse_attention(nc, "nsa", proj, a["ev_q_norm_g"][0, :], a["ev_k_norm_g"][0, :, :],
                             a["ev_cmp_pe"][0, :, :, :], a["ev_w_cmp1"][0, :, :, :], a["ev_w_cmp2"][0, :, :, :],
                             cst, con, mixer)
            with Pool_(nc, "out") as m:
                xT_hi, xT_lo = m.sb("xT_hi", [P, KT, S], F32R), m.sb("xT_lo", [P, KT, S], F32R)
                norm_transpose(nc, "tr0", mixer, cst.ident, xT_hi, xT_lo)
                project(nc, "out0", xT_hi, xT_lo, a["ev_w_out"][0, :, :], D, stream[0], residual=a["x"][0, :, :])
            moe(0, stream[0])

            with Pool_(nc, "odd") as m:
                zT_hi, zT_lo = m.sb("zT_hi", [P, KT, S], F32R), m.sb("zT_lo", [P, KT, S], F32R)
                with Pool_(nc, "oddx") as x:
                    xT_hi, xT_lo = x.sb("xT_hi", [P, KT, S], F32R), x.sb("xT_lo", [P, KT, S], F32R)
                    norm_transpose(nc, "mn1", stream[0], cst.ident, xT_hi, xT_lo, gain=a["mix_norm_g"][1, :],
                                   mix=(slots, gates, stream[1]))
                    gated_conv(nc, "conv", xT_hi, xT_lo, a["od_w_in"][0, :, :], a["od_conv_w"][0, :, :],
                               a["od_conv_b"][0, :], zT_hi, zT_lo)
                project(nc, "out1", zT_hi, zT_lo, a["od_w_out"][0, :, :], D, stream[2], residual=stream[1])
            moe(1, stream[2])
            finish(nc, "end", stream[2], slots, gates, out)


def finish(nc, name, src, slots, gates, out):
    with Pool_(nc, name) as m:
        rows = m.sb("rows", [P, NT, D])
        ya = m.sb("ya", [P, 2, 2, D])
        loaded, mixed, stored = m.sems("loaded", NT), m.sem("mixed"), m.sem("stored")
        with nc.Block() as block:
            @block.sync
            def _(sp):
                for t in range(NT):
                    sp.dma_start(rows[:, t, :], src[t * P:(t + 1) * P, :]).then_inc(loaded[t], 16)
                    if t >= 2:
                        sp.wait_ge(mixed, t - 1)
                    for c in range(2):
                        at = c * S + t * P
                        sp.dma_start(ya[:, t % 2, c, :], slots[at:at + P, :]).then_inc(loaded[t], 16)

            @block.vector
            def _(dve):
                for t in range(NT):
                    dve.wait_ge(loaded[t], 48)
                    for c in range(2):
                        last = dve.scalar_tensor_tensor(rows[:, t, :], ya[:, t % 2, c, :],
                                                        gates[:, c * NT + t:c * NT + t + 1], rows[:, t, :], ALU.mult, ALU.add)
                        if c == 0:
                            dve.drain()
                    last.then_inc(mixed, 1)

            @block.scalar
            def _(act):
                for t in range(NT):
                    act.wait_ge(mixed, t + 1)
                    act.dma_start(out[t * P:(t + 1) * P, :], rows[:, t, :]).then_inc(stored, 16)
                act.wait_ge(stored, 16 * NT)


class Constants:
    def __init__(self, m):
        self.ident, self.ones, self.before = (m.sb(n, [P, P]) for n in ("ident", "ones", "before"))
        self.iota, self.iota_i = m.sb("iota", [P, 64]), m.sb("iota_i", [P, 64], I32)


INPUTS = ["x", "mix_norm_g", "ffn_norm_g", "ev_w_in", "ev_cmp_pe", "ev_w_cmp1", "ev_w_cmp2", "ev_q_norm_g", "ev_k_norm_g",
          "ev_ret_norm_g", "ev_w_out", "od_w_in", "od_conv_w", "od_conv_b", "od_w_out", "moe_wg_group", "moe_bg_group",
          "moe_wg_expert", "moe_bg_expert", "moe_w_gate", "moe_w_up", "moe_w_down"]


def kernel(**inputs):
    import concourse.bacc as bacc
    from concourse.bass_utils import run_bass_kernel_spmd

    nc = bacc.Bacc("TRN2", target_bir_lowering=False, num_devices=1)
    arrays = {}

    def given(name, array):
        arrays[name] = np.ascontiguousarray(array)
        return nc.dram_tensor(name, array.shape, mybir.dt.from_np(arrays[name].dtype), kind="ExternalInput").ap()

    a = {n: given(f"in_{n}", np.asarray(inputs[n])) for n in INPUTS}
    con = {n: given(f"con_{n}", v) for n, v in sparse_constants(shape_constants()).items()}
    out = nc.dram_tensor("out", (1, S, D), F32, kind="ExternalOutput").ap()
    trunk(nc, a, con, out[0, :, :])
    r = run_bass_kernel_spmd(nc, [arrays], core_ids=[0])
    return np.asarray(r.results[0]["out"])
```

```python
import numpy as np
import concourse.bass as bass
from concourse import mybir
from contextlib import ExitStack

F32 = mybir.dt.float32
F32R = mybir.dt.float32r
BF16 = mybir.dt.bfloat16
I32 = mybir.dt.int32
ALU = mybir.AluOpType
ACT = mybir.ActivationFunctionType
X = mybir.AxisListType.X
ds = bass.ds

P = 128
S = 1024
D = 1024
NT = S // P
KT = D // P
HD = 64
RH = 8
NH = 8
G = 2
R = NH // G
RET_W = RH * HD
NSA_W = NH * HD
KV_W = G * HD
N_BRANCH = 3
IN_W = 4 * RET_W + NSA_W + 6 * KV_W + NH * N_BRANCH
C_NQ = 4 * RET_W
C_KC = C_NQ + NSA_W
C_VC, C_KS, C_VS, C_KW, C_VW, C_NG = (C_KC + KV_W * n for n in range(1, 7))
CMP_STRIDE = 16
CMP_HID = 128
NC_ = S // CMP_STRIDE
SEL = 64
NS = S // SEL
WINDOW = 256
NG = 4
EPG = 8
NE = NG * EPG
DE = 256
EPS = 1e-6
NEG = -1e30
COLS = 512


class Pool_:

    ENOUGH = 90
    used_up = []

    def __init__(self, nc, name, whole=False):
        self.nc, self.name, self.ctx, self.used, self.whole = nc, name, ExitStack(), [], whole
        if whole:
            Pool_.used_up = []

    def __enter__(self):
        return self

    def __exit__(self, *a):
        Pool_.used_up.extend(self.used)
        if (self.whole or len(Pool_.used_up) > self.ENOUGH) and a[0] is None:
            self.nc.clear_and_free_semaphores(Pool_.used_up)
            self.nc.all_engine_barrier()
            Pool_.used_up = []
        return self.ctx.__exit__(*a)

    def sb(self, name, shape, dt=F32):
        return self.ctx.enter_context(self.nc.sbuf_tensor(f"{self.name}_{name}", shape, dt))

    def ps(self, name, shape, dt=F32):
        return self.ctx.enter_context(self.nc.psum_tensor(f"{self.name}_{name}", shape, dt))

    def sem(self, name):
        self.used.append(self.nc.alloc_semaphore(f"{self.name}_{name}"))
        return self.used[-1]

    def sems(self, name, n=2):
        return [self.sem(f"{name}{j}") for j in range(n)]


def row_of(vec, n=P):
    return bass.AP(tensor=vec.tensor, offset=vec.offset, ap=[[0, n]] + [list(x) for x in vec.ap])


def warm_up(pe, bank, a, b, n=18):
    for _ in range(n):
        pe.matmul(bank, a, b, start=True, stop=True)


def norm_transpose(nc, name, src, ident, xT_hi, xT_lo=None, gain=None, xn_dram=None, mix=None):
    U = 4
    with Pool_(nc, name) as m:
        xin = m.sb("xin", [P, U, D])
        ps_t = m.ps("ps_t", [P, U, KT, P])
        loaded, mixed, stored = m.sems("loaded", U), m.sems("mixed", U), m.sems("stored", U)
        summed, root_ready, normed = m.sems("summed", U), m.sems("root_ready", U), m.sems("normed", U)
        transposed, hi_ready, lo_ready = m.sems("transposed", U), m.sems("hi_ready", U), m.sems("lo_ready", U)
        gain_loaded = m.sem("gain_loaded")
        apart = m.sem("apart")
        if gain is not None:
            gains = m.sb("gains", [P, D])
            xn = m.sb("xn", [P, U, D])
            ssq = m.sb("ssq", [P, U])
            root = m.sb("root", [P, U])
            rstd = m.sb("rstd", [P, U])
            eps = m.sb("eps", [P, 1])
            eps_ready = m.sem("eps_ready")
        if mix is not None:
            slots, gates, mix_out = mix
            ya = m.sb("ya", [P, U, 2, D])
        rows = xn if gain is not None else xin
        n_stores = (mix is not None) + (xn_dram is not None)

        with nc.Block() as block:
            @block.sync
            def _(sp):
                if gain is not None:
                    sp.dma_start(gains[:], row_of(gain)).then_inc(gain_loaded, 16)
                with sp.Fori(0, NT // U) as i:
                    for u in range(U):
                        first, second = sp.snap((U * i + u) * P), sp.snap((U * i + u) * P + S)
                        stores = sp.snap(i * (16 * n_stores)) if mix is not None else None
                        sp.wait_ge(transposed[u], i)
                        if mix is not None:
                            sp.sem_inc(apart, 1)
                            sp.wait_ge(stored[u], stores)
                        sp.dma_start(xin[:, u, :], src[ds(first, P), :]).then_inc(loaded[u], 16)
                        if mix is not None:
                            for c, row in enumerate((first, second)):
                                sp.dma_start(ya[:, u, c, :], slots[ds(row, P), :]
                                             ).then_inc(loaded[u], 16)
                    for u in range(U):
                        first = sp.snap((U * i + u) * P)
                        if mix is not None:
                            sp.wait_ge(mixed[u], i + 1)
                            sp.dma_start(mix_out[ds(first, P), :], xin[:, u, :]).then_inc(stored[u], 16)
                        if xn_dram is not None:
                            sp.wait_ge(normed[u], i + 1)
                            sp.dma_start(xn_dram[ds(first, P), :], xn[:, u, :]).then_inc(stored[u], 16)
                if n_stores:
                    for u in range(U):
                        sp.wait_ge(stored[u], 16 * n_stores * (NT // U))

            @block.scalar
            def _(act):
                if gain is not None:
                    act.wait_ge(eps_ready, 1)
                with act.Fori(0, NT // U) as i:
                    if gain is not None:
                        for u in range(U):
                            if mix is None:
                                act.wait_ge(loaded[u], 16 * i + 16)
                            else:
                                act.wait_ge(mixed[u], i + 1)
                            act.wait_ge(transposed[u], i)
                            if xn_dram is not None:
                                act.wait_ge(stored[u], 16 * n_stores * i)
                            act.activation(xn[:, u, :], xin[:, u, :], ACT.Square,
                                           accum_out=ssq[:, u:u + 1]).then_inc(summed[u], 1)
                            act.wait_ge(summed[u], i + 1)
                            act.wait_ge(normed[u], i)
                            act.activation(root[:, u:u + 1], ssq[:, u:u + 1], ACT.Sqrt, bias=eps[:],
                                           scale=1.0 / D).then_inc(root_ready[u], 1)
                    for u in range(U):
                        act.wait_ge(transposed[u], i + 1)
                        act.activation(xT_hi[:, :, ds((U * i + u) * P, P)], ps_t[:, u, :, :],
                                       ACT.Copy).then_inc(hi_ready[u], 1)

            @block.vector
            def _(dve):
                if gain is not None:
                    dve.memset(eps[:], EPS).then_inc(eps_ready, 1)
                    dve.wait_ge(gain_loaded, 16)
                with dve.Fori(0, NT // U) as i:
                    for u in range(U):
                        if mix is not None:
                            dve.wait_ge(loaded[u], 48 * i + 48)
                            for c in range(2):
                                last = dve.scalar_tensor_tensor(
                                    xin[:, u, :], ya[:, u, c, :], gates[:, ds(U * i + (u + c * NT), 1)],
                                    xin[:, u, :], ALU.mult, ALU.add)
                                if c == 1:
                                    last.then_inc(mixed[u], 1)
                                dve.drain()
                    for u in range(U):
                        if gain is not None:
                            dve.wait_ge(root_ready[u], i + 1)
                            dve.reciprocal(rstd[:, u:u + 1], root[:, u:u + 1])
                            dve.drain()
                            dve.scalar_tensor_tensor(xn[:, u, :], xin[:, u, :], rstd[:, u:u + 1], gains[:],
                                                     ALU.mult, ALU.mult).then_inc(normed[u], 1)
                    for u in range(U):
                        if xT_lo is not None:
                            dve.wait_ge(hi_ready[u], i + 1)
                            at = ds((U * i + u) * P, P)
                            dve.tensor_tensor(xT_lo[:, :, at], ps_t[:, u, :, :], xT_hi[:, :, at].bitcast(F32),
                                              ALU.subtract).then_inc(lo_ready[u], 1)

            @block.tensor
            def _(pe):
                with pe.Fori(0, NT // U) as i:
                    for u in range(U):
                        pe.wait_ge(*((normed[u], i + 1) if gain is not None else (loaded[u], 16 * i + 16)))
                        pe.wait_ge(*((lo_ready[u], i) if xT_lo is not None else (hi_ready[u], i)))
                        for k in range(KT):
                            last = pe.transpose(ps_t[:, u, k, :], rows[:, u, k * P:(k + 1) * P], ident[:])
                        last.then_inc(transposed[u], 1)


def project(nc, name, xT_hi, xT_lo, w, width, out, residual=None):
    full = width // COLS
    with Pool_(nc, name) as m:
        raw = m.sb("raw", [P, 2, KT, COLS])
        w_hi = m.sb("w_hi", [P, 2, KT, COLS], F32R)
        w_lo = m.sb("w_lo", [P, 2, KT, COLS], F32R)
        stage = m.sb("stage", [P, 4, COLS])
        ps = m.ps("ps", [P, NT, COLS])
        raw_loaded = m.sems("raw_loaded", 4)
        hi_ready, lo_ready = m.sems("hi_ready"), m.sems("lo_ready")
        product_ready = m.sems("product_ready", NT - 1)
        last_product = m.sems("last_product")
        tile_out = m.sems("tile_out", NT)
        stage_stored = m.sems("stage_stored", 4)
        res_loaded = m.sems("res_loaded", 4)
        if residual is not None:
            res = m.sb("res", [P, 4, COLS])
        w_k = w.rearrange("(k p) n -> p k n", p=P)

        n_blocks = -(-width // COLS)
        wide = [min(COLS, width - b * COLS) for b in range(n_blocks)]
        HALF = KT // 2

        with nc.Block() as block:
            @block.sync
            def _(sp):
                for b, n in enumerate(wide):
                    if b >= 2:
                        sp.wait_ge(lo_ready[b % 2], 2 * (b // 2))
                    for c in range(2):
                        at = slice(c * HALF, (c + 1) * HALF)
                        sp.dma_start(raw[:, b % 2, at, 0:n], w_k[:, at, b * COLS:b * COLS + n]
                                     ).then_inc(raw_loaded[2 * (b % 2) + c], 16)
                for s in range(4):
                    sp.wait_ge(stage_stored[s], 16 * n_blocks * (NT // 4))

            if residual is not None:
                @block.gpsimd
                def _(pool):
                    for b, n in enumerate(wide):
                        for t in range(NT):
                            if (b, t) >= (0, 4):
                                pool.wait_ge(tile_out[(t + 4) % NT], b + (t >= 4))
                            pool.dma_start(res[:, t % 4, 0:n], residual[t * P:(t + 1) * P, b * COLS:b * COLS + n]
                                           ).then_inc(res_loaded[t % 4], 16)

            @block.scalar
            def _(act):
                def high(b):
                    for c in range(2):
                        at, n = slice(c * HALF, (c + 1) * HALF), wide[b]
                        act.wait_ge(raw_loaded[2 * (b % 2) + c], 16 * (b // 2 + 1))
                        if b >= 2:
                            act.wait_ge(last_product[b % 2], b // 2)
                        act.activation(w_hi[:, b % 2, at, 0:n], raw[:, b % 2, at, 0:n], ACT.Copy
                                       ).then_inc(hi_ready[b % 2], 1)

                high(0)
                for b, n in enumerate(wide):
                    if b + 1 < n_blocks:
                        high(b + 1)
                    for t in range(NT):
                        act.wait_ge(tile_out[t], b + 1)
                        act.dma_start(out[t * P:(t + 1) * P, b * COLS:b * COLS + n], stage[:, t % 4, 0:n]
                                      ).then_inc(stage_stored[t % 4], 16)

            @block.vector
            def _(dve):
                def low(b):
                    for c in range(2):
                        at, n = slice(c * HALF, (c + 1) * HALF), wide[b]
                        dve.wait_ge(hi_ready[b % 2], 2 * (b // 2) + c + 1)
                        dve.tensor_tensor(w_lo[:, b % 2, at, 0:n], raw[:, b % 2, at, 0:n],
                                          w_hi[:, b % 2, at, 0:n].bitcast(F32), ALU.subtract
                                          ).then_inc(lo_ready[b % 2], 1)

                low(0)
                for b, n in enumerate(wide):
                    for t in range(NT):
                        if t == 2 and b + 1 < n_blocks:
                            low(b + 1)
                        if t < NT - 1:
                            dve.wait_ge(product_ready[t], b + 1)
                        else:
                            dve.wait_ge(last_product[b % 2], b // 2 + 1)
                        if (b, t) >= (0, 4):
                            dve.wait_ge(stage_stored[t % 4], 16 * (2 * b + t // 4))
                        if residual is None:
                            last = dve.tensor_copy(stage[:, t % 4, 0:n], ps[:, t, 0:n])
                        else:
                            dve.wait_ge(res_loaded[t % 4], 16 * (2 * b + t // 4 + 1))
                            last = dve.tensor_tensor(stage[:, t % 4, 0:n], ps[:, t, 0:n], res[:, t % 4, 0:n], ALU.add)
                        last.then_inc(tile_out[t], 1)

            @block.tensor
            def _(pe):
                def body(u, i, n):
                    for t in range(NT):
                        pe.wait_ge(tile_out[t], 2 * i + u)
                        at = slice(t * P, (t + 1) * P)
                        for k in range(KT):
                            if t == 0 and k % HALF == 0:
                                pe.wait_ge(lo_ready[u], 2 * i + k // HALF + 1)
                            for j, (a, w_part) in enumerate(((xT_hi, w_hi), (xT_hi, w_lo), (xT_lo, w_hi))):
                                last = pe.matmul(ps[:, t, 0:n], a[:, k, at], w_part[:, u, k, 0:n],
                                                 start=(k == 0 and j == 0), stop=(k == KT - 1 and j == 2))
                        last.then_inc(product_ready[t] if t < NT - 1 else last_product[u], 1)

                with pe.Fori(0, full // 2) as i:
                    for u in range(2):
                        body(u, i, COLS)
                for b in range(full // 2 * 2, n_blocks):
                    body(b % 2, b // 2, wide[b])

CAP = S
NOWHERE = 4 * S


EXPERT_BUFFERS = 4


class ExpertWeights:

    def __init__(self, m, w_gate, w_up, w_down):
        self.gu = m.sb("w_gu", [P, EXPERT_BUFFERS, KT, 2 * DE])
        self.down = m.sb("w_d", [P, EXPERT_BUFFERS, DE // P, D])
        self.gu_loaded, self.down_loaded = m.sems("gu_loaded", EXPERT_BUFFERS), m.sems("down_loaded", EXPERT_BUFFERS)
        self.w_gate, self.w_up, self.w_down = w_gate, w_up, w_down

    def load_gate_up(self, sp, e, buffer):
        for j, src in enumerate((self.w_gate, self.w_up)):
            sp.dma_start(self.gu[:, buffer, :, j * DE:(j + 1) * DE],
                         src[ds(e, 1), :, :].rearrange("a (k p) n -> p (a k) n", p=P)).then_inc(self.gu_loaded[buffer], 16)

    def load_down(self, sp, e, buffer):
        sp.dma_start(self.down[:, buffer, :, :],
                     self.w_down[ds(e, 1), :, :].rearrange("a (k p) n -> p (a k) n", p=P)
                     ).then_inc(self.down_loaded[buffer], 16)


def route(nc, name, xT, w_group, b_group, w_expert, b_expert, table, gates, most, weights, cst):
    NL = NG + NE
    with Pool_(nc, name) as m:
        w = m.sb("w", [P, KT, NL])
        bias = m.sb("bias", [P, NL])
        lg = m.sb("lg", [P, NT, NL])
        t4, e4, v4 = (m.sb(n, [P, NT, NG]) for n in ("t4", "e4", "v4"))
        em, v32 = (m.sb(n, [P, NT, NE]) for n in ("em", "v32"))
        chosen = m.sb("chosen", [P, 2, NT, NE])
        both = m.sb("both", [P, NT, NE])
        small = m.sb("small", [P, 8, NT])
        run = m.sb("run", [P, NT + 1, NE])
        pos = m.sb("pos", [P, NT, NE])
        dest_f = m.sb("dest_f", [P, 2, NT])
        dest = m.sb("dest", [P, 2, NT], I32)
        codes = m.sb("codes", [P, 2, NT, 2], I32)
        nowhere = m.sb("nowhere", [P, NE * CAP * 2 // P], I32)
        most_f = m.sb("most_f", [P, 1])
        ps_l = m.ps("ps_l", [P, NT, 64])
        ps_c = m.ps("ps_c", [P, 2, NT, NE])
        loaded, logits, shifted, exps = m.sem("loaded"), m.sem("logits"), m.sem("shifted"), m.sem("exps")
        chosen_ready, counted, dest_ready = m.sem("chosen_ready"), m.sem("counted"), m.sem("dest_ready")
        filled, cleared, scattered = m.sem("filled"), m.sem("cleared"), m.sem("scattered")
        top, gsum, best, second, e2, den, inv = (small[:, j, :] for j in range(7))

        with nc.Block() as block:
            @block.sync
            def _(sp):
                sp.dma_start(w[:, :, 0:NG], w_group.rearrange("(k p) n -> p k n", p=P)).then_inc(loaded, 16)
                sp.dma_start(w[:, :, NG:NL], w_expert.rearrange("(k p) n -> p k n", p=P)).then_inc(loaded, 16)
                sp.dma_start(bias[:, 0:NG], row_of(b_group)).then_inc(loaded, 16)
                sp.dma_start(bias[:, NG:NL], row_of(b_expert)).then_inc(loaded, 16)
                for e in range(EXPERT_BUFFERS):
                    weights.load_gate_up(sp, e, e)
                    weights.load_down(sp, e, e)

            @block.scalar
            def _(act):
                act.wait_ge(filled, 1)
                act.dma_start(table.rearrange("(p r) c -> p (r c)", p=P), nowhere[:]).then_inc(cleared, 16)
                act.wait_ge(shifted, 1)
                act.activation(e4[:], t4[:], ACT.Exp).then_inc(exps, 1)
                act.wait_ge(shifted, 2)
                act.activation(e2, den, ACT.Exp).then_inc(exps, 1)

            @block.gpsimd
            def _(pool):
                pool.memset(nowhere[:], NOWHERE).then_inc(filled, 1)
                pool.iota(codes[:, :, :, 0], pattern=[[0, 2], [P, NT]], base=0, channel_multiplier=1)
                pool.iota(codes[:, :, :, 1], pattern=[[S, 2], [P, NT]], base=0, channel_multiplier=1)
                pool.drain()
                pool.wait_ge(cleared, 16)
                pool.wait_ge(dest_ready, 1)
                for c in range(2):
                    for t in range(NT):
                        pool.indirect_dma_start(
                            out=table, out_offset=bass.IndirectOffsetOnAxis(ap=dest[:, c, t:t + 1], axis=0),
                            in_=codes[:, c, t, :], in_offset=None).then_inc(scattered, 16)
                pool.wait_ge(scattered, 16 * 2 * NT)

            @block.tensor
            def _(pe):
                pe.wait_ge(loaded, 64)
                for t in range(NT):
                    for k in range(KT):
                        last = pe.matmul(ps_l[:, t, 0:NL], xT[:, k, t * P:(t + 1) * P], w[:, k, :],
                                         start=(k == 0), stop=(k == KT - 1))
                last.then_inc(logits, 1)
                pe.wait_ge(chosen_ready, 1)
                pe.matmul(ps_c[:, 0, :, :], cst.before[:], both[:], start=True, stop=True)
                pe.matmul(ps_c[:, 1, :, :], cst.ones[:], both[:], start=True, stop=True).then_inc(counted, 1)

            @block.vector
            def _(dve):
                def one_hot(out, values, maximum, iota, v, n):
                    wide = [P, NT, n]
                    dve.tensor_tensor(v[:], values, maximum.unsqueeze(2).to_broadcast(wide), ALU.is_equal)
                    dve.drain()
                    dve.scalar_tensor_tensor(v[:], v[:], -64.0, iota.unsqueeze(1).to_broadcast(wide), ALU.mult, ALU.add)
                    dve.drain()
                    dve.tensor_reduce(inv, v[:], X, ALU.min)
                    dve.drain()
                    dve.tensor_tensor(out, v[:], inv.unsqueeze(2).to_broadcast(wide), ALU.is_equal)
                    dve.drain()

                dve.wait_ge(loaded, 64)
                dve.wait_ge(logits, 1)
                dve.tensor_tensor(lg[:], ps_l[:, :, 0:NL], bias[:].unsqueeze(1).to_broadcast([P, NT, NL]), ALU.add)
                dve.drain()
                dve.tensor_reduce(top, lg[:, :, 0:NG], X, ALU.max)
                dve.drain()
                dve.tensor_tensor(t4[:], lg[:, :, 0:NG], top.unsqueeze(2).to_broadcast([P, NT, NG]), ALU.subtract
                                  ).then_inc(shifted, 1)
                one_hot(v4[:], lg[:, :, 0:NG], top, cst.iota[:, 0:NG], v4, NG)
                dve.tensor_scalar(v4[:], v4[:], -1.0, -NEG, ALU.add, ALU.mult)
                dve.drain()
                dve.tensor_tensor(em[:].rearrange("p t (g e) -> p t g e", g=NG),
                                  lg[:, :, NG:NL].rearrange("p t (g e) -> p t g e", g=NG),
                                  v4[:].unsqueeze(3).to_broadcast([P, NT, NG, EPG]), ALU.add)
                dve.drain()
                dve.tensor_reduce(best, em[:], X, ALU.max)
                dve.drain()
                one_hot(chosen[:, 0, :, :], em[:], best, cst.iota[:, 0:NE], v32, NE)
                dve.scalar_tensor_tensor(em[:], chosen[:, 0, :, :], 2 * NEG, em[:], ALU.mult, ALU.add)
                dve.drain()
                dve.tensor_reduce(second, em[:], X, ALU.max)
                dve.drain()
                dve.tensor_tensor(den, second, best, ALU.subtract).then_inc(shifted, 1)
                one_hot(chosen[:, 1, :, :], em[:], second, cst.iota[:, 0:NE], v32, NE)
                dve.tensor_tensor(both[:], chosen[:, 0, :, :], chosen[:, 1, :, :], ALU.add).then_inc(chosen_ready, 1)
                dve.wait_ge(exps, 2)
                dve.tensor_reduce(gsum, e4[:], X, ALU.add)
                dve.drain()
                dve.scalar_tensor_tensor(inv, e2, 1.0, gsum, ALU.add, ALU.mult)
                dve.drain()
                dve.reciprocal(gates[:, 0:NT], inv)
                dve.drain()
                dve.tensor_tensor(gates[:, NT:2 * NT], e2, gates[:, 0:NT], ALU.mult)
                dve.memset(run[:, 0, :], 0.0)
                dve.wait_ge(counted, 1)
                for t in range(NT):
                    dve.drain()
                    dve.tensor_tensor(run[:, t + 1, :], run[:, t, :], ps_c[:, 1, t, :], ALU.add)
                dve.drain()
                dve.tensor_tensor(pos[:], ps_c[:, 0, :, :], run[:, 0:NT, :], ALU.add)
                dve.tensor_reduce(most_f[:], run[:, NT, :], X, ALU.max)
                dve.drain()
                dve.scalar_tensor_tensor(pos[:], cst.iota[:, 0:NE].unsqueeze(1).to_broadcast([P, NT, NE]),
                                         float(CAP), pos[:], ALU.mult, ALU.add)
                dve.tensor_copy(most[:], most_f[:])
                dve.drain()
                for c in range(2):
                    dve.tensor_tensor(v32[:], chosen[:, c, :, :], pos[:], ALU.mult)
                    dve.drain()
                    dve.tensor_reduce(dest_f[:, c, :], v32[:], X, ALU.add)
                    dve.drain()
                dve.tensor_copy(dest[:], dest_f[:]).then_inc(dest_ready, 1)


def experts(nc, name, xn_dram, weights, table, slots, most, ident):
    U, B = 8, EXPERT_BUFFERS
    STEPS = NE // U
    with Pool_(nc, name) as m:
        idx = m.sb("idx", [P, U, 2], I32)
        xg = m.sb("xg", [P, B, D])
        xgT = m.sb("xgT", [P, B, KT, P])
        silu = m.sb("silu", [P, B, DE])
        hid = m.sb("hid", [P, B, DE])
        hidT = m.sb("hidT", [P, B, DE // P, P])
        y = m.sb("y", [P, B, D])
        ps_x = m.ps("ps_x", [P, KT, P])
        ps_h = m.ps("ps_h", [P, 2, 2 * DE])
        ps_t = m.ps("ps_t", [P, 2, 2 * P])
        ps_y = m.ps("ps_y", [P, D])
        w_gu, w_d, gu_loaded, down_loaded = weights.gu, weights.down, weights.gu_loaded, weights.down_loaded
        idx_loaded = m.sems("idx_loaded", U)
        gathered, x_turned, xT_ready = m.sems("gathered", B), m.sems("x_turned", B), m.sems("xT_ready", B)
        h_ready, silu_ready, hid_ready = m.sems("h_ready", B), m.sems("silu_ready", B), m.sems("hid_ready", B)
        h_turned, hT_ready = m.sems("h_turned", B), m.sems("hT_ready", B)
        y_done, y_out, scattered = m.sems("y_done", B), m.sems("y_out", B), m.sems("scattered", U)
        cleared = m.sem("cleared")
        apart = m.sem("apart")

        def waves(eng, body, first=0):
            full = eng.value_load(most[0:1, 0:1], min_val=0, max_val=CAP)
            with eng.Fori(first, CAP // P) as w:
                with eng.If(full > w * P):
                    body(w)

        def steps(eng, w, body):
            with eng.Fori(0, STEPS) as i:
                body(w * STEPS + i)

        def uses(n, u):
            return n * (U // B) + u // B

        with nc.Block() as block:
            @block.sync
            def _(sp):
                def load(w, i, u, prefetched=False):
                    n = w * STEPS + i
                    k = sp.snap(uses(n, u))
                    row, expert = sp.snap((i * U + u) * CAP + w * P), sp.snap(i * U + u)
                    sp.wait_ge(scattered[u], 16 * n)
                    sp.dma_start(idx[:, u, :], table[ds(row, P), :]).then_inc(idx_loaded[u], 16)
                    if not prefetched:
                        sp.wait_ge(h_ready[u % B], k)
                        weights.load_gate_up(sp, expert, u % B)
                        sp.wait_ge(y_done[u % B], k)
                        weights.load_down(sp, expert, u % B)

                def wave(w):
                    with sp.Fori(0, STEPS) as i:
                        for u in range(U):
                            load(w, i, u)

                for u in range(U):
                    load(0, 0, u, prefetched=u < B)
                with sp.Fori(1, STEPS) as i:
                    for u in range(U):
                        load(0, i, u)
                waves(sp, wave, first=1)

            @block.gpsimd
            def _(pool):
                last_token, last_slot = pool.to_reg(S - 1), pool.to_reg(2 * S - 1)
                pool.wait_ge(cleared, 1)

                def gather(n, u):
                    pool.wait_ge(idx_loaded[u], 16 * n + 16)
                    pool.wait_ge(x_turned[u % B], uses(n, u))
                    pool.sem_inc(apart, 1)
                    pool.indirect_dma_start(
                        out=xg[:, u % B, :], out_offset=None, in_=xn_dram,
                        in_offset=bass.IndirectOffsetOnAxis(ap=idx[:, u, 0:1], axis=0),
                        bounds_check=last_token, oob_is_err=False).then_inc(gathered[u % B], 16)

                def scatter(n, u):
                    pool.wait_ge(y_out[u % B], uses(n, u) + 1)
                    pool.sem_inc(apart, 1)
                    pool.indirect_dma_start(
                        out=slots, out_offset=bass.IndirectOffsetOnAxis(ap=idx[:, u, 1:2], axis=0),
                        in_=y[:, u % B, :], in_offset=None,
                        bounds_check=last_slot, oob_is_err=False).then_inc(scattered[u], 16)

                def body(n, more):
                    for u in range(U):
                        if u + B < U:
                            gather(n, u + B)
                        elif more:
                            gather(n + 1, u + B - U)
                        scatter(n, u)

                def wave(w):
                    first = w * STEPS
                    for u in range(B):
                        gather(first, u)
                    with pool.Fori(0, STEPS - 1) as i:
                        body(w * STEPS + i, True)
                    body(first + (STEPS - 1), False)
                    for u in range(U):
                        pool.wait_ge(scattered[u], w * (16 * STEPS) + 16 * STEPS)
                    pool.sem_inc(apart, 1)
                waves(pool, wave)

            @block.tensor
            def _(pe):
                def turn_x(n, u):
                    pe.wait_ge(gathered[u % B], 16 * uses(n, u) + 16)
                    pe.wait_ge(xT_ready[(u - 1) % B], uses(n, u) + (u % B > 0))
                    for k in range(KT):
                        last = pe.transpose(ps_x[:, k, :], xg[:, u % B, k * P:(k + 1) * P], ident[:])
                    last.then_inc(x_turned[u % B], 1)

                def gate_up(n, u):
                    pe.wait_ge(xT_ready[u % B], uses(n, u) + 1)
                    pe.wait_ge(gu_loaded[u % B], 32 * uses(n, u) + 32)
                    pe.wait_ge(hid_ready[(u + 2) % B], uses(n, u) + (u % B >= 2))
                    for k in range(KT):
                        last = pe.matmul(ps_h[:, u % 2, :], xgT[:, u % B, k, :], w_gu[:, u % B, k, :],
                                         start=(k == 0), stop=(k == KT - 1))
                    last.then_inc(h_ready[u % B], 1)

                def turn_h(n, u):
                    pe.wait_ge(hid_ready[u % B], uses(n, u) + 1)
                    pe.wait_ge(hT_ready[(u + 2) % B], uses(n, u) + (u % B >= 2))
                    for k in range(DE // P):
                        last = pe.transpose(ps_t[:, u % 2, k * P:(k + 1) * P], hid[:, u % B, k * P:(k + 1) * P], ident[:])
                    last.then_inc(h_turned[u % B], 1)

                def down(n, u):
                    pe.wait_ge(hT_ready[u % B], uses(n, u) + 1)
                    pe.wait_ge(down_loaded[u % B], 16 * uses(n, u) + 16)
                    pe.wait_ge(y_out[(u - 1) % B], uses(n, u) + (u % B > 0))
                    for half in range(D // COLS):
                        for k in range(DE // P):
                            last = pe.matmul(ps_y[:, half * COLS:(half + 1) * COLS], hidT[:, u % B, k, :],
                                             w_d[:, u % B, k, half * COLS:(half + 1) * COLS],
                                             start=(k == 0), stop=(k == DE // P - 1))
                    last.then_inc(y_done[u % B], 1)

                def body(n):
                    turn_x(n, 0)
                    for u in range(U):
                        gate_up(n, u)
                        if u + 1 < U:
                            turn_x(n, u + 1)
                        if u:
                            turn_h(n, u - 1)
                            down(n, u - 1)
                    turn_h(n, U - 1)
                    down(n, U - 1)
                waves(pe, lambda w: steps(pe, w, body))

            @block.scalar
            def _(act):
                def x_out(n, u):
                    act.wait_ge(x_turned[u % B], uses(n, u) + 1)
                    act.wait_ge(h_ready[u % B], uses(n, u))
                    act.activation(xgT[:, u % B, :, :], ps_x[:], ACT.Copy).then_inc(xT_ready[u % B], 1)

                def gate(n, u):
                    act.wait_ge(h_ready[u % B], uses(n, u) + 1)
                    act.wait_ge(hid_ready[u % B], uses(n, u))
                    act.activation(silu[:, u % B, :], ps_h[:, u % 2, 0:DE], ACT.Silu).then_inc(silu_ready[u % B], 1)

                def body(n):
                    x_out(n, 0)
                    for u in range(U):
                        gate(n, u)
                        if u + 1 < U:
                            x_out(n, u + 1)
                waves(act, lambda w: steps(act, w, body))

            @block.vector
            def _(dve):
                dve.memset(xg[:], 0.0).then_inc(cleared, 1)

                def product(n, u):
                    dve.wait_ge(silu_ready[u % B], uses(n, u) + 1)
                    dve.wait_ge(h_turned[u % B], uses(n, u))
                    dve.tensor_tensor(hid[:, u % B, :], silu[:, u % B, :], ps_h[:, u % 2, DE:2 * DE], ALU.mult
                                      ).then_inc(hid_ready[u % B], 1)

                def h_out(n, u):
                    dve.wait_ge(h_turned[u % B], uses(n, u) + 1)
                    dve.wait_ge(y_done[u % B], uses(n, u))
                    dve.tensor_copy(hidT[:, u % B, :, :], ps_t[:, u % 2, :]).then_inc(hT_ready[u % B], 1)

                def rows_out(n, u):
                    dve.wait_ge(y_done[u % B], uses(n, u) + 1)
                    dve.wait_ge(scattered[(u + B) % U], 16 * (n + (u >= B)))
                    dve.tensor_copy(y[:, u % B, :], ps_y[:]).then_inc(y_out[u % B], 1)

                def body(n):
                    product(n, 0)
                    for u in range(1, U):
                        h_out(n, u - 1)
                        product(n, u)
                        rows_out(n, u - 1)
                    h_out(n, U - 1)
                    rows_out(n, U - 1)
                waves(dve, lambda w: steps(dve, w, body))


def constants(nc, cst, block):
    @block.gpsimd
    def _(pool):
        pool.memset(cst.ident[:], 0.0)
        pool.memset(cst.ones[:], 1.0)
        pool.iota(cst.iota_i[:], pattern=[[1, 64]], base=0, channel_multiplier=0)
        pool.drain()
        pool.affine_select(out=cst.ident[:], in_=cst.ident[:], compare_op=ALU.not_equal, fill=1.0, base=0,
                           pattern=[[-1, P]], channel_multiplier=1)
        pool.affine_select(out=cst.before[:], in_=cst.ones[:], compare_op=ALU.is_gt, fill=0.0, base=0,
                           pattern=[[1, P]], channel_multiplier=-1)
        pool.tensor_copy(cst.iota[:], cst.iota_i[:])
        pool.drain()


def gated_conv(nc, name, xT_hi, xT_lo, w, conv_w, conv_b, zT_hi, zT_lo):
    PARTS = (1, 2, 0)
    with Pool_(nc, name) as m:
        raw = m.sb("raw", [P, 3, KT, P])
        w_hi = m.sb("w_hi", [P, 3, KT, P], F32R)
        w_lo = m.sb("w_lo", [P, 3, KT, P], F32R)
        taps = m.sb("taps", [P, KT, 3])
        bias = m.sb("bias", [P, KT])
        c_sb = m.sb("c_sb", [P, S])
        u_sb = m.sb("u_sb", [P, S + 2])
        y_sb = m.sb("y_sb", [P, S])
        z_sb = m.sb("z_sb", [P, S])
        ps = m.ps("ps", [P, 3, S])
        raw_loaded, hi_ready, lo_ready = m.sems("raw_loaded", 3), m.sems("hi_ready", 3), m.sems("lo_ready", 3)
        product, taps_loaded = m.sems("product", 3), m.sem("taps_loaded")
        apart = m.sem("apart")
        c_out, u_ready, z_ready, z_hi, z_lo = (m.sem(n) for n in ("c_out", "u_ready", "z_ready", "z_hi", "z_lo"))
        w_k = w.rearrange("(k p) n -> p k n", p=P)

        with nc.Block() as block:
            @block.sync
            def _(sp):
                for j in range(3):
                    sp.dma_start(taps[:, :, j], conv_w[j, :].rearrange("(c p) -> p c", p=P),
                                 allow_slow_non_contiguous=True).then_inc(taps_loaded, 16)
                sp.dma_start(bias[:], conv_b.rearrange("(c p) -> p c", p=P),
                                 allow_slow_non_contiguous=True).then_inc(taps_loaded, 16)
                with sp.Fori(0, KT) as i:
                    for j in range(3):
                        col = sp.snap(i * P + PARTS[j] * D)
                        sp.wait_ge(lo_ready[j], i)
                        sp.sem_inc(apart, 1)
                        sp.dma_start(raw[:, j, :, :], w_k[:, :, ds(col, P)]).then_inc(raw_loaded[j], 16)

            @block.scalar
            def _(act):
                def high(i, j):
                    act.wait_ge(raw_loaded[j], 16 * i + 16)
                    act.wait_ge(product[j], i)
                    act.activation(w_hi[:, j, :, :], raw[:, j, :, :], ACT.Copy).then_inc(hi_ready[j], 1)

                def body(i, more):
                    for j in (1, 2):
                        high(i, j)
                    act.wait_ge(product[0], i + 1)
                    act.wait_ge(u_ready, i)
                    act.activation(c_sb[:], ps[:, 0, :], ACT.Copy).then_inc(c_out, 1)
                    if more:
                        high(i + 1, 0)
                    act.wait_ge(z_ready, i + 1)
                    act.activation(zT_hi[:, ds(i, 1), :], z_sb[:].unsqueeze(1), ACT.Copy).then_inc(z_hi, 1)

                high(0, 0)
                with act.Fori(0, KT - 1) as i:
                    body(i, True)
                body(KT - 1, False)

            @block.vector
            def _(dve):
                def low(i, j):
                    dve.wait_ge(hi_ready[j], i + 1)
                    dve.tensor_tensor(w_lo[:, j, :, :], raw[:, j, :, :], w_hi[:, j, :, :].bitcast(F32),
                                      ALU.subtract).then_inc(lo_ready[j], 1)

                def body(i, more):
                    for j in (1, 2):
                        low(i, j)
                    dve.wait_ge(c_out, i + 1)
                    dve.wait_ge(product[1], i + 1)
                    dve.tensor_tensor(u_sb[:, 2:S + 2], c_sb[:], ps[:, 1, :], ALU.mult).then_inc(u_ready, 1)
                    dve.drain()
                    dve.tensor_scalar(y_sb[:], u_sb[:, 2:S + 2], taps[:, ds(i, 1), 2], bias[:, ds(i, 1)], ALU.mult, ALU.add)
                    dve.drain()
                    for j in (1, 0):
                        dve.scalar_tensor_tensor(y_sb[:], u_sb[:, j:S + j], taps[:, ds(i, 1), j], y_sb[:], ALU.mult, ALU.add)
                        dve.drain()
                    if more:
                        low(i + 1, 0)
                    dve.wait_ge(product[2], i + 1)
                    dve.wait_ge(z_hi, i)
                    dve.tensor_tensor(z_sb[:], y_sb[:], ps[:, 2, :], ALU.mult).then_inc(z_ready, 1)
                    dve.wait_ge(z_hi, i + 1)
                    dve.tensor_tensor(zT_lo[:, ds(i, 1), :], z_sb[:].unsqueeze(1), zT_hi[:, ds(i, 1), :].bitcast(F32),
                                      ALU.subtract).then_inc(z_lo, 1)

                dve.memset(u_sb[:, 0:2], 0.0)
                low(0, 0)
                dve.wait_ge(taps_loaded, 64)
                with dve.Fori(0, KT - 1) as i:
                    body(i, True)
                body(KT - 1, False)

            @block.tensor
            def _(pe):
                with pe.Fori(0, KT) as i:
                    for j in range(3):
                        pe.wait_ge(lo_ready[j], i + 1)
                        pe.wait_ge((c_out, u_ready, z_ready)[j], i)
                        for half in range(S // COLS):
                            at = slice(half * COLS, (half + 1) * COLS)
                            for k in range(KT):
                                for q, (w_part, x_part) in enumerate(((w_hi, xT_hi), (w_hi, xT_lo), (w_lo, xT_hi))):
                                    last = pe.matmul(ps[:, j, at], w_part[:, j, k, :], x_part[:, k, at],
                                                     start=(k == 0 and q == 0), stop=(k == KT - 1 and q == 2))
                        last.then_inc(product[j], 1)


def shape_constants():
    f = np.float32
    con = {}
    log_g = np.log(f(1) - f(2) ** (f(-5) - np.arange(RH, dtype=f)))
    pos = np.arange(P, dtype=f)
    diff = pos[:, None] - pos[None, :]
    dec = np.where(diff >= 0, np.exp(log_g[:, None, None] * np.maximum(diff, 0)), 0) * f(HD ** -0.5)
    by = [[2 * b + a for b in range(RH // 2)] for a in range(2)]
    con["decay"] = dec.transpose(0, 2, 1)[by].transpose(2, 0, 1, 3).reshape(P, -1)
    q_dec = np.exp(log_g[:, None] * (pos + 1))
    con["q_decay"] = np.repeat(q_dec[by], HD, axis=0).reshape(P, -1)
    con["k_decay"] = (np.exp(log_g[:, None] * (P - 1 - pos)) * f(HD ** -0.5)).T
    con["c_decay"] = np.repeat(np.exp(log_g * P)[by], HD, axis=0)
    return {k: np.ascontiguousarray(v, dtype=f) for k, v in con.items()}

QR = HD + NS + 1


def retention_and_rows(nc, name, proj, ret_gain, q_gain, k_gains, cst, con, keep, y_out):
    PAIRS = RH // 2
    NK = 2 * G
    ROUND = 4
    ROUNDS = (NH + NK) // ROUND
    C_GATE = 3 * RET_W
    with Pool_(nc, name) as m:
        decay = m.sb("decay", [P, 2, PAIRS, P])
        q_decay = m.sb("q_decay", [P, PAIRS, P])
        k_decay = m.sb("k_decay", [P, RH])
        c_decay = m.sb("c_decay", [P, PAIRS])
        ret_gains = m.sb("ret_gains", [P, HD])
        gains = m.sb("gains", [P, 3, HD])
        qkv = m.sb("qkv", [P, 2, 3 * RET_W])
        nq = m.sb("nq", [P, 2, NSA_W])
        kv = m.sb("kv", [P, NT, 2 * KV_W])
        gate = m.sb("gate", [P, NT, RET_W])
        qkT = m.sb("qkT", [P, 2, 2, PAIRS, P])
        qdT = m.sb("qdT", [P, PAIRS, P])
        kd = m.sb("kd", [P, RET_W])
        scores = m.sb("scores", [P, 2, PAIRS, P])
        state = m.sb("state", [P, PAIRS, HD])
        y = m.sb("y", [P, 2, RET_W])
        y_sq = m.sb("y_sq", [P, RET_W])
        y_ssq, y_root, y_r = (m.sb(n, [P, RH]) for n in ("y_ssq", "y_root", "y_r"))
        n_sq = m.sb("n_sq", [P, NSA_W + 2 * KV_W])
        n_ssq, n_root, n_r = (m.sb(n, [P, NH + NK]) for n in ("n_ssq", "n_root", "n_r"))
        qa = m.sb("qa", [P, 2, NH, QR])
        ka = m.sb("ka", [P, 2, NK, HD])
        q_rows = m.sb("q_rows", [P, NT, NH, NS + 1])
        kvc = m.sb("kvc", [P, 2, NT, KV_W])
        masks_f = m.sb("masks_f", [P, 2 * P + NT * NC_])
        picks_f = m.sb("picks_f", [G * NS, G * S])
        eps = m.sb("eps", [P, 1])
        ps_t = m.ps("ps_t", [P, 2, PAIRS, P])
        ps_s = m.ps("ps_s", [P, 2, PAIRS, P])
        ps_y = m.ps("ps_y", [P, 2, COLS])
        ps_kv = m.ps("ps_kv", [P, 2 * PAIRS, HD])
        ps_n = m.ps("ps_n", [P, ROUND, P])
        const_loaded, rows_loaded, gate_loaded = m.sem("const_loaded"), m.sems("rows_loaded"), m.sem("gate_loaded")
        keys_loaded, pool_loaded, rest_loaded = m.sem("keys_loaded"), m.sem("pool_loaded"), m.sem("rest_loaded")
        turned, T_ready, qd_ready, kd_ready = (m.sem(n) for n in ("turned", "T_ready", "qd_ready", "kd_ready"))
        scored, decayed, y_taken = (m.sem(n) for n in ("scored", "decayed", "y_taken"))
        y_ready = m.sems("y_ready")
        kv_ready, state_ready, eps_ready = m.sem("kv_ready"), m.sem("state_ready"), m.sem("eps_ready")
        y_summed, y_rooted, silus, gated = (m.sem(n) for n in ("y_summed", "y_rooted", "silus", "gated"))
        y_done, stored = m.sem("y_done"), m.sems("stored")
        n_squared, n_summed, n_rooted, rows_added, n_ready = (
            m.sem(n) for n in ("n_squared", "n_summed", "n_rooted", "rows_added", "n_ready"))
        n_turned, n_taken = m.sem("n_turned"), m.sem("n_taken")
        apart = m.sem("apart")
        tiled = proj.rearrange("(t p) n -> p t n", p=P)

        def chunks(eng, body):
            with eng.Fori(0, NT // 2 - 1) as i:
                for u in range(2):
                    body(i, u, True)
            for u in range(2):
                body(NT // 2 - 1, u, u == 0)

        with nc.Block() as block:
            @block.sync
            def _(sp):
                for c in range(2):
                    sp.dma_start(qkv[:, c, :], proj[c * P:(c + 1) * P, 0:C_GATE]).then_inc(rows_loaded[c], 16)
                    sp.dma_start(nq[:, c, :], proj[c * P:(c + 1) * P, C_NQ:C_KC]).then_inc(rows_loaded[c], 16)
                    if c == 0:
                        for j, (a, b) in enumerate(((C_KS, C_VS), (C_KW, C_VW))):
                            sp.dma_start(kv[:, :, j * KV_W:(j + 1) * KV_W], tiled[:, :, a:b]).then_inc(keys_loaded, 16)
                        sp.dma_start(gains[:, 0, :], row_of(q_gain)).then_inc(keys_loaded, 16)
                        sp.dma_start(gains[:, 1:3, :], row_of(k_gains[1:3, :])).then_inc(keys_loaded, 16)
                        sp.dma_start(q_rows[:], con["q_rows"].rearrange("p (t h j) -> p t h j", t=NT, h=NH)
                                     ).then_inc(keys_loaded, 16)
                for j, (a, b) in enumerate(((C_KC, C_VC), (C_VC, C_KS))):
                    sp.dma_start(kvc[:, j, :, :], tiled[:, :, a:b]).then_inc(pool_loaded, 16)
                sp.dma_start(masks_f[:], con["masks"]).then_inc(pool_loaded, 16)
                sp.dma_start(picks_f[:], con["picks"]).then_inc(pool_loaded, 16)
                for j, (a, b) in enumerate(((C_VS, C_KW), (C_VW, C_NG))):
                    sp.dma_start(keep.v[:, :, j, :], tiled[:, :, a:b]).then_inc(rest_loaded, 16)
                sp.dma_start(keep.gate[:], tiled[:, :, C_NG:IN_W]).then_inc(rest_loaded, 16)
                for g in range(G):
                    for b in range(2):
                        sp.dma_start(keep.kT[HD:QR, b, g, :], con["key_rows"]).then_inc(rest_loaded, 16)
                    sp.dma_start(keep.kcT[HD:QR, g, :], con["cmp_rows"]).then_inc(rest_loaded, 16)
                sp.dma_start(keep.forced[:], con["forced"].rearrange("p (t j) -> p t j", t=NT)).then_inc(rest_loaded, 16)

                def store(c, row, u):
                    sp.wait_ge(y_done, c + 1)
                    sp.dma_start(y_out[ds(row, P), 0:RET_W], y[:, u, :]).then_inc(stored[u], 16)

                with sp.Fori(0, NT // 2 - 1) as i:
                    for u in range(2):
                        here, ahead = sp.snap((2 * i + u) * P), sp.snap((2 * i + u + 2) * P)
                        sp.wait_ge(y_ready[u], i + 1)
                        sp.dma_start(qkv[:, u, :], proj[ds(ahead, P), 0:C_GATE]).then_inc(rows_loaded[u], 16)
                        sp.dma_start(nq[:, u, :], proj[ds(ahead, P), C_NQ:C_KC]).then_inc(rows_loaded[u], 16)
                        store(2 * i + u, here, u)
                for c in (NT - 2, NT - 1):
                    store(c, c * P, c % 2)
                for u in range(2):
                    sp.wait_ge(stored[u], 16 * (NT // 2))
                sp.wait_ge(rest_loaded, 16 * 10)

            @block.gpsimd
            def _(pool):
                pool.tensor_copy(keep.ident_b[:], cst.ident[:])
                pool.wait_ge(silus, 1)
                heads = gate[:].rearrange("p t (h d) -> p (t h) d", d=HD)
                pool.tensor_tensor(heads, heads, ret_gains[:].unsqueeze(1).to_broadcast([P, NT * RH, HD]), ALU.mult
                                   ).then_inc(gated, 1)
                pool.wait_ge(pool_loaded, 64)
                pool.tensor_copy(keep.masks[:], masks_f[:])
                pool.tensor_copy(keep.picks[:], picks_f[:])
                for j in range(2):
                    for a in range(2):
                        pool.tensor_copy(keep.kvc2[:, j, :, :, a, :], kvc[:, j, :, :].rearrange("p t (g d) -> p t g d", d=HD))
                pool.drain()

            @block.scalar
            def _(act):
                for dst, src in ((decay[:], con["decay"].rearrange("p (a b c) -> p a b c", a=2, b=PAIRS)),
                                 (q_decay[:], con["q_decay"].rearrange("p (a b) -> p a b", a=PAIRS)),
                                 (k_decay[:], con["k_decay"]), (c_decay[:], con["c_decay"]),
                                 (ret_gains[:], row_of(ret_gain))):
                    act.dma_start(dst, src).then_inc(const_loaded, 16)
                act.dma_start(gate[:], tiled[:, :, C_GATE:C_NQ]).then_inc(gate_loaded, 16)
                act.wait_ge(eps_ready, 1)
                act.wait_ge(keys_loaded, 16 * 5)

                def ahead(c, i, v):
                    act.wait_ge(rows_loaded[v], 32 * i + 32)
                    act.activation(n_sq[:, 0:NSA_W], nq[:, v, :], ACT.Square)
                    act.activation(n_sq[:, NSA_W:NSA_W + 2 * KV_W].unsqueeze(1), kv[:, ds(c, 1), :], ACT.Square
                                   ).then_inc(n_squared, 1)
                    act.wait_ge(turned, c + 1)
                    act.wait_ge(y_ready[v], i)
                    act.activation(qkT[:, v, :, :, :], ps_t[:], ACT.Copy).then_inc(T_ready, 1)
                    act.activation(qa[:, v, :, HD:QR].unsqueeze(1), q_rows[:, ds(c, 1), :, :], ACT.Copy
                                   ).then_inc(rows_added, 1)
                    act.wait_ge(n_summed, c + 1)
                    act.activation(n_root[:], n_ssq[:], ACT.Sqrt, bias=eps[:], scale=1.0 / HD).then_inc(n_rooted, 1)

                def take_queries(c):
                    act.wait_ge(n_turned, ROUNDS * c + 2)
                    act.activation(keep.qT[0:QR, ds(c * NH + ROUND, ROUND), :], ps_n[0:QR, :, :], ACT.Copy
                                   ).then_inc(n_taken, 1)

                def take_keys(c):
                    act.wait_ge(n_turned, ROUNDS * c + 3)
                    act.activation(keep.kT[0:HD, :, :, ds(c * P, P)],
                                   ps_n[0:HD, :, :].rearrange("p (b g) n -> p b g n", b=2), ACT.Copy).then_inc(n_taken, 1)

                def body(i, u, more):
                    c = 2 * i + u
                    if more:
                        ahead(c + 1, i + u, 1 - u)
                    take_queries(c)
                    act.wait_ge(y_ready[u], i + 1)
                    act.wait_ge(stored[u], 16 * i)
                    halves = ps_y[:, :, 0:PAIRS * HD].rearrange("p a (b d) -> p a b d", d=HD)
                    act.activation(y_sq[:].rearrange("p (b a d) -> p a b d", a=2, d=HD), halves, ACT.Square)
                    act.activation(y[:, u, :].rearrange("p (b a d) -> p a b d", a=2, d=HD), halves, ACT.Copy
                                   ).then_inc(y_taken, 1)
                    take_keys(c)
                    act.wait_ge(y_summed, c + 1)
                    act.activation(y_root[:], y_ssq[:], ACT.Sqrt, bias=eps[:], scale=1.0 / HD).then_inc(y_rooted, 1)

                ahead(0, 0, 0)
                act.wait_ge(gate_loaded, 16)
                act.wait_ge(const_loaded, 16 * 5)
                act.activation(gate[:], gate[:], ACT.Silu).then_inc(silus, 1)
                chunks(act, body)

            @block.vector
            def _(dve):
                dve.memset(eps[:], EPS).then_inc(eps_ready, 1)
                dve.memset(state[:], 0.0).then_inc(state_ready, 1)
                dve.wait_ge(keys_loaded, 16 * 5)

                def sums(c):
                    dve.wait_ge(n_squared, c + 1)
                    dve.tensor_reduce(n_ssq[:], n_sq[:].rearrange("p (h d) -> p h d", d=HD), X, ALU.add).then_inc(n_summed, 1)

                def apply(c, v):
                    dve.wait_ge(n_rooted, c + 1)
                    dve.reciprocal(n_r[:], n_root[:])
                    dve.drain()
                    dve.tensor_scalar(n_r[:, 0:NH], n_r[:, 0:NH], HD ** -0.5, None, ALU.mult)
                    dve.drain()
                    q = qa[:, v, :, 0:HD]
                    dve.wait_ge(rows_added, c + 1)
                    dve.tensor_tensor(q, nq[:, v, :].rearrange("p (h d) -> p h d", d=HD),
                                      n_r[:, 0:NH].unsqueeze(2).to_broadcast([P, NH, HD]), ALU.mult)
                    dve.tensor_tensor(ka[:, v, :, :].unsqueeze(1),
                                      kv[:, ds(c, 1), :].rearrange("p t (h d) -> p t h d", d=HD),
                                      n_r[:, NH:NH + NK].unsqueeze(1).unsqueeze(3).to_broadcast([P, 1, NK, HD]), ALU.mult)
                    dve.drain()
                    dve.tensor_tensor(q, q, gains[:, 0, :].unsqueeze(1).to_broadcast([P, NH, HD]), ALU.mult)
                    k4 = ka[:, v, :, :].rearrange("p (b g) d -> p b g d", b=2)
                    dve.tensor_tensor(k4, k4, gains[:, 1:3, :].unsqueeze(2).to_broadcast([P, 2, G, HD]), ALU.mult
                                      ).then_inc(n_ready, 1)

                def body(i, u, more):
                    c = 2 * i + u
                    dve.wait_ge(rows_loaded[u], 32 * i + 32)
                    dve.wait_ge(kv_ready, c)
                    dve.tensor_tensor(kd[:].rearrange("p (h d) -> p h d", d=HD),
                                      qkv[:, u, RET_W:2 * RET_W].rearrange("p (h d) -> p h d", d=HD),
                                      k_decay[:].unsqueeze(2).to_broadcast([P, RH, HD]), ALU.mult).then_inc(kd_ready, 1)
                    dve.wait_ge(T_ready, c + 1)
                    dve.wait_ge(y_ready[1 - u], i + u)
                    dve.tensor_tensor(qdT[:], qkT[:, u, 0, :, :], q_decay[:], ALU.mult).then_inc(qd_ready, 1)
                    dve.wait_ge(scored, c + 1)
                    dve.tensor_tensor(scores[:], ps_s[:], decay[:], ALU.mult).then_inc(decayed, 1)
                    if more:
                        sums(c + 1)
                    dve.wait_ge(n_turned, ROUNDS * c + 1)
                    dve.tensor_copy(keep.qT[0:QR, ds(c * NH, ROUND), :], ps_n[0:QR, :, :]).then_inc(n_taken, 1)
                    if more:
                        apply(c + 1, 1 - u)
                    dve.wait_ge(kv_ready, c + 1)
                    dve.wait_ge(y_ready[u], i + 1)
                    dve.tensor_tensor(state[:], state[:], c_decay[:].unsqueeze(2).to_broadcast([P, PAIRS, HD]), ALU.mult)
                    dve.drain()
                    dve.tensor_tensor(state[:], state[:], ps_kv[:, 0:PAIRS, :], ALU.add).then_inc(state_ready, 1)
                    dve.wait_ge(y_taken, c + 1)
                    dve.tensor_reduce(y_ssq[:], y_sq[:].rearrange("p (h d) -> p h d", d=HD), X, ALU.add
                                      ).then_inc(y_summed, 1)
                    dve.wait_ge(y_rooted, c + 1)
                    dve.reciprocal(y_r[:], y_root[:])
                    dve.drain()
                    y_h = y[:, u, :].rearrange("p (h d) -> p h d", d=HD)
                    dve.tensor_tensor(y_h, y_h, y_r[:].unsqueeze(2).to_broadcast([P, RH, HD]), ALU.mult)
                    dve.drain()
                    dve.wait_ge(gated, 1)
                    dve.tensor_tensor(y[:, u, :].unsqueeze(1), y[:, u, :].unsqueeze(1), gate[:, ds(c, 1), :], ALU.mult
                                      ).then_inc(y_done, 1)

                sums(0)
                apply(0, 0)
                dve.wait_ge(const_loaded, 16 * 5)
                chunks(dve, body)

            @block.tensor
            def _(pe):
                def turn(c, i, v):
                    pe.wait_ge(rows_loaded[v], 32 * i + 32)
                    pe.wait_ge(T_ready, c)
                    for a in range(2):
                        for b in range(PAIRS):
                            last = pe.transpose(ps_t[:, a, b, :], qkv[:, v, a * RET_W + b * P:a * RET_W + (b + 1) * P],
                                                cst.ident[:])
                    last.then_inc(turned, 1)

                def rows(c, u, r):
                    pe.wait_ge(n_taken, ROUNDS * c + r)
                    if r == 0:
                        pe.wait_ge(n_ready, c + 1)
                    if r == ROUNDS - 1:
                        pe.sem_inc(apart, 1)
                    for j in range(ROUND):
                        h = r * ROUND + j
                        if h < NH:
                            last = pe.transpose(ps_n[0:QR, j, :], qa[:, u, h, :], cst.ident[:])
                        else:
                            last = pe.transpose(ps_n[0:HD, j, :], ka[:, u, h - NH, :], cst.ident[:])
                    last.then_inc(n_turned, 1)

                def body(i, u, more):
                    c = 2 * i + u
                    pe.wait_ge(T_ready, c + 1)
                    pe.wait_ge(decayed, c)
                    for a in range(2):
                        at = slice(a * HD, (a + 1) * HD)
                        for b in range(PAIRS):
                            last = pe.matmul(ps_s[:, a, b, :], qkT[at, u, 1, b, :], qkT[at, u, 0, b, :], start=True, stop=True)
                    last.then_inc(scored, 1)
                    if more:
                        turn(c + 1, i + u, 1 - u)
                    rows(c, u, 0)
                    pe.wait_ge(kd_ready, c + 1)
                    pe.wait_ge(state_ready, c + 1)
                    for a in range(2):
                        for b in range(PAIRS):
                            h = 2 * b + a
                            last = pe.matmul(ps_kv[a * HD:(a + 1) * HD, b, :], kd[:, h * HD:(h + 1) * HD],
                                             qkv[:, u, 2 * RET_W + h * HD:2 * RET_W + (h + 1) * HD], start=True, stop=True)
                    last.then_inc(kv_ready, 1)
                    rows(c, u, 1)
                    pe.wait_ge(qd_ready, c + 1)
                    pe.wait_ge(y_taken, c)
                    pe.wait_ge(decayed, c + 1)
                    for a in range(2):
                        at = slice(a * HD, (a + 1) * HD)
                        for b in range(PAIRS):
                            h = 2 * b + a
                            pe.matmul(ps_y[:, a, b * HD:(b + 1) * HD], scores[:, a, b, :],
                                      qkv[:, u, 2 * RET_W + h * HD:2 * RET_W + (h + 1) * HD], start=True, stop=False)
                            last = pe.matmul(ps_y[:, a, b * HD:(b + 1) * HD], qdT[at, b, :], state[at, b, :],
                                             start=False, stop=True)
                    last.then_inc(y_ready[u], 1)
                    rows(c, u, 2)

                turn(0, 0, 0)
                chunks(pe, body)


def sparse_prepare(nc, name, k_gains, pe, w1, w2, cst, keep):
    with Pool_(nc, name) as m:
        eps = m.sb("eps", [P, 1])
        with Pool_(nc, name + "C") as s:
            L = CMP_STRIDE
            xb = s.sb("xb", [P, L, G, NC_])[:]
            gains = s.sb("gains", [P, HD])
            peT = s.sb("peT", [P, 2, L])
            w1s = s.sb("w1s", [P, 2, L, CMP_HID])
            w2s = s.sb("w2s", [P, 2, HD])
            hid = s.sb("hid", [P, G, 2, NC_])
            kc = s.sb("kc", [NC_, G, HD])
            ksq = s.sb("ksq", [NC_, G, HD])
            kss = s.sb("kss", [NC_, G])
            ps_x = s.ps("ps_x", [P, G, S])
            ps_h = s.ps("ps_h", [P, G, NC_])
            ps_k = s.ps("ps_k", [P, G, HD])
            ps_t = s.ps("ps_t", [HD, G, NC_])
            w_loaded, x_turned, xb_ready, h_done, hid_ready = (
                s.sem(n) for n in ("w_loaded", "x_turned", "xb_ready", "h_done", "hid_ready"))
            k_done, k_sq, k_sum, k_root, k_ready, k_turned, v_done, v_taken = (
                s.sem(n) for n in ("k_done", "k_sq", "k_sum", "k_root", "k_ready", "k_turned", "v_done", "v_taken"))

            with nc.Block() as block:
                @block.sync
                def _(sp):
                    for j in range(2):
                        for a in range(2):
                            rows = slice(a * HD, (a + 1) * HD)
                            sp.dma_start(peT[rows, j, :], pe[j, a * L:(a + 1) * L, :].rearrange("l d -> d l"),
                                         allow_slow_non_contiguous=True).then_inc(w_loaded, 16)
                            sp.dma_start(w1s[rows, j, :, :],
                                         w1[j, a * L * HD:(a + 1) * L * HD, :].rearrange("(l d) n -> d l n", d=HD)
                                         ).then_inc(w_loaded, 16)
                    sp.dma_start(w2s[:], w2.rearrange("j p d -> p j d")).then_inc(w_loaded, 16)
                    sp.dma_start(gains[:], row_of(k_gains[0, :])).then_inc(w_loaded, 16)

                @block.tensor
                def _(pe_):
                    for j in range(2):
                        if j:
                            pe_.wait_ge(xb_ready, 1)
                        for g in range(G):
                            for t in range(NT):
                                last = pe_.transpose(ps_x[:, g, t * P:(t + 1) * P],
                                                     keep.kvc2[:, j, t, g, :, :].rearrange("p a d -> p (a d)"), cst.ident[:])
                        last.then_inc(x_turned, 1)
                        pe_.wait_ge(xb_ready, j + 1)
                        pe_.wait_ge(w_loaded, 16 * 10)
                        for l in range(L):
                            last = pe_.matmul(ps_h[:], w1s[:, j, l, :], xb[:, l, :, :], start=(l == 0), stop=(l == L - 1))
                        last.then_inc(h_done, 1)
                        pe_.wait_ge(hid_ready, j + 1)
                        if j == 0:
                            for g in range(G):
                                last = pe_.matmul(ps_k[0:NC_, g, :], hid[:, g, 0, :], w2s[:, 0, :], start=True, stop=True)
                            last.then_inc(k_done, 1)
                            pe_.wait_ge(k_ready, 1)
                            for g in range(G):
                                last = pe_.transpose(ps_t[:, g, :], kc[:, g, :], cst.ident[0:NC_, 0:NC_])
                            last.then_inc(k_turned, 1)
                        else:
                            for g in range(G):
                                last = pe_.matmul(ps_k[:, g, :], hid[:, g, :, :].rearrange("p a n -> p (a n)"), w2s[:, 1, :], start=True, stop=True)
                            last.then_inc(v_done, 1)

                @block.scalar
                def _(act):
                    for j in range(2):
                        act.wait_ge(h_done, j + 1)
                        act.activation(hid[:], ps_h[:].unsqueeze(2).to_broadcast([P, G, 2, NC_]), ACT.Gelu_apprx_tanh).then_inc(hid_ready, 1)
                        if j == 0:
                            act.wait_ge(k_done, 1)
                            act.activation(ksq[:], ps_k[0:NC_, :, :], ACT.Square).then_inc(k_sq, 1)
                            act.wait_ge(k_sum, 1)
                            act.activation(kss[:], kss[:], ACT.Sqrt, bias=eps[0:NC_, :], scale=1.0 / HD).then_inc(k_root, 1)

                @block.vector
                def _(dve):
                    dve.memset(eps[:], EPS)
                    dve.memset(xb, 0.0)
                    dve.memset(keep.v_cmp[:], 0.0)
                    dve.drain()
                    dve.wait_ge(w_loaded, 16 * 10)
                    for j in range(2):
                        dve.wait_ge(x_turned, j + 1)
                        if j:
                            dve.wait_ge(h_done, 1)
                        for a in range(2):
                            rows, n = slice(a * HD, (a + 1) * HD), NC_ - a
                            for g in range(G):
                                last = dve.tensor_tensor(
                                    xb[rows, :, g, 0:n],
                                    ps_x[rows, g, a * L:S].rearrange("p (n l) -> p l n", l=L),
                                    peT[rows, j, :].unsqueeze(2).to_broadcast([HD, L, n]), ALU.add)
                        last.then_inc(xb_ready, 1)
                        if j == 0:
                            dve.wait_ge(k_sq, 1)
                            dve.tensor_reduce(kss[:], ksq[:], X, ALU.add).then_inc(k_sum, 1)
                            dve.wait_ge(k_root, 1)
                            dve.reciprocal(kss[:], kss[:])
                            dve.drain()
                            dve.tensor_tensor(kc[:], ps_k[0:NC_, :, :], kss[:].unsqueeze(2).to_broadcast([NC_, G, HD]), ALU.mult)
                            dve.drain()
                            dve.tensor_tensor(kc[:], kc[:], gains[0:NC_, :].unsqueeze(1).to_broadcast([NC_, G, HD]), ALU.mult
                                              ).then_inc(k_ready, 1)
                            dve.wait_ge(k_turned, 1)
                            dve.tensor_copy(keep.kcT[0:HD, :, :], ps_t[:]).then_inc(v_taken, 1)
                        else:
                            dve.wait_ge(v_done, 1)
                            for a in range(2):
                                rows = slice(a * HD, (a + 1) * HD)
                                dve.tensor_copy(keep.v_cmp[rows, :, a * HD:(a + 1) * HD], ps_k[rows, :, :])
                            dve.drain()

    with Pool_(nc, name + "S") as s:
        BATCH = NT // 2
        pc = s.sb("pc", [P, NT, NH, NC_])
        mx = s.sb("mx", [P, NT * NH])
        hs = s.sb("hs", [P, NT, G, NC_])
        imp = s.sb("imp", [P, NT, G, NS])
        best = s.sb("best", [P, NT * G, 8])
        left = s.sb("left", [P, NT * G, NS])
        bias_q = s.sb("bias_q", [P, NT, G * NS], BF16)
        scored, shifted, exped, prob_ready, picked = (
            s.sem(n) for n in ("scored", "shifted", "exped", "prob_ready", "picked"))
        with Pool_(nc, name + "S1") as b1:
            ps = b1.ps("ps", [P, NT, NH, NC_])
            with nc.Block() as block:
                @block.tensor
                def _(pe_):
                    for t in range(NT):
                        c_mask = keep.masks[:, 2 * P + t * NC_:2 * P + (t + 1) * NC_]
                        for h in range(NH):
                            pe_.matmul(ps[:, t, h, :], keep.ident_b[:], c_mask, start=True, stop=False)
                            last = pe_.matmul(ps[:, t, h, :], keep.qT[0:QR, t * NH + h, :], keep.kcT[0:QR, h // R, :],
                                              start=False, stop=True)
                        if t % BATCH == BATCH - 1:
                            last.then_inc(scored, 1)

                @block.scalar
                def _(act):
                    for b in range(2):
                        at = slice(b * BATCH, (b + 1) * BATCH)
                        act.wait_ge(shifted, b + 1)
                        act.activation(pc[:, at, :, :], pc[:, at, :, :], ACT.Exp).then_inc(exped, 1)

                @block.vector
                def _(dve):
                    n = BATCH * NH

                    def shift(b):
                        at = slice(b * BATCH, (b + 1) * BATCH)
                        m_b = mx[:, b * n:(b + 1) * n]
                        src = ps[:, at, :, :].rearrange("p t h n -> p (t h) n")
                        dve.wait_ge(scored, b + 1)
                        dve.tensor_reduce(m_b, src, X, ALU.max)
                        dve.drain()
                        dve.tensor_scalar(m_b, m_b, -1e20, None, ALU.max)
                        dve.drain()
                        dve.tensor_tensor(pc[:, at, :, :].rearrange("p t h n -> p (t h) n"), src,
                                          m_b.unsqueeze(2).to_broadcast([P, n, NC_]), ALU.subtract).then_inc(shifted, 1)

                    def select(b):
                        at = slice(b * BATCH, (b + 1) * BATCH)
                        m_b = mx[:, b * n:(b + 1) * n]
                        p_b = pc[:, at, :, :].rearrange("p t h n -> p (t h) n")
                        dve.wait_ge(exped, b + 1)
                        dve.tensor_reduce(m_b, p_b, X, ALU.add)
                        dve.drain()
                        dve.tensor_scalar(m_b, m_b, 1e-30, None, ALU.max)
                        dve.drain()
                        dve.reciprocal(m_b, m_b)
                        dve.drain()
                        dve.tensor_tensor(p_b, p_b, m_b.unsqueeze(2).to_broadcast([P, n, NC_]), ALU.mult
                                          ).then_inc(prob_ready, 1)
                        dve.drain()
                        dve.tensor_reduce(hs[:, at, :, :].rearrange("p t g n -> p (t g) n"),
                                          pc[:, at, :, :].rearrange("p t (g r) n -> p (t g) n r", g=G), X, ALU.add)
                        dve.drain()
                        h_b = hs[:, at, :, :].rearrange("p t g n -> p (t g) n")
                        i_b = imp[:, at, :, :].rearrange("p t g j -> p (t g) j")
                        dve.tensor_reduce(i_b, h_b.rearrange("p a (j i) -> p a j i", i=4), X, ALU.add)
                        dve.drain()
                        dve.tensor_tensor(i_b[:, :, 1:NS], i_b[:, :, 1:NS], h_b[:, :, 3:NC_ - 1:4], ALU.add)
                        dve.drain()
                        dve.tensor_tensor(imp[:, at, :, :], imp[:, at, :, :],
                                          keep.forced[:, at, :].unsqueeze(2).to_broadcast([P, BATCH, G, NS]), ALU.add)
                        dve.drain()
                        pairs = range(b * BATCH * G, (b + 1) * BATCH * G)
                        flat = imp[:].rearrange("p t g j -> p (t g) j")
                        for a in pairs:
                            dve.max(best[:, a, :], flat[:, a, :])
                        dve.drain()
                        for a in pairs:
                            dve.match_replace(left[:, a, :], best[:, a, :], flat[:, a, :], -3e38)
                        dve.drain()
                        dve.tensor_scalar(bias_q[:, at, :].rearrange("p t j -> p (t j)"),
                                          left[:, pairs[0]:pairs[-1] + 1, :].rearrange("p a j -> p (a j)"),
                                          -3e38, NEG, ALU.not_equal, ALU.mult).then_inc(picked, 1)

                    shift(0)
                    shift(1)
                    select(0)
                    select(1)
                    dve.drain()

        with Pool_(nc, name + "S2") as b2:
            pT = b2.sb("pT", [P, 2, NH // 2, P])
            ps_sel = b2.ps("ps_sel", [G * NS, NT, P], BF16)
            ps_p = b2.ps("ps_p", [P, 2, NH // 2, P])
            ps_o = b2.ps("ps_o", [P, 2, NSA_W])
            sel_turned, p_turned, pT_ready = b2.sem("sel_turned"), b2.sems("p_turned"), b2.sems("pT_ready")
            o_done, o_taken = b2.sems("o_done"), b2.sems("o_taken")
            g_exp, g_gate = b2.sem("g_exp"), b2.sem("g_gate")
            with nc.Block() as block:
                @block.tensor
                def _(pe_):
                    for t in range(NT):
                        last = pe_.transpose(ps_sel[:, t, :], bias_q[:, t, :], keep.ident_b[:])
                    last.then_inc(sel_turned, 1)

                    def turn(t):
                        u = t % 2
                        if t >= 2:
                            pe_.wait_ge(pT_ready[u], t // 2)
                        for a in range(NH // 2):
                            last = pe_.transpose(ps_p[:, u, a, :], pc[:, t, 2 * a:2 * a + 2, :], cst.ident[:])
                        last.then_inc(p_turned[u], 1)

                    turn(0)
                    for t in range(NT):
                        u = t % 2
                        if t + 1 < NT:
                            turn(t + 1)
                        pe_.wait_ge(pT_ready[u], t // 2 + 1)
                        if t >= 2:
                            pe_.wait_ge(o_taken[u], t // 2)
                        for a in range(NH // 2):
                            last = pe_.matmul(ps_o[:, u, a * P:(a + 1) * P], pT[:, u, a, :], keep.v_cmp[:, 2 * a // R, :],
                                              start=True, stop=True)
                        last.then_inc(o_done[u], 1)

                @block.scalar
                def _(act):
                    act.activation(keep.gate[:], keep.gate[:], ACT.Exp, scale=-1.0).then_inc(g_exp, 1)
                    for t in range(NT):
                        act.wait_ge(p_turned[t % 2], t // 2 + 1)
                        if t >= 2:
                            act.wait_ge(o_done[t % 2], t // 2)
                        act.activation(pT[:, t % 2, :, :], ps_p[:, t % 2, :, :], ACT.Copy).then_inc(pT_ready[t % 2], 1)

                @block.vector
                def _(dve):
                    dve.wait_ge(g_exp, 1)
                    dve.tensor_scalar(keep.gate[:], keep.gate[:], 1.0, None, ALU.add)
                    dve.drain()
                    dve.reciprocal(keep.gate[:], keep.gate[:])
                    dve.wait_ge(sel_turned, 1)
                    dve.tensor_copy(keep.selT[:], ps_sel[:])
                    dve.drain()
                    for t in range(NT):
                        dve.wait_ge(o_done[t % 2], t // 2 + 1)
                        g_cmp = keep.gate[:, t, :].rearrange("p (h b) -> p h b", b=N_BRANCH)[:, :, 0]
                        dve.tensor_tensor(keep.o[:, t, :].rearrange("p (h d) -> p h d", d=HD),
                                          ps_o[:, t % 2, :].rearrange("p (h d) -> p h d", d=HD),
                                          g_cmp.unsqueeze(2).to_broadcast([P, NH, HD]), ALU.mult).then_inc(o_taken[t % 2], 1)
                    dve.drain()


def sparse_attend(nc, name, cst, keep, y_out):
    FAR = WINDOW // P
    SELB, WINB = 0, 1
    units = []
    order = list(range(NT - 1, -1, -1))
    for t in order:
        for h in range(NH):
            units.append((t, h, SELB, 0, t + 1))
            first = max(0, t - FAR)
            units.append((t, h, WINB, first, t + 1 - first))
    PIECE = COLS // P
    pieces = [[(a, min(PIECE, n - a)) for a in range(0, n, PIECE)] for *_, n in units]
    with Pool_(nc, name) as m:
        prob = m.sb("prob", [P, 2, S])
        probT = m.sb("probT", [P, 2, NT, P])
        low = m.sb("low", [P, 4])
        mass = m.sb("mass", [P, 2, 2, NH])
        coef = m.sb("coef", [P, 2])
        ps_s = m.ps("ps_s", [P, 2, S])
        ps_t = m.ps("ps_t", [P, 2, COLS])
        ps_o = m.ps("ps_o", [P, 2, 2, COLS // 2])
        scored, lowest, exped, turned, turned_out, valued = (
            m.sem(n) for n in ("scored", "lowest", "exped", "turned", "turned_out", "valued"))
        head_mixed, stored = m.sem("head_mixed"), m.sem("stored")
        n_pieces = [0]
        for p in pieces:
            n_pieces.append(n_pieces[-1] + len(p))

        with nc.Block() as block:
            @block.tensor
            def _(pe):
                def score(n):
                    t, h, b, first, tiles = units[n]
                    s, g = n % 2, h // R
                    if n >= 2:
                        pe.wait_ge(exped, n - 1)
                    for a, k in pieces[n]:
                        keys = slice((first + a) * P, (first + a + k) * P)
                        out = ps_s[:, s, a * P:(a + k) * P]
                        masks = []
                        if first + a + k == t + 1:
                            masks.append((k - 1, keep.masks[:, 0:P]))
                        if b == WINB and first == t - FAR and a == 0:
                            masks.append((0, keep.masks[:, P:2 * P]))
                        for j, (at, mask) in enumerate(masks):
                            pe.matmul(ps_s[:, s, (a + at) * P:(a + at + 1) * P], keep.ident_b[:], mask,
                                      start=(j == 0), stop=False, skip_group_check=True)
                        if b == SELB:
                            pe.matmul(out, keep.selT[:, t, :], keep.picks[:, g * S + keys.start:g * S + keys.stop],
                                      start=not masks, stop=False, skip_group_check=True)
                        last = pe.matmul(out, keep.qT[0:QR, t * NH + h, :], keep.kT[0:QR, b, g, keys],
                                         start=(b == WINB and not masks), stop=True, skip_group_check=True)
                    last.then_inc(scored, 1)

                def turn(n):
                    pe.wait_ge(exped, n + 1)
                    for j, (a, k) in enumerate(pieces[n]):
                        q = n_pieces[n] + j
                        if q >= 2:
                            pe.wait_ge(turned_out, q - 1)
                        for i in range(k):
                            last = pe.transpose(ps_t[:, q % 2, i * P:(i + 1) * P],
                                                prob[:, n % 2, (a + i) * P:(a + i + 1) * P], cst.ident[:])
                        last.then_inc(turned, 1)

                def value(n):
                    t, h, b, first, tiles = units[n]
                    pe.wait_ge(turned_out, n_pieces[n + 1])
                    if b == 0 and n >= 4:
                        pe.wait_ge(head_mixed, n // 2 - 1)
                    g = h // R
                    for i in range(tiles):
                        last = pe.matmul(ps_o[:, h % 2, b, 0:HD], probT[:, n % 2, i, :],
                                         keep.v[:, first + i, b, g * HD:(g + 1) * HD], start=(i == 0), stop=(i == tiles - 1))
                    last.then_inc(valued, 1)

                warm_up(pe, ps_t[:, 0, :], keep.ident_b[:], keep.masks[:, 0:COLS])
                score(0)
                score(1)
                for n in range(len(units)):
                    if n + 2 < len(units):
                        score(n + 2)
                    if n:
                        value(n - 1)
                    turn(n)
                value(len(units) - 1)

            def take(eng, copy, n, j):
                a, k = pieces[n][j]
                q = n_pieces[n] + j
                eng.wait_ge(turned, q + 1)
                if n >= 2:
                    eng.wait_ge(valued, n - 1)
                eng.wait_ge(turned_out, q)
                copy(probT[:, n % 2, a:a + k, :], ps_t[:, q % 2, 0:k * P]).then_inc(turned_out, 1)

            @block.scalar
            def _(act):
                def exps(n):
                    t, h, b, first, tiles = units[n]
                    act.wait_ge(lowest, n + 1)
                    if n >= 2:
                        act.wait_ge(turned, n_pieces[n - 1])
                    if h == 0 and b == 0 and order.index(t) >= 2:
                        act.wait_ge(head_mixed, NH * (order.index(t) - 1))
                    act.activation(prob[:, n % 2, 0:tiles * P], ps_s[:, n % 2, 0:tiles * P], ACT.Exp,
                                   bias=low[:, n % 4:n % 4 + 1], accum_out=mass[:, t % 2, b, h:h + 1]).then_inc(exped, 1)

                exps(0)
                for n in range(len(units)):
                    if n + 1 < len(units):
                        exps(n + 1)
                    if len(pieces[n]) > 1:
                        take(act, lambda o, i: act.activation(o, i, ACT.Copy), n, 1)

            @block.vector
            def _(dve):
                def maximum(n):
                    tiles = units[n][-1]
                    dve.wait_ge(scored, n + 1)
                    if n >= 4:
                        dve.wait_ge(exped, n - 3)
                    dve.tensor_reduce(low[:, n % 4:n % 4 + 1], ps_s[:, n % 2, 0:tiles * P], X, ALU.max, negate=True
                                      ).then_inc(lowest, 1)

                def mix(n):
                    t, h = units[n][:2]
                    o_h = keep.o[:, t, h * HD:(h + 1) * HD]
                    dve.wait_ge(valued, n + 2)
                    dve.reciprocal(coef[:], mass[:, t % 2, :, h])
                    dve.drain()
                    dve.tensor_tensor(coef[:], coef[:], keep.gate[:, t, h * N_BRANCH + 1:(h + 1) * N_BRANCH], ALU.mult)
                    for b in range(2):
                        dve.drain()
                        last = dve.scalar_tensor_tensor(o_h, ps_o[:, h % 2, b, 0:HD], coef[:, b:b + 1], o_h,
                                                        ALU.mult, ALU.add)
                    last.then_inc(head_mixed, 1)
                    dve.drain()

                maximum(0)
                maximum(1)
                for n in range(len(units)):
                    if n + 2 < len(units):
                        maximum(n + 2)
                    take(dve, lambda o, i: dve.tensor_copy(o, i), n, 0)
                    if n >= 2 and n % 2 == 0:
                        mix(n - 2)
                mix(len(units) - 2)

            @block.sync
            def _(sp):
                for n, t in enumerate(order):
                    sp.wait_ge(head_mixed, NH * (n + 1))
                    sp.dma_start(y_out[t * P:(t + 1) * P, RET_W:RET_W + NSA_W], keep.o[:, t, :]).then_inc(stored, 16)
                sp.wait_ge(stored, 16 * NT)


def sparse_constants(con):
    f = np.float32
    slopes = f(2) ** (f(-8) * np.arange(1, NH + 1, dtype=f) / f(NH))
    tok = np.arange(S).reshape(NT, P).T
    j = np.arange(NS)
    away = (SEL * j[None, None, :] - tok[:, :, None]).astype(f)
    rows = np.concatenate([slopes[None, None, :, None] * away[:, :, None, :],
                           np.broadcast_to(slopes[None, None, :, None], (P, NT, NH, 1))], axis=3)
    con["q_rows"] = rows.reshape(P, -1)

    def key_rows(at):
        return np.concatenate([(at[None, :] // SEL == j[:, None]), (at % SEL)[None, :] * (at < S)[None, :]], axis=0)
    con["key_rows"] = key_rows(np.arange(S))
    con["cmp_rows"] = key_rows(np.arange(NC_) * CMP_STRIDE + 2 * CMP_STRIDE - 1)
    q_block = tok[:, :, None] // SEL
    forced = (j == 0) | (j == q_block) | (j == q_block - 1)
    con["forced"] = np.where(forced, 1e3, np.where(SEL * j <= tok[:, :, None], 0.0, -1e3)).reshape(P, -1)
    p = np.arange(P)
    causal = np.where(p[None, :] <= p[:, None], 0.0, NEG)
    far = np.where(p[None, :] > p[:, None], 0.0, NEG)
    cmp_end = np.arange(NC_) * CMP_STRIDE + 2 * CMP_STRIDE - 1
    c_mask = np.where(cmp_end[None, None, :] <= tok[:, :, None], 0.0, NEG).reshape(P, -1)
    con["masks"] = np.concatenate([causal, far, c_mask], axis=1)
    picks = np.zeros((G, NS, G, S))
    for g in range(G):
        picks[g, :, g, :] = np.arange(S)[None, :] // SEL == j[:, None]
    con["picks"] = picks.reshape(G * NS, G * S)
    return {k: np.ascontiguousarray(v, dtype=f) for k, v in con.items()}


class Kept:

    def __init__(self, m):
        self.v = m.sb("v", [P, NT, 2, KV_W])
        self.gate = m.sb("gate", [P, NT, NH * N_BRANCH])
        self.kT = m.sb("kT", [QR, 2, G, S])
        self.kcT = m.sb("kcT", [QR, G, NC_])
        self.qT = m.sb("qT", [QR, NT * NH, P])
        self.forced = m.sb("forced", [P, NT, NS])
        self.masks = m.sb("masks", [P, 2 * P + NT * NC_], BF16)
        self.picks = m.sb("picks", [G * NS, G * S], BF16)
        self.ident_b = m.sb("ident_b", [P, P], BF16)
        self.v_cmp = m.sb("v_cmp", [P, G, 2 * HD])
        self.selT = m.sb("selT", [G * NS, NT, P], BF16)
        self.o = m.sb("o", [P, NT, NSA_W])


def trunk(nc, a, con, out):
    ctx = ExitStack()
    with ctx:
        def dram(name, shape, dt=F32):
            return nc.dram_tensor(name, shape, dt).ap()

        proj = dram("proj", [S, IN_W])
        mixer = dram("mixer", [S, D])
        stream = [dram(f"stream{j}", [S, D]) for j in range(3)]
        xn = dram("xn", [S, D])
        table = dram("table", [NE * CAP, 2], I32)
        slots = dram("slots", [2 * S, D])

        with Pool_(nc, "all", whole=True) as top:
            cst = Constants(top)
            gates = top.sb("gates", [P, 2 * NT])
            most = top.sb("most", [P, 1], I32)
            with nc.Block() as block:
                constants(nc, cst, block)

            def moe(layer, src):
                with Pool_(nc, f"weights{layer}") as held:
                    weights = ExpertWeights(held, a["moe_w_gate"][layer, :, :, :], a["moe_w_up"][layer, :, :, :],
                                            a["moe_w_down"][layer, :, :, :])
                    with Pool_(nc, f"moe{layer}") as m:
                        xT = m.sb("xT", [P, KT, S])
                        norm_transpose(nc, f"fn{layer}", src, cst.ident, xT, gain=a["ffn_norm_g"][layer, :], xn_dram=xn)
                        route(nc, f"rt{layer}", xT, a["moe_wg_group"][layer, :, :], a["moe_bg_group"][layer, :],
                              a["moe_wg_expert"][layer, :, :], a["moe_bg_expert"][layer, :], table, gates, most,
                              weights, cst)
                    experts(nc, f"ex{layer}", xn, weights, table, slots, most, cst.ident)

            with Pool_(nc, "in") as m:
                xT_hi, xT_lo = m.sb("xT_hi", [P, KT, S], F32R), m.sb("xT_lo", [P, KT, S], F32R)
                norm_transpose(nc, "mn0", a["x"][0, :, :], cst.ident, xT_hi, xT_lo, gain=a["mix_norm_g"][0, :])
                project(nc, "in0", xT_hi, xT_lo, a["ev_w_in"][0, :, :], IN_W, proj)
            with Pool_(nc, "mix0") as m:
                keep = Kept(m)
                with Pool_(nc, "raw") as raw:
                    keep.kvc2 = raw.sb("kvc2", [P, 2, NT, G, 2, HD])
                    retention_and_rows(nc, "ret", proj, a["ev_ret_norm_g"][0, :], a["ev_q_norm_g"][0, :],
                                       a["ev_k_norm_g"][0, :, :], cst, con, keep, mixer)
                    sparse_prepare(nc, "prep", a["ev_k_norm_g"][0, :, :], a["ev_cmp_pe"][0, :, :, :],
                                   a["ev_w_cmp1"][0, :, :, :], a["ev_w_cmp2"][0, :, :, :], cst, keep)
                sparse_attend(nc, "att", cst, keep, mixer)
            with Pool_(nc, "out") as m:
                xT_hi, xT_lo = m.sb("xT_hi", [P, KT, S], F32R), m.sb("xT_lo", [P, KT, S], F32R)
                norm_transpose(nc, "tr0", mixer, cst.ident, xT_hi, xT_lo)
                project(nc, "out0", xT_hi, xT_lo, a["ev_w_out"][0, :, :], D, stream[0], residual=a["x"][0, :, :])
            moe(0, stream[0])

            with Pool_(nc, "odd") as m:
                zT_hi, zT_lo = m.sb("zT_hi", [P, KT, S], F32R), m.sb("zT_lo", [P, KT, S], F32R)
                with Pool_(nc, "oddx") as x:
                    xT_hi, xT_lo = x.sb("xT_hi", [P, KT, S], F32R), x.sb("xT_lo", [P, KT, S], F32R)
                    norm_transpose(nc, "mn1", stream[0], cst.ident, xT_hi, xT_lo, gain=a["mix_norm_g"][1, :],
                                   mix=(slots, gates, stream[1]))
                    gated_conv(nc, "conv", xT_hi, xT_lo, a["od_w_in"][0, :, :], a["od_conv_w"][0, :, :],
                               a["od_conv_b"][0, :], zT_hi, zT_lo)
                project(nc, "out1", zT_hi, zT_lo, a["od_w_out"][0, :, :], D, stream[2], residual=stream[1])
            moe(1, stream[2])
            finish(nc, "end", stream[2], slots, gates, out)


def finish(nc, name, src, slots, gates, out):
    with Pool_(nc, name) as m:
        rows = m.sb("rows", [P, NT, D])
        ya = m.sb("ya", [P, 2, 2, D])
        loaded, mixed, stored = m.sems("loaded", NT), m.sem("mixed"), m.sem("stored")
        with nc.Block() as block:
            @block.sync
            def _(sp):
                for t in range(NT):
                    sp.dma_start(rows[:, t, :], src[t * P:(t + 1) * P, :]).then_inc(loaded[t], 16)
                    if t >= 2:
                        sp.wait_ge(mixed, t - 1)
                    for c in range(2):
                        at = c * S + t * P
                        sp.dma_start(ya[:, t % 2, c, :], slots[at:at + P, :]).then_inc(loaded[t], 16)

            @block.vector
            def _(dve):
                for t in range(NT):
                    dve.wait_ge(loaded[t], 48)
                    for c in range(2):
                        last = dve.scalar_tensor_tensor(rows[:, t, :], ya[:, t % 2, c, :],
                                                        gates[:, c * NT + t:c * NT + t + 1], rows[:, t, :], ALU.mult, ALU.add)
                        if c == 0:
                            dve.drain()
                    last.then_inc(mixed, 1)

            @block.scalar
            def _(act):
                for t in range(NT):
                    act.wait_ge(mixed, t + 1)
                    act.dma_start(out[t * P:(t + 1) * P, :], rows[:, t, :]).then_inc(stored, 16)
                act.wait_ge(stored, 16 * NT)


class Constants:
    def __init__(self, m):
        self.ident, self.ones, self.before = (m.sb(n, [P, P]) for n in ("ident", "ones", "before"))
        self.iota, self.iota_i = m.sb("iota", [P, 64]), m.sb("iota_i", [P, 64], I32)


INPUTS = ["x", "mix_norm_g", "ffn_norm_g", "ev_w_in", "ev_cmp_pe", "ev_w_cmp1", "ev_w_cmp2", "ev_q_norm_g", "ev_k_norm_g",
          "ev_ret_norm_g", "ev_w_out", "od_w_in", "od_conv_w", "od_conv_b", "od_w_out", "moe_wg_group", "moe_bg_group",
          "moe_wg_expert", "moe_bg_expert", "moe_w_gate", "moe_w_up", "moe_w_down"]


def kernel(**inputs):
    import concourse.bacc as bacc
    from concourse.bass_utils import run_bass_kernel_spmd

    nc = bacc.Bacc("TRN2", target_bir_lowering=False, num_devices=1)
    arrays = {}

    def given(name, array):
        arrays[name] = np.ascontiguousarray(array)
        return nc.dram_tensor(name, array.shape, mybir.dt.from_np(arrays[name].dtype), kind="ExternalInput").ap()

    a = {n: given(f"in_{n}", np.asarray(inputs[n])) for n in INPUTS}
    con = {n: given(f"con_{n}", v) for n, v in sparse_constants(shape_constants()).items()}
    out = nc.dram_tensor("out", (1, S, D), F32, kind="ExternalOutput").ap()
    trunk(nc, a, con, out[0, :, :])
    r = run_bass_kernel_spmd(nc, [arrays], core_ids=[0])
    return np.asarray(r.results[0]["out"])
```

```python
import numpy as np
import concourse.bass as bass
from concourse import mybir
from contextlib import ExitStack

F32 = mybir.dt.float32
F32R = mybir.dt.float32r
BF16 = mybir.dt.bfloat16
I32 = mybir.dt.int32
ALU = mybir.AluOpType
ACT = mybir.ActivationFunctionType
X = mybir.AxisListType.X
ds = bass.ds

P = 128
S = 1024
D = 1024
NT = S // P
KT = D // P
HD = 64
RH = 8
NH = 8
G = 2
R = NH // G
RET_W = RH * HD
NSA_W = NH * HD
KV_W = G * HD
N_BRANCH = 3
IN_W = 4 * RET_W + NSA_W + 6 * KV_W + NH * N_BRANCH
C_NQ = 4 * RET_W
C_KC = C_NQ + NSA_W
C_VC, C_KS, C_VS, C_KW, C_VW, C_NG = (C_KC + KV_W * n for n in range(1, 7))
CMP_STRIDE = 16
CMP_HID = 128
NC_ = S // CMP_STRIDE
SEL = 64
NS = S // SEL
WINDOW = 256
NG = 4
EPG = 8
NE = NG * EPG
DE = 256
EPS = 1e-6
NEG = -1e30
COLS = 512


class Pool_:

    ENOUGH = 80
    used_up = []

    def __init__(self, nc, name, whole=False, clear=True):
        self.nc, self.name, self.ctx, self.used, self.whole, self.clear = nc, name, ExitStack(), [], whole, clear
        if whole:
            Pool_.used_up = []

    def __enter__(self):
        return self

    def __exit__(self, *a):
        Pool_.used_up.extend(self.used)
        if (self.whole or self.clear and len(Pool_.used_up) > self.ENOUGH) and a[0] is None:
            self.nc.clear_and_free_semaphores(Pool_.used_up)
            self.nc.all_engine_barrier()
            Pool_.used_up = []
        return self.ctx.__exit__(*a)

    def sb(self, name, shape, dt=F32):
        return self.ctx.enter_context(self.nc.sbuf_tensor(f"{self.name}_{name}", shape, dt))

    def ps(self, name, shape, dt=F32):
        return self.ctx.enter_context(self.nc.psum_tensor(f"{self.name}_{name}", shape, dt))

    def sem(self, name):
        self.used.append(self.nc.alloc_semaphore(f"{self.name}_{name}"))
        return self.used[-1]

    def sems(self, name, n=2):
        return [self.sem(f"{name}{j}") for j in range(n)]


def row_of(vec, n=P):
    return bass.AP(tensor=vec.tensor, offset=vec.offset, ap=[[0, n]] + [list(x) for x in vec.ap])


def warm_up(pe, bank, a, b, n=18):
    for _ in range(n):
        pe.matmul(bank, a, b, start=True, stop=True)


def norm_transpose(nc, name, src, ident, xT_hi, xT_lo=None, gain=None, mix=None, ahead=None):
    U = 4
    with Pool_(nc, name) as m:
        xin = m.sb("xin", [P, U, D])
        ps_t = m.ps("ps_t", [P, U, KT, P])
        loaded, mixed, stored = m.sems("loaded", U), m.sems("mixed", U), m.sems("stored", U)
        summed, root_ready, normed = m.sems("summed", U), m.sems("root_ready", U), m.sems("normed", U)
        transposed, hi_ready, lo_ready = m.sems("transposed", U), m.sems("hi_ready", U), m.sems("lo_ready", U)
        gain_loaded = m.sem("gain_loaded")
        apart = m.sem("apart")
        if gain is not None:
            gains = m.sb("gains", [P, D])
            xn = m.sb("xn", [P, U, D])
            ssq = m.sb("ssq", [P, U])
            root = m.sb("root", [P, U])
            rstd = m.sb("rstd", [P, U])
            eps = m.sb("eps", [P, 1])
            eps_ready = m.sem("eps_ready")
        if mix is not None:
            slots, gates, mix_out = mix
            ya = m.sb("ya", [P, U, D])
            expert_rows = (ya, xn)
        rows = xn if gain is not None else xin

        with nc.Block() as block:
            @block.sync
            def _(sp):
                if gain is not None:
                    sp.dma_start(gains[:], row_of(gain)).then_inc(gain_loaded, 16)
                with sp.Fori(0, NT // U) as i:
                    for u in range(U):
                        first, second = sp.snap((U * i + u) * P), sp.snap((U * i + u) * P + S)
                        stores = sp.snap(i * 16) if mix is not None else None
                        sp.wait_ge(transposed[u], i)
                        if mix is not None:
                            sp.sem_inc(apart, 1)
                            sp.wait_ge(stored[u], stores)
                        sp.dma_start(xin[:, u, :], src[ds(first, P), :]).then_inc(loaded[u], 16)
                        if mix is not None:
                            for c, row in enumerate((first, second)):
                                sp.dma_start(expert_rows[c][:, u, :], slots[ds(row, P), :]
                                             ).then_inc(loaded[u], 16)
                    for u in range(U):
                        first = sp.snap((U * i + u) * P)
                        if mix is not None:
                            sp.wait_ge(mixed[u], i + 1)
                            sp.dma_start(mix_out[ds(first, P), :], xin[:, u, :]).then_inc(stored[u], 16)
                if ahead is not None:
                    ahead.load(sp)
                if mix is not None:
                    for u in range(U):
                        sp.wait_ge(stored[u], 16 * (NT // U))

            @block.scalar
            def _(act):
                if gain is not None:
                    act.wait_ge(eps_ready, 1)
                with act.Fori(0, NT // U) as i:
                    if gain is not None:
                        for u in range(U):
                            if mix is None:
                                act.wait_ge(loaded[u], 16 * i + 16)
                            else:
                                act.wait_ge(mixed[u], i + 1)
                            act.wait_ge(transposed[u], i)
                            act.activation(xn[:, u, :], xin[:, u, :], ACT.Square,
                                           accum_out=ssq[:, u:u + 1]).then_inc(summed[u], 1)
                            act.wait_ge(summed[u], i + 1)
                            act.wait_ge(normed[u], i)
                            act.activation(root[:, u:u + 1], ssq[:, u:u + 1], ACT.Sqrt, bias=eps[:],
                                           scale=1.0 / D).then_inc(root_ready[u], 1)
                    for u in range(U):
                        act.wait_ge(transposed[u], i + 1)
                        act.activation(xT_hi[:, :, ds((U * i + u) * P, P)], ps_t[:, u, :, :],
                                       ACT.Copy).then_inc(hi_ready[u], 1)

            @block.vector
            def _(dve):
                if gain is not None:
                    dve.memset(eps[:], EPS).then_inc(eps_ready, 1)
                    dve.wait_ge(gain_loaded, 16)
                with dve.Fori(0, NT // U) as i:
                    for u in range(U):
                        if mix is not None:
                            dve.wait_ge(loaded[u], 48 * i + 48)
                            for c in range(2):
                                last = dve.scalar_tensor_tensor(
                                    xin[:, u, :], expert_rows[c][:, u, :], gates[:, ds(U * i + (u + c * NT), 1)],
                                    xin[:, u, :], ALU.mult, ALU.add)
                                if c == 1:
                                    last.then_inc(mixed[u], 1)
                                dve.drain()
                    for u in range(U):
                        if gain is not None:
                            dve.wait_ge(root_ready[u], i + 1)
                            dve.reciprocal(rstd[:, u:u + 1], root[:, u:u + 1])
                            dve.drain()
                            dve.scalar_tensor_tensor(xn[:, u, :], xin[:, u, :], rstd[:, u:u + 1], gains[:],
                                                     ALU.mult, ALU.mult).then_inc(normed[u], 1)
                    for u in range(U):
                        if xT_lo is not None:
                            dve.wait_ge(hi_ready[u], i + 1)
                            at = ds((U * i + u) * P, P)
                            dve.tensor_tensor(xT_lo[:, :, at], ps_t[:, u, :, :], xT_hi[:, :, at].bitcast(F32),
                                              ALU.subtract).then_inc(lo_ready[u], 1)

            @block.tensor
            def _(pe):
                with pe.Fori(0, NT // U) as i:
                    for u in range(U):
                        pe.wait_ge(*((normed[u], i + 1) if gain is not None else (loaded[u], 16 * i + 16)))
                        pe.wait_ge(*((lo_ready[u], i) if xT_lo is not None else (hi_ready[u], i)))
                        for k in range(KT):
                            last = pe.transpose(ps_t[:, u, k, :], rows[:, u, k * P:(k + 1) * P], ident[:])
                        last.then_inc(transposed[u], 1)


class FirstWeights:

    def __init__(self, m, w):
        self.w_k = w.rearrange("(k p) n -> p k n", p=P)
        self.raw = m.sb("first_raw", [P, KT, COLS])
        self.loaded = m.sems("first_loaded")

    def load(self, sp):
        for c in range(2):
            at = slice(c * (KT // 2), (c + 1) * (KT // 2))
            sp.dma_start(self.raw[:, at, :], self.w_k[:, at, 0:COLS]).then_inc(self.loaded[c], 16)


def project(nc, name, xT_hi, xT_lo, w, width, out, ahead, residual=None):
    full = width // COLS
    with Pool_(nc, name) as m:
        raw = [ahead.raw, m.sb("raw", [P, KT, COLS])]
        w_hi = m.sb("w_hi", [P, 2, KT, COLS], F32R)
        w_lo = m.sb("w_lo", [P, 2, KT, COLS], F32R)
        stage = m.sb("stage", [P, 4, COLS])
        ps = m.ps("ps", [P, NT, COLS])
        raw_loaded = ahead.loaded + m.sems("raw_loaded")
        hi_ready, lo_ready = m.sems("hi_ready"), m.sems("lo_ready")
        product_ready = m.sems("product_ready", NT - 1)
        last_product = m.sems("last_product")
        tile_out = m.sems("tile_out", NT)
        stage_stored = m.sems("stage_stored", 4)
        res_loaded = m.sems("res_loaded", 4)
        if residual is not None:
            res = m.sb("res", [P, 4, COLS])
        w_k = w.rearrange("(k p) n -> p k n", p=P)

        n_blocks = -(-width // COLS)
        wide = [min(COLS, width - b * COLS) for b in range(n_blocks)]
        HALF = KT // 2

        with nc.Block() as block:
            @block.sync
            def _(sp):
                for b, n in list(enumerate(wide))[1:]:
                    if b >= 2:
                        sp.wait_ge(lo_ready[b % 2], 2 * (b // 2))
                    for c in range(2):
                        at = slice(c * HALF, (c + 1) * HALF)
                        sp.dma_start(raw[b % 2][:, at, 0:n], w_k[:, at, b * COLS:b * COLS + n]
                                     ).then_inc(raw_loaded[2 * (b % 2) + c], 16)
                for s in range(4):
                    sp.wait_ge(stage_stored[s], 16 * n_blocks * (NT // 4))

            if residual is not None:
                @block.gpsimd
                def _(pool):
                    for b, n in enumerate(wide):
                        for t in range(NT):
                            if (b, t) >= (0, 4):
                                pool.wait_ge(tile_out[(t + 4) % NT], b + (t >= 4))
                            pool.dma_start(res[:, t % 4, 0:n], residual[t * P:(t + 1) * P, b * COLS:b * COLS + n]
                                           ).then_inc(res_loaded[t % 4], 16)

            @block.scalar
            def _(act):
                def high(b):
                    for c in range(2):
                        at, n = slice(c * HALF, (c + 1) * HALF), wide[b]
                        act.wait_ge(raw_loaded[2 * (b % 2) + c], 16 * (b // 2 + 1))
                        if b >= 2:
                            act.wait_ge(last_product[b % 2], b // 2)
                        act.activation(w_hi[:, b % 2, at, 0:n], raw[b % 2][:, at, 0:n], ACT.Copy
                                       ).then_inc(hi_ready[b % 2], 1)

                high(0)
                for b, n in enumerate(wide):
                    if b + 1 < n_blocks:
                        high(b + 1)
                    for t in range(NT):
                        act.wait_ge(tile_out[t], b + 1)
                        act.dma_start(out[t * P:(t + 1) * P, b * COLS:b * COLS + n], stage[:, t % 4, 0:n]
                                      ).then_inc(stage_stored[t % 4], 16)

            @block.vector
            def _(dve):
                def low(b):
                    for c in range(2):
                        at, n = slice(c * HALF, (c + 1) * HALF), wide[b]
                        dve.wait_ge(hi_ready[b % 2], 2 * (b // 2) + c + 1)
                        dve.tensor_tensor(w_lo[:, b % 2, at, 0:n], raw[b % 2][:, at, 0:n],
                                          w_hi[:, b % 2, at, 0:n].bitcast(F32), ALU.subtract
                                          ).then_inc(lo_ready[b % 2], 1)

                low(0)
                for b, n in enumerate(wide):
                    for t in range(NT):
                        if t == 2 and b + 1 < n_blocks:
                            low(b + 1)
                        if t < NT - 1:
                            dve.wait_ge(product_ready[t], b + 1)
                        else:
                            dve.wait_ge(last_product[b % 2], b // 2 + 1)
                        if (b, t) >= (0, 4):
                            dve.wait_ge(stage_stored[t % 4], 16 * (2 * b + t // 4))
                        if residual is None:
                            last = dve.tensor_copy(stage[:, t % 4, 0:n], ps[:, t, 0:n])
                        else:
                            dve.wait_ge(res_loaded[t % 4], 16 * (2 * b + t // 4 + 1))
                            last = dve.tensor_tensor(stage[:, t % 4, 0:n], ps[:, t, 0:n], res[:, t % 4, 0:n], ALU.add)
                        last.then_inc(tile_out[t], 1)

            @block.tensor
            def _(pe):
                warm_up(pe, ps[:, NT - 1, :], xT_hi[:, 0, 0:P], xT_hi[:, 0, 0:COLS], 12)

                def body(u, i, n):
                    for t in range(NT):
                        pe.wait_ge(tile_out[t], 2 * i + u)
                        at = slice(t * P, (t + 1) * P)
                        for k in range(KT):
                            if t == 0 and k % HALF == 0:
                                pe.wait_ge(lo_ready[u], 2 * i + k // HALF + 1)
                            for j, (a, w_part) in enumerate(((xT_hi, w_hi), (xT_hi, w_lo), (xT_lo, w_hi))):
                                last = pe.matmul(ps[:, t, 0:n], a[:, k, at], w_part[:, u, k, 0:n],
                                                 start=(k == 0 and j == 0), stop=(k == KT - 1 and j == 2))
                        last.then_inc(product_ready[t] if t < NT - 1 else last_product[u], 1)

                with pe.Fori(0, full // 2) as i:
                    for u in range(2):
                        body(u, i, COLS)
                for b in range(full // 2 * 2, n_blocks):
                    body(b % 2, b // 2, wide[b])

CAP = S
NOWHERE = 4 * S


EXPERT_BUFFERS = 4


class ExpertData:

    def __init__(self, m, w_gate, w_up, w_down):
        self.gu = m.sb("w_gu", [P, EXPERT_BUFFERS, KT, 2 * DE])
        self.down = m.sb("w_d", [P, EXPERT_BUFFERS, DE // P, D])
        self.xg = m.sb("xg", [P, EXPERT_BUFFERS, D])
        self.dest = m.sb("dest", [P, 2, NT], I32)
        self.codes = m.sb("codes", [P, 2, NT, 2], I32)
        self.gu_loaded, self.down_loaded = m.sems("gu_loaded", EXPERT_BUFFERS), m.sems("down_loaded", EXPERT_BUFFERS)
        self.w_gate, self.w_up, self.w_down = w_gate, w_up, w_down

    def load_gate_up(self, sp, e, buffer):
        for j, src in enumerate((self.w_gate, self.w_up)):
            sp.dma_start(self.gu[:, buffer, :, j * DE:(j + 1) * DE],
                         src[ds(e, 1), :, :].rearrange("a (k p) n -> p (a k) n", p=P)).then_inc(self.gu_loaded[buffer], 16)

    def load_down(self, sp, e, buffer):
        sp.dma_start(self.down[:, buffer, :, :],
                     self.w_down[ds(e, 1), :, :].rearrange("a (k p) n -> p (a k) n", p=P)
                     ).then_inc(self.down_loaded[buffer], 16)


def norm_and_logits(nc, name, src, gain, w_group, b_group, w_expert, b_expert, xn_dram, lg, table, data,
                    ident):
    NL = NG + NE
    U = 4
    with Pool_(nc, name, clear=False) as m:
        gains = m.sb("gains", [P, D])
        w = m.sb("w", [P, KT, NL])
        bias = m.sb("bias", [P, NL])
        xin = m.sb("xin", [P, U, D])
        xn = m.sb("xn", [P, U, D])
        xT = m.sb("xT", [P, 2, KT, P])
        nowhere = m.sb("nowhere", [P, NE * CAP * 2 // P], I32)
        ssq, root, rstd = (m.sb(n, [P, U]) for n in ("ssq", "root", "rstd"))
        eps = m.sb("eps", [P, 1])
        ps_t = m.ps("ps_t", [P, 2, KT, P])
        ps_l = m.ps("ps_l", [P, U, COLS])
        gain_loaded, router_loaded, eps_ready = m.sem("gain_loaded"), m.sem("router_loaded"), m.sem("eps_ready")
        filled, cleared = m.sem("filled"), m.sem("cleared")
        loaded, summed, root_ready, normed = (m.sems(n, U) for n in ("loaded", "summed", "root_ready", "normed"))
        stored, transposed, xT_ready = (m.sems(n, U) for n in ("stored", "transposed", "xT_ready"))
        logits, logits_out = m.sems("logits", U), m.sems("logits_out", U)

        def two_before(sems, i, u):
            return (sems[u - 2], i + 1) if u >= 2 else (sems[u + 2], i)

        with nc.Block() as block:
            @block.sync
            def _(sp):
                sp.dma_start(gains[:], row_of(gain)).then_inc(gain_loaded, 16)
                with sp.Fori(0, NT // U) as i:
                    for u in range(U):
                        first = sp.snap((U * i + u) * P)
                        sp.wait_ge(normed[u], i)
                        sp.dma_start(xin[:, u, :], src[ds(first, P), :]).then_inc(loaded[u], 16)
                    for u in range(U):
                        first = sp.snap((U * i + u) * P)
                        sp.wait_ge(normed[u], i + 1)
                        sp.dma_start(xn_dram[ds(first, P), :], xn[:, u, :]).then_inc(stored[u], 16)
                for e in range(EXPERT_BUFFERS):
                    data.load_gate_up(sp, e, e)
                    data.load_down(sp, e, e)
                for u in range(U):
                    sp.wait_ge(stored[u], 16 * (NT // U))

            @block.scalar
            def _(act):
                act.dma_start(w[:, :, 0:NG], w_group.rearrange("(k p) n -> p k n", p=P)).then_inc(router_loaded, 16)
                act.dma_start(w[:, :, NG:NL], w_expert.rearrange("(k p) n -> p k n", p=P)).then_inc(router_loaded, 16)
                act.dma_start(bias[:, 0:NG], row_of(b_group)).then_inc(router_loaded, 16)
                act.dma_start(bias[:, NG:NL], row_of(b_expert)).then_inc(router_loaded, 16)
                act.wait_ge(filled, 1)
                act.dma_start(table.rearrange("(p r) c -> p (r c)", p=P), nowhere[:]).then_inc(cleared, 16)
                act.wait_ge(eps_ready, 1)
                with act.Fori(0, NT // U) as i:
                    for u in range(U):
                        act.wait_ge(loaded[u], 16 * i + 16)
                        act.wait_ge(transposed[u], i)
                        act.wait_ge(stored[u], 16 * i)
                        act.activation(xn[:, u, :], xin[:, u, :], ACT.Square, accum_out=ssq[:, u:u + 1]
                                       ).then_inc(summed[u], 1)
                        act.wait_ge(summed[u], i + 1)
                        act.activation(root[:, u:u + 1], ssq[:, u:u + 1], ACT.Sqrt, bias=eps[:], scale=1.0 / D
                                       ).then_inc(root_ready[u], 1)
                    for u in range(U):
                        act.wait_ge(transposed[u], i + 1)
                        act.wait_ge(*two_before(logits, i, u))
                        act.activation(xT[:, u % 2, :, :], ps_t[:, u % 2, :, :], ACT.Copy).then_inc(xT_ready[u], 1)
                act.wait_ge(cleared, 16)

            @block.gpsimd
            def _(pool):
                pool.memset(nowhere[:], NOWHERE).then_inc(filled, 1)
                pool.iota(data.codes[:, :, :, 0], pattern=[[0, 2], [P, NT]], base=0, channel_multiplier=1)
                pool.iota(data.codes[:, :, :, 1], pattern=[[S, 2], [P, NT]], base=0, channel_multiplier=1)
                pool.memset(data.xg[:], 0.0)
                pool.drain()

            @block.vector
            def _(dve):
                dve.memset(eps[:], EPS).then_inc(eps_ready, 1)
                dve.wait_ge(gain_loaded, 16)
                dve.wait_ge(router_loaded, 64)
                with dve.Fori(0, NT // U) as i:
                    for u in range(U):
                        dve.wait_ge(root_ready[u], i + 1)
                        dve.reciprocal(rstd[:, u:u + 1], root[:, u:u + 1])
                        dve.drain()
                        dve.scalar_tensor_tensor(xn[:, u, :], xin[:, u, :], rstd[:, u:u + 1], gains[:],
                                                 ALU.mult, ALU.mult).then_inc(normed[u], 1)
                    for u in range(U):
                        dve.wait_ge(logits[u], i + 1)
                        dve.tensor_tensor(lg[:, ds(U * i + u, 1), :], ps_l[:, u, 0:NL].unsqueeze(1), bias[:].unsqueeze(1),
                                          ALU.add).then_inc(logits_out[u], 1)
                dve.drain()

            @block.tensor
            def _(pe):
                warm_up(pe, ps_t[:, 0, 0, :], ident[:], ident[:])
                pe.wait_ge(router_loaded, 64)

                def turn(i, u):
                    pe.wait_ge(normed[u], i + 1)
                    pe.wait_ge(*two_before(xT_ready, i, u))
                    for k in range(KT):
                        last = pe.transpose(ps_t[:, u % 2, k, :], xn[:, u, k * P:(k + 1) * P], ident[:])
                    last.then_inc(transposed[u], 1)

                def multiply(i, u):
                    pe.wait_ge(xT_ready[u], i + 1)
                    pe.wait_ge(logits_out[u], i)
                    for k in range(KT):
                        last = pe.matmul(ps_l[:, u, 0:NL], xT[:, u % 2, k, :], w[:, k, :], start=(k == 0), stop=(k == KT - 1))
                    last.then_inc(logits[u], 1)

                with pe.Fori(0, NT // U) as i:
                    for u in range(U + 1):
                        if u < U:
                            turn(i, u)
                        if u:
                            multiply(i, u - 1)


def route(nc, name, lg, gates, most, data, cst):
    NL = NG + NE
    with Pool_(nc, name, clear=False) as m:
        t4, e4, v4 = (m.sb(n, [P, NT, NG]) for n in ("t4", "e4", "v4"))
        em, v32 = (m.sb(n, [P, NT, NE]) for n in ("em", "v32"))
        chosen = m.sb("chosen", [P, 2, NT, NE])
        both = m.sb("both", [P, NT, NE])
        small = m.sb("small", [P, 8, NT])
        run = m.sb("run", [P, NT + 1, NE])
        pos = m.sb("pos", [P, NT, NE])
        dest_f = m.sb("dest_f", [P, 2, NT])
        dest = data.dest
        most_f = m.sb("most_f", [P, 1])
        ps_c = m.ps("ps_c", [P, 2, NT, NE])
        shifted, exps = m.sem("shifted"), m.sem("exps")
        chosen_ready, counted = m.sem("chosen_ready"), m.sem("counted")
        top, gsum, best, second, e2, den, inv = (small[:, j, :] for j in range(7))

        with nc.Block() as block:
            @block.scalar
            def _(act):
                act.wait_ge(shifted, 1)
                act.activation(e4[:], t4[:], ACT.Exp).then_inc(exps, 1)
                act.wait_ge(shifted, 2)
                act.activation(e2, den, ACT.Exp).then_inc(exps, 1)

            @block.tensor
            def _(pe):
                pe.wait_ge(chosen_ready, 1)
                pe.matmul(ps_c[:, 0, :, :], cst.before[:], both[:], start=True, stop=True)
                pe.matmul(ps_c[:, 1, :, :], cst.ones[:], both[:], start=True, stop=True).then_inc(counted, 1)

            @block.vector
            def _(dve):
                def one_hot(out, values, maximum, iota, v, n):
                    wide = [P, NT, n]
                    dve.tensor_tensor(v[:], values, maximum.unsqueeze(2).to_broadcast(wide), ALU.is_equal)
                    dve.drain()
                    dve.scalar_tensor_tensor(v[:], v[:], -64.0, iota.unsqueeze(1).to_broadcast(wide), ALU.mult, ALU.add)
                    dve.drain()
                    dve.tensor_reduce(inv, v[:], X, ALU.min)
                    dve.drain()
                    dve.tensor_tensor(out, v[:], inv.unsqueeze(2).to_broadcast(wide), ALU.is_equal)
                    dve.drain()

                dve.tensor_reduce(top, lg[:, :, 0:NG], X, ALU.max)
                dve.drain()
                dve.tensor_tensor(t4[:], lg[:, :, 0:NG], top.unsqueeze(2).to_broadcast([P, NT, NG]), ALU.subtract
                                  ).then_inc(shifted, 1)
                one_hot(v4[:], lg[:, :, 0:NG], top, cst.iota[:, 0:NG], v4, NG)
                dve.tensor_scalar(v4[:], v4[:], -1.0, -NEG, ALU.add, ALU.mult)
                dve.drain()
                dve.tensor_tensor(em[:].rearrange("p t (g e) -> p t g e", g=NG),
                                  lg[:, :, NG:NL].rearrange("p t (g e) -> p t g e", g=NG),
                                  v4[:].unsqueeze(3).to_broadcast([P, NT, NG, EPG]), ALU.add)
                dve.drain()
                dve.tensor_reduce(best, em[:], X, ALU.max)
                dve.drain()
                one_hot(chosen[:, 0, :, :], em[:], best, cst.iota[:, 0:NE], v32, NE)
                dve.scalar_tensor_tensor(em[:], chosen[:, 0, :, :], 2 * NEG, em[:], ALU.mult, ALU.add)
                dve.drain()
                dve.tensor_reduce(second, em[:], X, ALU.max)
                dve.drain()
                dve.tensor_tensor(den, second, best, ALU.subtract).then_inc(shifted, 1)
                one_hot(chosen[:, 1, :, :], em[:], second, cst.iota[:, 0:NE], v32, NE)
                dve.tensor_tensor(both[:], chosen[:, 0, :, :], chosen[:, 1, :, :], ALU.add).then_inc(chosen_ready, 1)
                dve.wait_ge(exps, 2)
                dve.tensor_reduce(gsum, e4[:], X, ALU.add)
                dve.drain()
                dve.scalar_tensor_tensor(inv, e2, 1.0, gsum, ALU.add, ALU.mult)
                dve.drain()
                dve.reciprocal(gates[:, 0:NT], inv)
                dve.drain()
                dve.tensor_tensor(gates[:, NT:2 * NT], e2, gates[:, 0:NT], ALU.mult)
                dve.memset(run[:, 0, :], 0.0)
                dve.wait_ge(counted, 1)
                for t in range(NT):
                    dve.drain()
                    dve.tensor_tensor(run[:, t + 1, :], run[:, t, :], ps_c[:, 1, t, :], ALU.add)
                dve.drain()
                dve.tensor_tensor(pos[:], ps_c[:, 0, :, :], run[:, 0:NT, :], ALU.add)
                dve.tensor_reduce(most_f[:], run[:, NT, :], X, ALU.max)
                dve.drain()
                dve.scalar_tensor_tensor(pos[:], cst.iota[:, 0:NE].unsqueeze(1).to_broadcast([P, NT, NE]),
                                         float(CAP), pos[:], ALU.mult, ALU.add)
                dve.tensor_copy(most[:], most_f[:])
                dve.drain()
                for c in range(2):
                    dve.tensor_tensor(v32[:], chosen[:, c, :, :], pos[:], ALU.mult)
                    dve.drain()
                    dve.tensor_reduce(dest_f[:, c, :], v32[:], X, ALU.add)
                    dve.drain()
                dve.tensor_copy(dest[:], dest_f[:])
                dve.drain()


def experts(nc, name, xn_dram, data, table, slots, most, ident):
    U, B = 8, EXPERT_BUFFERS
    STEPS = NE // U
    with Pool_(nc, name) as m:
        idx = m.sb("idx", [P, U, 2], I32)
        gu_hi, gu_lo = (m.sb(n, [P, KT, 2 * DE], F32R) for n in ("gu_hi", "gu_lo"))
        d_hi, d_lo = (m.sb(n, [P, DE // P, D], F32R) for n in ("d_hi", "d_lo"))
        x_hi, x_lo = (m.sb(n, [P, 2, KT, P], F32R) for n in ("x_hi", "x_lo"))
        h_hi, h_lo = (m.sb(n, [P, 2, DE // P, P], F32R) for n in ("h_hi", "h_lo"))
        silu = m.sb("silu", [P, 2, DE])
        hid = m.sb("hid", [P, 2, DE])
        y = m.sb("y", [P, 2, D])
        ps_x = m.ps("ps_x", [P, KT, P])
        ps_h = m.ps("ps_h", [P, 2, 2 * DE])
        ps_t = m.ps("ps_t", [P, 2, 2 * P])
        ps_y = m.ps("ps_y", [P, D])
        xg, w_gu, w_d, gu_loaded, down_loaded = data.xg, data.gu, data.down, data.gu_loaded, data.down_loaded
        HALF = KT // 2
        first, second = slice(0, HALF), slice(HALF, KT)
        pieces = [(gu_hi[:, at, :], gu_lo[:, at, :], lambda v, at=at: w_gu[:, v, at, :]) for at in (first, second)]
        pieces.append((d_hi[:], d_lo[:], lambda v: w_d[:, v, :, :]))
        FIRST, SECOND, DOWN = range(3)
        idx_loaded, gathered, x_turned = m.sems("idx_loaded", U), m.sems("gathered", B), m.sems("x_turned", B)
        scattered = m.sems("scattered", U)
        piece_hi, piece_lo, piece_used = m.sems("piece_hi", 3), m.sems("piece_lo", 3), m.sems("piece_used", 3)
        x_hi_ready, x_lo_ready, silu_ready = m.sem("x_hi_ready"), m.sem("x_lo_ready"), m.sem("silu_ready")
        hid_ready = m.sems("hid_ready")
        h_turned, h_hi_ready, h_lo_ready, y_out = (m.sem(n) for n in ("h_turned", "h_hi_ready", "h_lo_ready", "y_out"))
        listed = m.sem("listed")
        apart = m.sem("apart")

        def waves(eng, body, first=0):
            full = eng.value_load(most[0:1, 0:1], min_val=0, max_val=CAP)
            with eng.Fori(first, CAP // P) as w:
                with eng.If(full > w * P):
                    body(w)

        def rounds(eng, start, step, end):
            def at(n, u):
                return (n + u // U, u % U)

            def body(n, more):
                for u in range(1, U + more):
                    step(at(n, u), at(n, u - 1), at(n, u + 1) if u + 1 < U or more else None)

            def wave(w):
                start(w * STEPS)
                with eng.Fori(0, STEPS - 1) as i:
                    body(w * STEPS + i, True)
                body(w * STEPS + (STEPS - 1), False)
                end((w * STEPS + (STEPS - 1), U - 1))
            waves(eng, wave)

        def uses(n, u):
            return n * (U // B) + u // B

        with nc.Block() as block:
            @block.sync
            def _(sp):
                def load_indices(u, row):
                    sp.dma_start(idx[:, u, :], table[ds(row, P), :]).then_inc(idx_loaded[u], 16)

                def load_weights(expert, u, split):
                    sp.wait_ge(piece_lo[SECOND], split)
                    data.load_gate_up(sp, expert, u % B)
                    sp.wait_ge(piece_lo[DOWN], split)
                    data.load_down(sp, expert, u % B)

                def round_(w, i):
                    n = w * STEPS + i
                    for u in range(U):
                        split = sp.snap(n * U + (u - B + 1))
                        row, expert = sp.snap((i * U + u) * CAP + w * P), sp.snap(i * U + u)
                        sp.wait_ge(scattered[u], 16 * n)
                        load_indices(u, row)
                        load_weights(expert, u, split)

                load_weights(B, B, 1)
                sp.wait_ge(listed, 16 * 2 * NT)
                for u in range(U):
                    load_indices(u, u * CAP)
                for u in range(B + 1, U):
                    load_weights(u, u, u - B + 1)
                with sp.Fori(1, STEPS) as i:
                    round_(0, i)

                def wave(w):
                    with sp.Fori(0, STEPS) as i:
                        round_(w, i)
                waves(sp, wave, first=1)

            @block.gpsimd
            def _(pool):
                last_token, last_slot = pool.to_reg(S - 1), pool.to_reg(2 * S - 1)
                for c in range(2):
                    for t in range(NT):
                        pool.indirect_dma_start(
                            out=table, out_offset=bass.IndirectOffsetOnAxis(ap=data.dest[:, c, t:t + 1], axis=0),
                            in_=data.codes[:, c, t, :], in_offset=None).then_inc(listed, 16)

                def gather(n, u):
                    pool.wait_ge(idx_loaded[u], 16 * n + 16)
                    pool.wait_ge(x_turned[u % B], uses(n, u))
                    pool.sem_inc(apart, 1)
                    pool.indirect_dma_start(
                        out=xg[:, u % B, :], out_offset=None, in_=xn_dram,
                        in_offset=bass.IndirectOffsetOnAxis(ap=idx[:, u, 0:1], axis=0),
                        bounds_check=last_token, oob_is_err=False).then_inc(gathered[u % B], 16)

                def scatter(n, u):
                    pool.wait_ge(y_out, n * U + (u + 1))
                    pool.sem_inc(apart, 1)
                    pool.indirect_dma_start(
                        out=slots, out_offset=bass.IndirectOffsetOnAxis(ap=idx[:, u, 1:2], axis=0),
                        in_=y[:, u % 2, :], in_offset=None,
                        bounds_check=last_slot, oob_is_err=False).then_inc(scattered[u], 16)

                def body(n, more):
                    for u in range(U):
                        if u + B < U:
                            gather(n, u + B)
                        elif more:
                            gather(n + 1, u + B - U)
                        scatter(n, u)

                def wave(w):
                    first = w * STEPS
                    for u in range(B):
                        gather(first, u)
                    with pool.Fori(0, STEPS - 1) as i:
                        body(w * STEPS + i, True)
                    body(first + (STEPS - 1), False)
                    for u in range(U):
                        pool.wait_ge(scattered[u], w * (16 * STEPS) + 16 * STEPS)
                    pool.sem_inc(apart, 1)
                waves(pool, wave)

            @block.tensor
            def _(pe):
                def turn_x(n, u):
                    pe.wait_ge(gathered[u % B], 16 * uses(n, u) + 16)
                    pe.wait_ge(x_lo_ready, n * U + u)
                    for k in range(KT):
                        last = pe.transpose(ps_x[:, k, :], xg[:, u % B, k * P:(k + 1) * P], ident[:])
                    last.then_inc(x_turned[u % B], 1)

                def gate_up(n, u, half):
                    if half == FIRST:
                        pe.wait_ge(x_lo_ready, n * U + (u + 1))
                        pe.wait_ge(hid_ready[u % 2], n * (U // 2) + u // 2)
                    pe.wait_ge(piece_lo[half], n * U + (u + 1))
                    for k in range(half * HALF, (half + 1) * HALF):
                        for j, (a, w) in enumerate(((x_hi, gu_hi), (x_hi, gu_lo), (x_lo, gu_hi))):
                            last = pe.matmul(ps_h[:, u % 2, :], a[:, u % 2, k, :], w[:, k, :],
                                             start=(k == 0 and j == 0), stop=(k == KT - 1 and j == 2))
                    last.then_inc(piece_used[half], 1)

                def turn_h(n, u):
                    pe.wait_ge(hid_ready[u % 2], n * (U // 2) + (u // 2 + 1))
                    pe.wait_ge(h_lo_ready, n * U + u)
                    for k in range(DE // P):
                        last = pe.transpose(ps_t[:, u % 2, k * P:(k + 1) * P], hid[:, u % 2, k * P:(k + 1) * P], ident[:])
                    last.then_inc(h_turned, 1)

                def down(n, u):
                    pe.wait_ge(h_lo_ready, n * U + (u + 1))
                    pe.wait_ge(piece_lo[DOWN], n * U + (u + 1))
                    pe.wait_ge(y_out, n * U + u)
                    for half in range(D // COLS):
                        at = slice(half * COLS, (half + 1) * COLS)
                        for k in range(DE // P):
                            for j, (a, w) in enumerate(((h_hi, d_hi), (h_hi, d_lo), (h_lo, d_hi))):
                                last = pe.matmul(ps_y[:, at], a[:, u % 2, k, :], w[:, k, at],
                                                 start=(k == 0 and j == 0), stop=(k == DE // P - 1 and j == 2))
                    last.then_inc(piece_used[DOWN], 1)

                def start(n):
                    turn_x(n, 0)
                    gate_up(n, 0, FIRST)
                    gate_up(n, 0, SECOND)
                    turn_x(n, 1)

                def step(this, last, following):
                    gate_up(*this, FIRST)
                    turn_h(*last)
                    gate_up(*this, SECOND)
                    if following:
                        turn_x(*following)
                    down(*last)

                def end(last):
                    turn_h(*last)
                    down(*last)
                rounds(pe, start, step, end)

            @block.scalar
            def _(act):
                def high(n, u, piece):
                    if piece == FIRST:
                        act.wait_ge(gu_loaded[u % B], 32 * uses(n, u) + 32)
                    if piece == DOWN:
                        act.wait_ge(down_loaded[u % B], 16 * uses(n, u) + 16)
                    act.wait_ge(piece_used[piece], n * U + u)
                    hi, _, raw = pieces[piece]
                    act.activation(hi, raw(u % B), ACT.Copy).then_inc(piece_hi[piece], 1)

                def tokens(n, u):
                    act.wait_ge(x_turned[u % B], uses(n, u) + 1)
                    act.activation(x_hi[:, u % 2, :, :], ps_x[:], ACT.Copy).then_inc(x_hi_ready, 1)

                def gate(n, u):
                    act.wait_ge(piece_used[SECOND], n * U + (u + 1))
                    act.wait_ge(hid_ready[u % 2], n * (U // 2) + u // 2)
                    act.activation(silu[:, u % 2, :], ps_h[:, u % 2, 0:DE], ACT.Silu).then_inc(silu_ready, 1)

                def hidden(n, u):
                    act.wait_ge(h_turned, n * U + (u + 1))
                    act.wait_ge(piece_used[DOWN], n * U + (u - 1) if u else n * U)
                    act.activation(h_hi[:, u % 2, :, :], ps_t[:, u % 2, :], ACT.Copy).then_inc(h_hi_ready, 1)

                def rows_out(n, u):
                    act.wait_ge(piece_used[DOWN], n * U + (u + 1))
                    act.wait_ge(scattered[(u - 2) % U], 16 * (n + (u >= 2)))
                    act.activation(y[:, u % 2, :], ps_y[:], ACT.Copy).then_inc(y_out, 1)

                def start(n):
                    for piece in range(3):
                        high(n, 0, piece)
                    tokens(n, 0)
                    high(n, 1, FIRST)
                    gate(n, 0)
                    tokens(n, 1)
                    high(n, 1, SECOND)

                def step(this, last, following):
                    hidden(*last)
                    if following:
                        high(*following, FIRST)
                    gate(*this)
                    if following:
                        tokens(*following)
                        high(*following, SECOND)
                    rows_out(*last)
                    high(*this, DOWN)

                def end(last):
                    hidden(*last)
                    rows_out(*last)
                rounds(act, start, step, end)

            @block.vector
            def _(dve):
                def low(n, u, piece):
                    dve.wait_ge(piece_hi[piece], n * U + (u + 1))
                    hi, lo, raw = pieces[piece]
                    dve.tensor_tensor(lo, raw(u % B), hi.bitcast(F32), ALU.subtract).then_inc(piece_lo[piece], 1)

                def tokens(n, u):
                    dve.wait_ge(x_hi_ready, n * U + (u + 1))
                    dve.tensor_tensor(x_lo[:, u % 2, :, :], ps_x[:], x_hi[:, u % 2, :, :].bitcast(F32), ALU.subtract
                                      ).then_inc(x_lo_ready, 1)

                def product(n, u):
                    dve.wait_ge(silu_ready, n * U + (u + 1))
                    dve.tensor_tensor(hid[:, u % 2, :], silu[:, u % 2, :], ps_h[:, u % 2, DE:2 * DE], ALU.mult
                                      ).then_inc(hid_ready[u % 2], 1)

                def hidden(n, u):
                    dve.wait_ge(h_hi_ready, n * U + (u + 1))
                    dve.tensor_tensor(h_lo[:, u % 2, :, :], ps_t[:, u % 2, :].rearrange("p (k n) -> p k n", k=DE // P),
                                      h_hi[:, u % 2, :, :].bitcast(F32), ALU.subtract).then_inc(h_lo_ready, 1)

                def start(n):
                    for piece in range(3):
                        low(n, 0, piece)
                    tokens(n, 0)
                    low(n, 1, FIRST)
                    product(n, 0)
                    tokens(n, 1)
                    low(n, 1, SECOND)

                def step(this, last, following):
                    hidden(*last)
                    if following:
                        low(*following, FIRST)
                    product(*this)
                    if following:
                        tokens(*following)
                        low(*following, SECOND)
                    low(*this, DOWN)
                rounds(dve, start, step, lambda last: hidden(*last))


def constants(nc, cst, block):
    @block.gpsimd
    def _(pool):
        pool.memset(cst.ident[:], 0.0)
        pool.memset(cst.ones[:], 1.0)
        pool.iota(cst.iota_i[:], pattern=[[1, 64]], base=0, channel_multiplier=0)
        pool.drain()
        pool.affine_select(out=cst.ident[:], in_=cst.ident[:], compare_op=ALU.not_equal, fill=1.0, base=0,
                           pattern=[[-1, P]], channel_multiplier=1)
        pool.affine_select(out=cst.before[:], in_=cst.ones[:], compare_op=ALU.is_gt, fill=0.0, base=0,
                           pattern=[[1, P]], channel_multiplier=-1)
        pool.tensor_copy(cst.iota[:], cst.iota_i[:])
        pool.drain()


def gated_conv(nc, name, xT_hi, xT_lo, w, conv_w, conv_b, zT_hi, zT_lo, ahead):
    PARTS = (1, 2, 0)
    with Pool_(nc, name) as m:
        raw = m.sb("raw", [P, 3, KT, P])
        w_hi = m.sb("w_hi", [P, 3, KT, P], F32R)
        w_lo = m.sb("w_lo", [P, 3, KT, P], F32R)
        taps = m.sb("taps", [P, KT, 3])
        bias = m.sb("bias", [P, KT])
        c_sb = m.sb("c_sb", [P, S])
        u_sb = m.sb("u_sb", [P, S + 2])
        y_sb = m.sb("y_sb", [P, S])
        z_sb = m.sb("z_sb", [P, S])
        ps = m.ps("ps", [P, 3, S])
        raw_loaded, hi_ready, lo_ready = m.sems("raw_loaded", 3), m.sems("hi_ready", 3), m.sems("lo_ready", 3)
        product, taps_loaded = m.sems("product", 3), m.sem("taps_loaded")
        apart = m.sem("apart")
        c_out, u_ready, z_ready, z_hi, z_lo = (m.sem(n) for n in ("c_out", "u_ready", "z_ready", "z_hi", "z_lo"))
        w_k = w.rearrange("(k p) n -> p k n", p=P)

        with nc.Block() as block:
            @block.sync
            def _(sp):
                for j in range(3):
                    sp.dma_start(taps[:, :, j], conv_w[j, :].rearrange("(c p) -> p c", p=P),
                                 allow_slow_non_contiguous=True).then_inc(taps_loaded, 16)
                sp.dma_start(bias[:], conv_b.rearrange("(c p) -> p c", p=P),
                                 allow_slow_non_contiguous=True).then_inc(taps_loaded, 16)
                with sp.Fori(0, KT) as i:
                    for j in range(3):
                        col = sp.snap(i * P + PARTS[j] * D)
                        sp.wait_ge(lo_ready[j], i)
                        sp.sem_inc(apart, 1)
                        sp.dma_start(raw[:, j, :, :], w_k[:, :, ds(col, P)]).then_inc(raw_loaded[j], 16)
                ahead.load(sp)

            @block.scalar
            def _(act):
                def high(i, j):
                    act.wait_ge(raw_loaded[j], 16 * i + 16)
                    act.wait_ge(product[j], i)
                    act.activation(w_hi[:, j, :, :], raw[:, j, :, :], ACT.Copy).then_inc(hi_ready[j], 1)

                def body(i, more):
                    for j in (1, 2):
                        high(i, j)
                    act.wait_ge(product[0], i + 1)
                    act.wait_ge(u_ready, i)
                    act.activation(c_sb[:], ps[:, 0, :], ACT.Copy).then_inc(c_out, 1)
                    if more:
                        high(i + 1, 0)
                    act.wait_ge(z_ready, i + 1)
                    act.activation(zT_hi[:, ds(i, 1), :], z_sb[:].unsqueeze(1), ACT.Copy).then_inc(z_hi, 1)

                high(0, 0)
                with act.Fori(0, KT - 1) as i:
                    body(i, True)
                body(KT - 1, False)

            @block.vector
            def _(dve):
                def low(i, j):
                    dve.wait_ge(hi_ready[j], i + 1)
                    dve.tensor_tensor(w_lo[:, j, :, :], raw[:, j, :, :], w_hi[:, j, :, :].bitcast(F32),
                                      ALU.subtract).then_inc(lo_ready[j], 1)

                def body(i, more):
                    for j in (1, 2):
                        low(i, j)
                    dve.wait_ge(c_out, i + 1)
                    dve.wait_ge(product[1], i + 1)
                    dve.tensor_tensor(u_sb[:, 2:S + 2], c_sb[:], ps[:, 1, :], ALU.mult).then_inc(u_ready, 1)
                    dve.drain()
                    dve.tensor_scalar(y_sb[:], u_sb[:, 2:S + 2], taps[:, ds(i, 1), 2], bias[:, ds(i, 1)], ALU.mult, ALU.add)
                    dve.drain()
                    for j in (1, 0):
                        dve.scalar_tensor_tensor(y_sb[:], u_sb[:, j:S + j], taps[:, ds(i, 1), j], y_sb[:], ALU.mult, ALU.add)
                        dve.drain()
                    if more:
                        low(i + 1, 0)
                    dve.wait_ge(product[2], i + 1)
                    dve.wait_ge(z_hi, i)
                    dve.tensor_tensor(z_sb[:], y_sb[:], ps[:, 2, :], ALU.mult).then_inc(z_ready, 1)
                    dve.wait_ge(z_hi, i + 1)
                    dve.tensor_tensor(zT_lo[:, ds(i, 1), :], z_sb[:].unsqueeze(1), zT_hi[:, ds(i, 1), :].bitcast(F32),
                                      ALU.subtract).then_inc(z_lo, 1)

                dve.memset(u_sb[:, 0:2], 0.0)
                low(0, 0)
                dve.wait_ge(taps_loaded, 64)
                with dve.Fori(0, KT - 1) as i:
                    body(i, True)
                body(KT - 1, False)

            @block.tensor
            def _(pe):
                with pe.Fori(0, KT) as i:
                    for j in range(3):
                        pe.wait_ge(lo_ready[j], i + 1)
                        pe.wait_ge((c_out, u_ready, z_ready)[j], i)
                        for half in range(S // COLS):
                            at = slice(half * COLS, (half + 1) * COLS)
                            for k in range(KT):
                                for q, (w_part, x_part) in enumerate(((w_hi, xT_hi), (w_hi, xT_lo), (w_lo, xT_hi))):
                                    last = pe.matmul(ps[:, j, at], w_part[:, j, k, :], x_part[:, k, at],
                                                     start=(k == 0 and q == 0), stop=(k == KT - 1 and q == 2))
                        last.then_inc(product[j], 1)


def shape_constants():
    f = np.float32
    con = {}
    log_g = np.log(f(1) - f(2) ** (f(-5) - np.arange(RH, dtype=f)))
    pos = np.arange(P, dtype=f)
    diff = pos[:, None] - pos[None, :]
    dec = np.where(diff >= 0, np.exp(log_g[:, None, None] * np.maximum(diff, 0)), 0) * f(HD ** -0.5)
    by = [[2 * b + a for b in range(RH // 2)] for a in range(2)]
    con["decay"] = dec.transpose(0, 2, 1)[by].transpose(2, 0, 1, 3).reshape(P, -1)
    q_dec = np.exp(log_g[:, None] * (pos + 1))
    con["q_decay"] = np.repeat(q_dec[by], HD, axis=0).reshape(P, -1)
    con["k_decay"] = (np.exp(log_g[:, None] * (P - 1 - pos)) * f(HD ** -0.5)).T
    con["c_decay"] = np.repeat(np.exp(log_g * P)[by], HD, axis=0)
    return {k: np.ascontiguousarray(v, dtype=f) for k, v in con.items()}

QR = HD + NS + 1


def retention_and_rows(nc, name, proj, ret_gain, q_gain, k_gains, cst, con, keep, y_out):
    PAIRS = RH // 2
    NK = 2 * G
    ROUND = 4
    ROUNDS = (NH + NK) // ROUND
    C_GATE = 3 * RET_W
    with Pool_(nc, name) as m:
        decay = m.sb("decay", [P, 2, PAIRS, P])
        q_decay = m.sb("q_decay", [P, PAIRS, P])
        k_decay = m.sb("k_decay", [P, RH])
        c_decay = m.sb("c_decay", [P, PAIRS])
        ret_gains = m.sb("ret_gains", [P, HD])
        gains = m.sb("gains", [P, 3, HD])
        qkv = m.sb("qkv", [P, 2, 3 * RET_W])
        nq = m.sb("nq", [P, 2, NSA_W])
        kv = m.sb("kv", [P, NT, 2 * KV_W])
        gate = m.sb("gate", [P, NT, RET_W])
        qkT = m.sb("qkT", [P, 2, 2, PAIRS, P])
        qdT = m.sb("qdT", [P, PAIRS, P])
        kd = m.sb("kd", [P, RET_W])
        scores = m.sb("scores", [P, 2, PAIRS, P])
        state = m.sb("state", [P, PAIRS, HD])
        y = m.sb("y", [P, 2, RET_W])
        y_sq = m.sb("y_sq", [P, RET_W])
        y_ssq, y_root, y_r = (m.sb(n, [P, RH]) for n in ("y_ssq", "y_root", "y_r"))
        n_sq = m.sb("n_sq", [P, NSA_W + 2 * KV_W])
        n_ssq, n_root, n_r = (m.sb(n, [P, NH + NK]) for n in ("n_ssq", "n_root", "n_r"))
        qa = m.sb("qa", [P, 2, NH, QR])
        ka = m.sb("ka", [P, 2, NK, HD])
        q_rows = m.sb("q_rows", [P, NT, NH, NS + 1])
        kvc = m.sb("kvc", [P, 2, NT, KV_W])
        masks_f = m.sb("masks_f", [P, 2 * P + NT * NC_])
        picks_f = m.sb("picks_f", [G * NS, G * S])
        eps = m.sb("eps", [P, 1])
        ps_t = m.ps("ps_t", [P, 2, PAIRS, P])
        ps_s = m.ps("ps_s", [P, 2, PAIRS, P])
        ps_y = m.ps("ps_y", [P, 2, COLS])
        ps_kv = m.ps("ps_kv", [P, 2 * PAIRS, HD])
        ps_n = m.ps("ps_n", [P, ROUND, P])
        const_loaded, rows_loaded, gate_loaded = m.sem("const_loaded"), m.sems("rows_loaded"), m.sem("gate_loaded")
        keys_loaded, pool_loaded, rest_loaded = m.sem("keys_loaded"), m.sem("pool_loaded"), m.sem("rest_loaded")
        turned, T_ready, qd_ready, kd_ready = (m.sem(n) for n in ("turned", "T_ready", "qd_ready", "kd_ready"))
        scored, decayed, y_taken = (m.sem(n) for n in ("scored", "decayed", "y_taken"))
        y_ready = m.sems("y_ready")
        kv_ready, state_ready, eps_ready = m.sem("kv_ready"), m.sem("state_ready"), m.sem("eps_ready")
        y_summed, y_rooted, silus, gated = (m.sem(n) for n in ("y_summed", "y_rooted", "silus", "gated"))
        y_done, stored = m.sem("y_done"), m.sems("stored")
        n_squared, n_summed, n_rooted, rows_added, n_ready = (
            m.sem(n) for n in ("n_squared", "n_summed", "n_rooted", "rows_added", "n_ready"))
        n_turned, n_taken = m.sem("n_turned"), m.sem("n_taken")
        apart = m.sem("apart")
        tiled = proj.rearrange("(t p) n -> p t n", p=P)

        def chunks(eng, body):
            with eng.Fori(0, NT // 2 - 1) as i:
                for u in range(2):
                    body(i, u, True)
            for u in range(2):
                body(NT // 2 - 1, u, u == 0)

        with nc.Block() as block:
            @block.sync
            def _(sp):
                for c in range(2):
                    sp.dma_start(qkv[:, c, :], proj[c * P:(c + 1) * P, 0:C_GATE]).then_inc(rows_loaded[c], 16)
                    sp.dma_start(nq[:, c, :], proj[c * P:(c + 1) * P, C_NQ:C_KC]).then_inc(rows_loaded[c], 16)
                    if c == 0:
                        for j, (a, b) in enumerate(((C_KS, C_VS), (C_KW, C_VW))):
                            sp.dma_start(kv[:, :, j * KV_W:(j + 1) * KV_W], tiled[:, :, a:b]).then_inc(keys_loaded, 16)
                        sp.dma_start(gains[:, 0, :], row_of(q_gain)).then_inc(keys_loaded, 16)
                        sp.dma_start(gains[:, 1:3, :], row_of(k_gains[1:3, :])).then_inc(keys_loaded, 16)
                        sp.dma_start(q_rows[:], con["q_rows"].rearrange("p (t h j) -> p t h j", t=NT, h=NH)
                                     ).then_inc(keys_loaded, 16)
                        for dst, src in ((decay[:], con["decay"].rearrange("p (a b c) -> p a b c", a=2, b=PAIRS)),
                                         (q_decay[:], con["q_decay"].rearrange("p (a b) -> p a b", a=PAIRS)),
                                         (k_decay[:], con["k_decay"]), (c_decay[:], con["c_decay"]),
                                         (ret_gains[:], row_of(ret_gain))):
                            sp.dma_start(dst, src).then_inc(const_loaded, 16)
                sp.dma_start(gate[:], tiled[:, :, C_GATE:C_NQ]).then_inc(gate_loaded, 16)
                for j, (a, b) in enumerate(((C_KC, C_VC), (C_VC, C_KS))):
                    sp.dma_start(kvc[:, j, :, :], tiled[:, :, a:b]).then_inc(pool_loaded, 16)
                sp.dma_start(masks_f[:], con["masks"]).then_inc(pool_loaded, 16)
                sp.dma_start(picks_f[:], con["picks"]).then_inc(pool_loaded, 16)
                for j, (a, b) in enumerate(((C_VS, C_KW), (C_VW, C_NG))):
                    sp.dma_start(keep.v[:, :, j, :], tiled[:, :, a:b]).then_inc(rest_loaded, 16)
                sp.dma_start(keep.gate[:], tiled[:, :, C_NG:IN_W]).then_inc(rest_loaded, 16)
                for g in range(G):
                    for b in range(2):
                        sp.dma_start(keep.kT[HD:QR, b, g, :], con["key_rows"]).then_inc(rest_loaded, 16)
                    sp.dma_start(keep.kcT[HD:QR, g, :], con["cmp_rows"]).then_inc(rest_loaded, 16)
                sp.dma_start(keep.forced[:], con["forced"].rearrange("p (t j) -> p t j", t=NT)).then_inc(rest_loaded, 16)

                def store(c, row, u):
                    sp.wait_ge(y_done, c + 1)
                    sp.dma_start(y_out[ds(row, P), 0:RET_W], y[:, u, :]).then_inc(stored[u], 16)

                with sp.Fori(0, NT // 2 - 1) as i:
                    for u in range(2):
                        here, ahead = sp.snap((2 * i + u) * P), sp.snap((2 * i + u + 2) * P)
                        sp.wait_ge(y_ready[u], i + 1)
                        sp.dma_start(qkv[:, u, :], proj[ds(ahead, P), 0:C_GATE]).then_inc(rows_loaded[u], 16)
                        sp.dma_start(nq[:, u, :], proj[ds(ahead, P), C_NQ:C_KC]).then_inc(rows_loaded[u], 16)
                        store(2 * i + u, here, u)
                for c in (NT - 2, NT - 1):
                    store(c, c * P, c % 2)
                for u in range(2):
                    sp.wait_ge(stored[u], 16 * (NT // 2))
                sp.wait_ge(rest_loaded, 16 * 10)

            @block.gpsimd
            def _(pool):
                pool.tensor_copy(keep.ident_b[:], cst.ident[:])
                pool.wait_ge(silus, 1)
                heads = gate[:].rearrange("p t (h d) -> p (t h) d", d=HD)
                pool.tensor_tensor(heads, heads, ret_gains[:].unsqueeze(1).to_broadcast([P, NT * RH, HD]), ALU.mult
                                   ).then_inc(gated, 1)
                pool.wait_ge(pool_loaded, 64)
                pool.tensor_copy(keep.masks[:], masks_f[:])
                pool.tensor_copy(keep.picks[:], picks_f[:])
                for j in range(2):
                    for a in range(2):
                        pool.tensor_copy(keep.kvc2[:, j, :, :, a, :], kvc[:, j, :, :].rearrange("p t (g d) -> p t g d", d=HD))
                pool.drain()

            @block.scalar
            def _(act):
                act.wait_ge(eps_ready, 1)
                act.wait_ge(keys_loaded, 16 * 5)

                def ahead(c, i, v):
                    act.wait_ge(rows_loaded[v], 32 * i + 32)
                    act.activation(n_sq[:, 0:NSA_W], nq[:, v, :], ACT.Square)
                    act.activation(n_sq[:, NSA_W:NSA_W + 2 * KV_W].unsqueeze(1), kv[:, ds(c, 1), :], ACT.Square
                                   ).then_inc(n_squared, 1)
                    act.wait_ge(turned, c + 1)
                    act.wait_ge(y_ready[v], i)
                    act.activation(qkT[:, v, :, :, :], ps_t[:], ACT.Copy).then_inc(T_ready, 1)
                    act.activation(qa[:, v, :, HD:QR].unsqueeze(1), q_rows[:, ds(c, 1), :, :], ACT.Copy
                                   ).then_inc(rows_added, 1)
                    act.wait_ge(n_summed, c + 1)
                    act.activation(n_root[:], n_ssq[:], ACT.Sqrt, bias=eps[:], scale=1.0 / HD).then_inc(n_rooted, 1)

                def take_queries(c):
                    act.wait_ge(n_turned, ROUNDS * c + 2)
                    act.activation(keep.qT[0:QR, ds(c * NH + ROUND, ROUND), :], ps_n[0:QR, :, :], ACT.Copy
                                   ).then_inc(n_taken, 1)

                def take_keys(c):
                    act.wait_ge(n_turned, ROUNDS * c + 3)
                    act.activation(keep.kT[0:HD, :, :, ds(c * P, P)],
                                   ps_n[0:HD, :, :].rearrange("p (b g) n -> p b g n", b=2), ACT.Copy).then_inc(n_taken, 1)

                def body(i, u, more):
                    c = 2 * i + u
                    if more:
                        ahead(c + 1, i + u, 1 - u)
                    take_queries(c)
                    act.wait_ge(y_ready[u], i + 1)
                    act.wait_ge(stored[u], 16 * i)
                    halves = ps_y[:, :, 0:PAIRS * HD].rearrange("p a (b d) -> p a b d", d=HD)
                    act.activation(y_sq[:].rearrange("p (b a d) -> p a b d", a=2, d=HD), halves, ACT.Square)
                    act.activation(y[:, u, :].rearrange("p (b a d) -> p a b d", a=2, d=HD), halves, ACT.Copy
                                   ).then_inc(y_taken, 1)
                    take_keys(c)
                    act.wait_ge(y_summed, c + 1)
                    act.activation(y_root[:], y_ssq[:], ACT.Sqrt, bias=eps[:], scale=1.0 / HD).then_inc(y_rooted, 1)

                ahead(0, 0, 0)
                act.wait_ge(gate_loaded, 16)
                act.wait_ge(const_loaded, 16 * 5)
                act.activation(gate[:], gate[:], ACT.Silu).then_inc(silus, 1)
                chunks(act, body)

            @block.vector
            def _(dve):
                dve.memset(eps[:], EPS).then_inc(eps_ready, 1)
                dve.memset(state[:], 0.0).then_inc(state_ready, 1)
                dve.wait_ge(keys_loaded, 16 * 5)

                def sums(c):
                    dve.wait_ge(n_squared, c + 1)
                    dve.tensor_reduce(n_ssq[:], n_sq[:].rearrange("p (h d) -> p h d", d=HD), X, ALU.add).then_inc(n_summed, 1)

                def apply(c, v):
                    dve.wait_ge(n_rooted, c + 1)
                    dve.reciprocal(n_r[:], n_root[:])
                    dve.drain()
                    dve.tensor_scalar(n_r[:, 0:NH], n_r[:, 0:NH], HD ** -0.5, None, ALU.mult)
                    dve.drain()
                    q = qa[:, v, :, 0:HD]
                    dve.wait_ge(rows_added, c + 1)
                    dve.tensor_tensor(q, nq[:, v, :].rearrange("p (h d) -> p h d", d=HD),
                                      n_r[:, 0:NH].unsqueeze(2).to_broadcast([P, NH, HD]), ALU.mult)
                    dve.tensor_tensor(ka[:, v, :, :].unsqueeze(1),
                                      kv[:, ds(c, 1), :].rearrange("p t (h d) -> p t h d", d=HD),
                                      n_r[:, NH:NH + NK].unsqueeze(1).unsqueeze(3).to_broadcast([P, 1, NK, HD]), ALU.mult)
                    dve.drain()
                    dve.tensor_tensor(q, q, gains[:, 0, :].unsqueeze(1).to_broadcast([P, NH, HD]), ALU.mult)
                    k4 = ka[:, v, :, :].rearrange("p (b g) d -> p b g d", b=2)
                    dve.tensor_tensor(k4, k4, gains[:, 1:3, :].unsqueeze(2).to_broadcast([P, 2, G, HD]), ALU.mult
                                      ).then_inc(n_ready, 1)

                def body(i, u, more):
                    c = 2 * i + u
                    dve.wait_ge(rows_loaded[u], 32 * i + 32)
                    dve.wait_ge(kv_ready, c)
                    dve.tensor_tensor(kd[:].rearrange("p (h d) -> p h d", d=HD),
                                      qkv[:, u, RET_W:2 * RET_W].rearrange("p (h d) -> p h d", d=HD),
                                      k_decay[:].unsqueeze(2).to_broadcast([P, RH, HD]), ALU.mult).then_inc(kd_ready, 1)
                    dve.wait_ge(T_ready, c + 1)
                    dve.wait_ge(y_ready[1 - u], i + u)
                    dve.tensor_tensor(qdT[:], qkT[:, u, 0, :, :], q_decay[:], ALU.mult).then_inc(qd_ready, 1)
                    dve.wait_ge(scored, c + 1)
                    dve.tensor_tensor(scores[:], ps_s[:], decay[:], ALU.mult).then_inc(decayed, 1)
                    if more:
                        sums(c + 1)
                    dve.wait_ge(n_turned, ROUNDS * c + 1)
                    dve.tensor_copy(keep.qT[0:QR, ds(c * NH, ROUND), :], ps_n[0:QR, :, :]).then_inc(n_taken, 1)
                    if more:
                        apply(c + 1, 1 - u)
                    dve.wait_ge(kv_ready, c + 1)
                    dve.wait_ge(y_ready[u], i + 1)
                    dve.tensor_tensor(state[:], state[:], c_decay[:].unsqueeze(2).to_broadcast([P, PAIRS, HD]), ALU.mult)
                    dve.drain()
                    dve.tensor_tensor(state[:], state[:], ps_kv[:, 0:PAIRS, :], ALU.add).then_inc(state_ready, 1)
                    dve.wait_ge(y_taken, c + 1)
                    dve.tensor_reduce(y_ssq[:], y_sq[:].rearrange("p (h d) -> p h d", d=HD), X, ALU.add
                                      ).then_inc(y_summed, 1)
                    dve.wait_ge(y_rooted, c + 1)
                    dve.reciprocal(y_r[:], y_root[:])
                    dve.drain()
                    y_h = y[:, u, :].rearrange("p (h d) -> p h d", d=HD)
                    dve.tensor_tensor(y_h, y_h, y_r[:].unsqueeze(2).to_broadcast([P, RH, HD]), ALU.mult)
                    dve.drain()
                    dve.wait_ge(gated, 1)
                    dve.tensor_tensor(y[:, u, :].unsqueeze(1), y[:, u, :].unsqueeze(1), gate[:, ds(c, 1), :], ALU.mult
                                      ).then_inc(y_done, 1)

                sums(0)
                apply(0, 0)
                dve.wait_ge(const_loaded, 16 * 5)
                chunks(dve, body)

            @block.tensor
            def _(pe):
                def turn(c, i, v):
                    pe.wait_ge(rows_loaded[v], 32 * i + 32)
                    pe.wait_ge(T_ready, c)
                    for a in range(2):
                        for b in range(PAIRS):
                            last = pe.transpose(ps_t[:, a, b, :], qkv[:, v, a * RET_W + b * P:a * RET_W + (b + 1) * P],
                                                cst.ident[:])
                    last.then_inc(turned, 1)

                def rows(c, u, r):
                    pe.wait_ge(n_taken, ROUNDS * c + r)
                    if r == 0:
                        pe.wait_ge(n_ready, c + 1)
                    if r == ROUNDS - 1:
                        pe.sem_inc(apart, 1)
                    for j in range(ROUND):
                        h = r * ROUND + j
                        if h < NH:
                            last = pe.transpose(ps_n[0:QR, j, :], qa[:, u, h, :], cst.ident[:])
                        else:
                            last = pe.transpose(ps_n[0:HD, j, :], ka[:, u, h - NH, :], cst.ident[:])
                    last.then_inc(n_turned, 1)

                def body(i, u, more):
                    c = 2 * i + u
                    pe.wait_ge(T_ready, c + 1)
                    pe.wait_ge(decayed, c)
                    for a in range(2):
                        at = slice(a * HD, (a + 1) * HD)
                        for b in range(PAIRS):
                            last = pe.matmul(ps_s[:, a, b, :], qkT[at, u, 1, b, :], qkT[at, u, 0, b, :], start=True, stop=True)
                    last.then_inc(scored, 1)
                    if more:
                        turn(c + 1, i + u, 1 - u)
                    rows(c, u, 0)
                    pe.wait_ge(kd_ready, c + 1)
                    pe.wait_ge(state_ready, c + 1)
                    for a in range(2):
                        for b in range(PAIRS):
                            h = 2 * b + a
                            last = pe.matmul(ps_kv[a * HD:(a + 1) * HD, b, :], kd[:, h * HD:(h + 1) * HD],
                                             qkv[:, u, 2 * RET_W + h * HD:2 * RET_W + (h + 1) * HD], start=True, stop=True)
                    last.then_inc(kv_ready, 1)
                    rows(c, u, 1)
                    pe.wait_ge(qd_ready, c + 1)
                    pe.wait_ge(y_taken, c)
                    pe.wait_ge(decayed, c + 1)
                    for a in range(2):
                        at = slice(a * HD, (a + 1) * HD)
                        for b in range(PAIRS):
                            h = 2 * b + a
                            pe.matmul(ps_y[:, a, b * HD:(b + 1) * HD], scores[:, a, b, :],
                                      qkv[:, u, 2 * RET_W + h * HD:2 * RET_W + (h + 1) * HD], start=True, stop=False)
                            last = pe.matmul(ps_y[:, a, b * HD:(b + 1) * HD], qdT[at, b, :], state[at, b, :],
                                             start=False, stop=True)
                    last.then_inc(y_ready[u], 1)
                    rows(c, u, 2)

                turn(0, 0, 0)
                chunks(pe, body)


def sparse_prepare(nc, name, k_gains, pe, w1, w2, cst, keep):
    with Pool_(nc, name) as m:
        eps = m.sb("eps", [P, 1])
        with Pool_(nc, name + "C") as s:
            L = CMP_STRIDE
            xb = s.sb("xb", [P, 2, L, G, NC_])
            gains = s.sb("gains", [P, HD])
            peT = s.sb("peT", [P, 2, L])
            w1s = s.sb("w1s", [P, 2, L, CMP_HID])
            w2s = s.sb("w2s", [P, 2, HD])
            hid = s.sb("hid", [P, 2, G, 2, NC_])
            kc = s.sb("kc", [NC_, G, HD])
            ksq = s.sb("ksq", [NC_, G, HD])
            kss = s.sb("kss", [NC_, G])
            ps_x = s.ps("ps_x", [P, G, S])
            ps_h = s.ps("ps_h", [P, 2, COLS])
            ps_k = s.ps("ps_k", [P, G, HD])
            ps_t = s.ps("ps_t", [HD, G, NC_])
            pe_loaded = s.sem("pe_loaded")
            w_loaded, x_turned, xb_ready, h_done, hid_ready = (
                s.sem(n) for n in ("w_loaded", "x_turned", "xb_ready", "h_done", "hid_ready"))
            k_done, k_sq, k_sum, k_root, k_ready, k_turned, v_done = (
                s.sem(n) for n in ("k_done", "k_sq", "k_sum", "k_root", "k_ready", "k_turned", "v_done"))

            with nc.Block() as block:
                @block.sync
                def _(sp):
                    for j in range(2):
                        for a in range(2):
                            rows = slice(a * HD, (a + 1) * HD)
                            sp.dma_start(peT[rows, j, :], pe[j, a * L:(a + 1) * L, :].rearrange("l d -> d l"),
                                         allow_slow_non_contiguous=True).then_inc(pe_loaded, 16)
                    for j in range(2):
                        for a in range(2):
                            rows = slice(a * HD, (a + 1) * HD)
                            sp.dma_start(w1s[rows, j, :, :],
                                         w1[j, a * L * HD:(a + 1) * L * HD, :].rearrange("(l d) n -> d l n", d=HD)
                                         ).then_inc(w_loaded, 16)
                    sp.dma_start(w2s[:], w2.rearrange("j p d -> p j d")).then_inc(w_loaded, 16)
                    sp.dma_start(gains[:], row_of(k_gains[0, :])).then_inc(w_loaded, 16)

                @block.tensor
                def _(pe_):
                    for j in range(2):
                        if j:
                            pe_.wait_ge(xb_ready, 1)
                        for g in range(G):
                            for t in range(NT):
                                last = pe_.transpose(ps_x[:, g, t * P:(t + 1) * P],
                                                     keep.kvc2[:, j, t, g, :, :].rearrange("p a d -> p (a d)"), cst.ident[:])
                        last.then_inc(x_turned, 1)
                    pe_.wait_ge(w_loaded, 16 * 6)
                    for j in range(2):
                        pe_.wait_ge(xb_ready, j + 1)
                        for l in range(L):
                            last = pe_.matmul(ps_h[:, j, 0:G * NC_].rearrange("p (g n) -> p g n", g=G), w1s[:, j, l, :],
                                              xb[:, j, l, :, :], start=(l == 0), stop=(l == L - 1))
                        last.then_inc(h_done, 1)
                    pe_.wait_ge(hid_ready, 1)
                    for g in range(G):
                        last = pe_.matmul(ps_k[0:NC_, g, :], hid[:, 0, g, 0, :], w2s[:, 0, :], start=True, stop=True)
                    last.then_inc(k_done, 1)
                    pe_.wait_ge(k_ready, 1)
                    for g in range(G):
                        last = pe_.transpose(ps_t[:, g, :], kc[:, g, :], cst.ident[0:NC_, 0:NC_])
                    last.then_inc(k_turned, 1)
                    pe_.wait_ge(hid_ready, 2)
                    for g in range(G):
                        last = pe_.matmul(ps_k[:, g, :], hid[:, 1, g, :, :].rearrange("p a n -> p (a n)"), w2s[:, 1, :],
                                          start=True, stop=True)
                    last.then_inc(v_done, 1)

                @block.scalar
                def _(act):
                    for j in range(2):
                        act.wait_ge(h_done, j + 1)
                        act.activation(hid[:, j, :, :, :],
                                       ps_h[:, j, 0:G * NC_].rearrange("p (g n) -> p g n", g=G).unsqueeze(2).to_broadcast([P, G, 2, NC_]),
                                       ACT.Gelu_apprx_tanh).then_inc(hid_ready, 1)
                    act.wait_ge(k_done, 1)
                    act.activation(ksq[:], ps_k[0:NC_, :, :], ACT.Square).then_inc(k_sq, 1)
                    act.wait_ge(k_sum, 1)
                    act.activation(kss[:], kss[:], ACT.Sqrt, bias=eps[0:NC_, :], scale=1.0 / HD).then_inc(k_root, 1)

                @block.vector
                def _(dve):
                    dve.memset(eps[:], EPS)
                    dve.memset(xb[:], 0.0)
                    dve.memset(keep.v_cmp[:], 0.0)
                    dve.drain()
                    dve.wait_ge(pe_loaded, 16 * 4)
                    for j in range(2):
                        dve.wait_ge(x_turned, j + 1)
                        for a in range(2):
                            rows, n = slice(a * HD, (a + 1) * HD), NC_ - a
                            for g in range(G):
                                last = dve.tensor_tensor(
                                    xb[rows, j, :, g, 0:n],
                                    ps_x[rows, g, a * L:S].rearrange("p (n l) -> p l n", l=L),
                                    peT[rows, j, :].unsqueeze(2).to_broadcast([HD, L, n]), ALU.add)
                        last.then_inc(xb_ready, 1)
                    dve.wait_ge(k_sq, 1)
                    dve.tensor_reduce(kss[:], ksq[:], X, ALU.add).then_inc(k_sum, 1)
                    dve.wait_ge(k_root, 1)
                    dve.reciprocal(kss[:], kss[:])
                    dve.drain()
                    dve.tensor_tensor(kc[:], ps_k[0:NC_, :, :], kss[:].unsqueeze(2).to_broadcast([NC_, G, HD]), ALU.mult)
                    dve.drain()
                    dve.wait_ge(w_loaded, 16 * 6)
                    dve.tensor_tensor(kc[:], kc[:], gains[0:NC_, :].unsqueeze(1).to_broadcast([NC_, G, HD]), ALU.mult
                                      ).then_inc(k_ready, 1)
                    dve.wait_ge(k_turned, 1)
                    dve.tensor_copy(keep.kcT[0:HD, :, :], ps_t[:])
                    dve.wait_ge(v_done, 1)
                    for a in range(2):
                        rows = slice(a * HD, (a + 1) * HD)
                        dve.tensor_copy(keep.v_cmp[rows, :, a * HD:(a + 1) * HD], ps_k[rows, :, :])
                    dve.drain()

    with Pool_(nc, name + "S") as s:
        BATCHES = 4
        BATCH = NT // BATCHES
        pc = s.sb("pc", [P, NT, NH, NC_])
        mx = s.sb("mx", [P, NT * NH])
        hs = s.sb("hs", [P, NT, G, NC_])
        imp = s.sb("imp", [P, NT, G, NS])
        best = s.sb("best", [P, NT * G, 8])
        left = s.sb("left", [P, NT * G, NS])
        bias_q = s.sb("bias_q", [P, NT, G * NS], BF16)
        scored, shifted, exped, prob_ready, picked = (
            s.sem(n) for n in ("scored", "shifted", "exped", "prob_ready", "picked"))
        with Pool_(nc, name + "S1") as b1:
            ps = b1.ps("ps", [P, NT, NH, NC_])
            with nc.Block() as block:
                @block.tensor
                def _(pe_):
                    for t in range(NT):
                        c_mask = keep.masks[:, 2 * P + t * NC_:2 * P + (t + 1) * NC_]
                        pe_.matmul(ps[:, t, :, :], keep.ident_b[:], c_mask.unsqueeze(1).to_broadcast([P, NH, NC_]),
                                   start=True, stop=False, skip_group_check=True)
                        for h in range(NH):
                            last = pe_.matmul(ps[:, t, h, :], keep.qT[0:QR, t * NH + h, :], keep.kcT[0:QR, h // R, :],
                                              start=False, stop=True, skip_group_check=True)
                        if t % BATCH == BATCH - 1:
                            last.then_inc(scored, 1)

                @block.scalar
                def _(act):
                    for b in range(BATCHES):
                        at = slice(b * BATCH, (b + 1) * BATCH)
                        act.wait_ge(shifted, b + 1)
                        act.activation(pc[:, at, :, :], pc[:, at, :, :], ACT.Exp).then_inc(exped, 1)

                @block.vector
                def _(dve):
                    n = BATCH * NH

                    def shift(b):
                        at = slice(b * BATCH, (b + 1) * BATCH)
                        m_b = mx[:, b * n:(b + 1) * n]
                        src = ps[:, at, :, :].rearrange("p t h n -> p (t h) n")
                        dve.wait_ge(scored, b + 1)
                        dve.tensor_reduce(m_b, src, X, ALU.max)
                        dve.drain()
                        dve.tensor_scalar(m_b, m_b, -1e20, None, ALU.max)
                        dve.drain()
                        dve.tensor_tensor(pc[:, at, :, :].rearrange("p t h n -> p (t h) n"), src,
                                          m_b.unsqueeze(2).to_broadcast([P, n, NC_]), ALU.subtract).then_inc(shifted, 1)

                    def select(b):
                        at = slice(b * BATCH, (b + 1) * BATCH)
                        m_b = mx[:, b * n:(b + 1) * n]
                        p_b = pc[:, at, :, :].rearrange("p t h n -> p (t h) n")
                        dve.wait_ge(exped, b + 1)
                        dve.tensor_reduce(m_b, p_b, X, ALU.add)
                        dve.drain()
                        dve.tensor_scalar(m_b, m_b, 1e-30, None, ALU.max)
                        dve.drain()
                        dve.reciprocal(m_b, m_b)
                        dve.drain()
                        dve.tensor_tensor(p_b, p_b, m_b.unsqueeze(2).to_broadcast([P, n, NC_]), ALU.mult
                                          ).then_inc(prob_ready, 1)
                        dve.drain()
                        dve.tensor_reduce(hs[:, at, :, :].rearrange("p t g n -> p (t g) n"),
                                          pc[:, at, :, :].rearrange("p t (g r) n -> p (t g) n r", g=G), X, ALU.add)
                        dve.drain()
                        h_b = hs[:, at, :, :].rearrange("p t g n -> p (t g) n")
                        i_b = imp[:, at, :, :].rearrange("p t g j -> p (t g) j")
                        dve.tensor_reduce(i_b, h_b.rearrange("p a (j i) -> p a j i", i=4), X, ALU.add)
                        dve.drain()
                        dve.tensor_tensor(i_b[:, :, 1:NS], i_b[:, :, 1:NS], h_b[:, :, 3:NC_ - 1:4], ALU.add)
                        dve.drain()
                        dve.tensor_tensor(imp[:, at, :, :], imp[:, at, :, :],
                                          keep.forced[:, at, :].unsqueeze(2).to_broadcast([P, BATCH, G, NS]), ALU.add)
                        dve.drain()
                        pairs = range(b * BATCH * G, (b + 1) * BATCH * G)
                        flat = imp[:].rearrange("p t g j -> p (t g) j")
                        for a in pairs:
                            dve.max(best[:, a, :], flat[:, a, :])
                        dve.drain()
                        for a in pairs:
                            dve.match_replace(left[:, a, :], best[:, a, :], flat[:, a, :], -3e38)
                        dve.drain()
                        dve.tensor_scalar(bias_q[:, at, :].rearrange("p t j -> p (t j)"),
                                          left[:, pairs[0]:pairs[-1] + 1, :].rearrange("p a j -> p (a j)"),
                                          -3e38, NEG, ALU.not_equal, ALU.mult).then_inc(picked, 1)

                    shift(0)
                    for b in range(BATCHES):
                        if b + 1 < BATCHES:
                            shift(b + 1)
                        select(b)
                    dve.drain()

        with Pool_(nc, name + "S2") as b2:
            pT = b2.sb("pT", [P, 2, NH // 2, P])
            ps_sel = b2.ps("ps_sel", [G * NS, NT, P], BF16)
            ps_p = b2.ps("ps_p", [P, 2, NH // 2, P])
            ps_o = b2.ps("ps_o", [P, 2, NSA_W])
            sel_turned, p_turned, pT_ready = b2.sem("sel_turned"), b2.sems("p_turned"), b2.sems("pT_ready")
            o_done, o_taken = b2.sems("o_done"), b2.sems("o_taken")
            g_exp, g_gate = b2.sem("g_exp"), b2.sem("g_gate")
            with nc.Block() as block:
                @block.tensor
                def _(pe_):
                    for t in range(NT):
                        last = pe_.transpose(ps_sel[:, t, :], bias_q[:, t, :], keep.ident_b[:])
                    last.then_inc(sel_turned, 1)

                    def turn(t):
                        u = t % 2
                        if t >= 2:
                            pe_.wait_ge(pT_ready[u], t // 2)
                        for a in range(NH // 2):
                            last = pe_.transpose(ps_p[:, u, a, :], pc[:, t, 2 * a:2 * a + 2, :], cst.ident[:])
                        last.then_inc(p_turned[u], 1)

                    turn(0)
                    for t in range(NT):
                        u = t % 2
                        if t + 1 < NT:
                            turn(t + 1)
                        pe_.wait_ge(pT_ready[u], t // 2 + 1)
                        if t >= 2:
                            pe_.wait_ge(o_taken[u], t // 2)
                        for a in range(NH // 2):
                            last = pe_.matmul(ps_o[:, u, a * P:(a + 1) * P], pT[:, u, a, :], keep.v_cmp[:, 2 * a // R, :],
                                              start=True, stop=True)
                        last.then_inc(o_done[u], 1)

                @block.scalar
                def _(act):
                    act.activation(keep.gate[:], keep.gate[:], ACT.Exp, scale=-1.0).then_inc(g_exp, 1)
                    for t in range(NT):
                        act.wait_ge(p_turned[t % 2], t // 2 + 1)
                        if t >= 2:
                            act.wait_ge(o_done[t % 2], t // 2)
                        act.activation(pT[:, t % 2, :, :], ps_p[:, t % 2, :, :], ACT.Copy).then_inc(pT_ready[t % 2], 1)

                @block.vector
                def _(dve):
                    dve.wait_ge(g_exp, 1)
                    dve.tensor_scalar(keep.gate[:], keep.gate[:], 1.0, None, ALU.add)
                    dve.drain()
                    dve.reciprocal(keep.gate[:], keep.gate[:])
                    dve.wait_ge(sel_turned, 1)
                    dve.tensor_copy(keep.selT[:], ps_sel[:])
                    dve.drain()
                    for t in range(NT):
                        dve.wait_ge(o_done[t % 2], t // 2 + 1)
                        g_cmp = keep.gate[:, t, :].rearrange("p (h b) -> p h b", b=N_BRANCH)[:, :, 0]
                        dve.tensor_tensor(keep.o[:, t, :].rearrange("p (h d) -> p h d", d=HD),
                                          ps_o[:, t % 2, :].rearrange("p (h d) -> p h d", d=HD),
                                          g_cmp.unsqueeze(2).to_broadcast([P, NH, HD]), ALU.mult).then_inc(o_taken[t % 2], 1)
                    dve.drain()


def sparse_attend(nc, name, cst, keep, y_out):
    FAR = WINDOW // P
    SELB, WINB = 0, 1
    units = []
    order = list(range(NT - 1, -1, -1))
    for t in order:
        for h in range(NH):
            units.append((t, h, SELB, 0, t + 1))
            first = max(0, t - FAR)
            units.append((t, h, WINB, first, t + 1 - first))
    PIECE = COLS // P
    pieces = [[(a, min(PIECE, n - a)) for a in range(0, n, PIECE)] for *_, n in units]
    with Pool_(nc, name) as m:
        prob = m.sb("prob", [P, 2, S])
        probT = m.sb("probT", [P, 2, NT, P])
        low = m.sb("low", [P, 4])
        mass = m.sb("mass", [P, 2, 2, NH])
        coef = m.sb("coef", [P, 2])
        ps_s = m.ps("ps_s", [P, 2, S])
        ps_t = m.ps("ps_t", [P, 2, COLS])
        ps_o = m.ps("ps_o", [P, 2, 2, COLS // 2])
        scored, lowest, exped, turned, turned_out, valued = (
            m.sem(n) for n in ("scored", "lowest", "exped", "turned", "turned_out", "valued"))
        head_mixed, stored = m.sem("head_mixed"), m.sem("stored")
        n_pieces = [0]
        for p in pieces:
            n_pieces.append(n_pieces[-1] + len(p))

        with nc.Block() as block:
            @block.tensor
            def _(pe):
                def score(n):
                    t, h, b, first, tiles = units[n]
                    s, g = n % 2, h // R
                    if n >= 2:
                        pe.wait_ge(exped, n - 1)
                    for a, k in pieces[n]:
                        keys = slice((first + a) * P, (first + a + k) * P)
                        out = ps_s[:, s, a * P:(a + k) * P]
                        masks = []
                        if first + a + k == t + 1:
                            masks.append((k - 1, keep.masks[:, 0:P]))
                        if b == WINB and first == t - FAR and a == 0:
                            masks.append((0, keep.masks[:, P:2 * P]))
                        for j, (at, mask) in enumerate(masks):
                            pe.matmul(ps_s[:, s, (a + at) * P:(a + at + 1) * P], keep.ident_b[:], mask,
                                      start=(j == 0), stop=False, skip_group_check=True)
                        if b == SELB:
                            pe.matmul(out, keep.selT[:, t, :], keep.picks[:, g * S + keys.start:g * S + keys.stop],
                                      start=not masks, stop=False, skip_group_check=True)
                        last = pe.matmul(out, keep.qT[0:QR, t * NH + h, :], keep.kT[0:QR, b, g, keys],
                                         start=(b == WINB and not masks), stop=True, skip_group_check=True)
                    last.then_inc(scored, 1)

                def turn(n):
                    pe.wait_ge(exped, n + 1)
                    for j, (a, k) in enumerate(pieces[n]):
                        q = n_pieces[n] + j
                        if q >= 2:
                            pe.wait_ge(turned_out, q - 1)
                        for i in range(k):
                            last = pe.transpose(ps_t[:, q % 2, i * P:(i + 1) * P],
                                                prob[:, n % 2, (a + i) * P:(a + i + 1) * P], cst.ident[:])
                        last.then_inc(turned, 1)

                def value(n):
                    t, h, b, first, tiles = units[n]
                    pe.wait_ge(turned_out, n_pieces[n + 1])
                    if b == 0 and n >= 4:
                        pe.wait_ge(head_mixed, n // 2 - 1)
                    g = h // R
                    for i in range(tiles):
                        last = pe.matmul(ps_o[:, h % 2, b, 0:HD], probT[:, n % 2, i, :],
                                         keep.v[:, first + i, b, g * HD:(g + 1) * HD], start=(i == 0), stop=(i == tiles - 1))
                    last.then_inc(valued, 1)

                warm_up(pe, ps_t[:, 0, :], keep.ident_b[:], keep.masks[:, 0:COLS])
                score(0)
                score(1)
                for n in range(len(units)):
                    if n + 2 < len(units):
                        score(n + 2)
                    if n:
                        value(n - 1)
                    turn(n)
                value(len(units) - 1)

            def take(eng, copy, n, j):
                a, k = pieces[n][j]
                q = n_pieces[n] + j
                eng.wait_ge(turned, q + 1)
                if n >= 2:
                    eng.wait_ge(valued, n - 1)
                eng.wait_ge(turned_out, q)
                copy(probT[:, n % 2, a:a + k, :], ps_t[:, q % 2, 0:k * P]).then_inc(turned_out, 1)

            @block.scalar
            def _(act):
                def exps(n):
                    t, h, b, first, tiles = units[n]
                    act.wait_ge(lowest, n + 1)
                    if n >= 2:
                        act.wait_ge(turned, n_pieces[n - 1])
                    if h == 0 and b == 0 and order.index(t) >= 2:
                        act.wait_ge(head_mixed, NH * (order.index(t) - 1))
                    act.activation(prob[:, n % 2, 0:tiles * P], ps_s[:, n % 2, 0:tiles * P], ACT.Exp,
                                   bias=low[:, n % 4:n % 4 + 1], accum_out=mass[:, t % 2, b, h:h + 1]).then_inc(exped, 1)

                exps(0)
                for n in range(len(units)):
                    if n + 1 < len(units):
                        exps(n + 1)
                    if len(pieces[n]) > 1:
                        take(act, lambda o, i: act.activation(o, i, ACT.Copy), n, 1)

            @block.vector
            def _(dve):
                def maximum(n):
                    tiles = units[n][-1]
                    dve.wait_ge(scored, n + 1)
                    if n >= 4:
                        dve.wait_ge(exped, n - 3)
                    dve.tensor_reduce(low[:, n % 4:n % 4 + 1], ps_s[:, n % 2, 0:tiles * P], X, ALU.max, negate=True
                                      ).then_inc(lowest, 1)

                def mix(n):
                    t, h = units[n][:2]
                    o_h = keep.o[:, t, h * HD:(h + 1) * HD]
                    dve.wait_ge(valued, n + 2)
                    dve.reciprocal(coef[:], mass[:, t % 2, :, h])
                    dve.drain()
                    dve.tensor_tensor(coef[:], coef[:], keep.gate[:, t, h * N_BRANCH + 1:(h + 1) * N_BRANCH], ALU.mult)
                    for b in range(2):
                        dve.drain()
                        last = dve.scalar_tensor_tensor(o_h, ps_o[:, h % 2, b, 0:HD], coef[:, b:b + 1], o_h,
                                                        ALU.mult, ALU.add)
                    last.then_inc(head_mixed, 1)
                    dve.drain()

                maximum(0)
                maximum(1)
                for n in range(len(units)):
                    if n + 2 < len(units):
                        maximum(n + 2)
                    take(dve, lambda o, i: dve.tensor_copy(o, i), n, 0)
                    if n >= 2 and n % 2 == 0:
                        mix(n - 2)
                mix(len(units) - 2)

            @block.sync
            def _(sp):
                for n, t in enumerate(order):
                    sp.wait_ge(head_mixed, NH * (n + 1))
                    sp.dma_start(y_out[t * P:(t + 1) * P, RET_W:RET_W + NSA_W], keep.o[:, t, :]).then_inc(stored, 16)
                sp.wait_ge(stored, 16 * NT)


def sparse_constants(con):
    f = np.float32
    slopes = f(2) ** (f(-8) * np.arange(1, NH + 1, dtype=f) / f(NH))
    tok = np.arange(S).reshape(NT, P).T
    j = np.arange(NS)
    away = (SEL * j[None, None, :] - tok[:, :, None]).astype(f)
    rows = np.concatenate([slopes[None, None, :, None] * away[:, :, None, :],
                           np.broadcast_to(slopes[None, None, :, None], (P, NT, NH, 1))], axis=3)
    con["q_rows"] = rows.reshape(P, -1)

    def key_rows(at):
        return np.concatenate([(at[None, :] // SEL == j[:, None]), (at % SEL)[None, :] * (at < S)[None, :]], axis=0)
    con["key_rows"] = key_rows(np.arange(S))
    con["cmp_rows"] = key_rows(np.arange(NC_) * CMP_STRIDE + 2 * CMP_STRIDE - 1)
    q_block = tok[:, :, None] // SEL
    forced = (j == 0) | (j == q_block) | (j == q_block - 1)
    con["forced"] = np.where(forced, 1e3, np.where(SEL * j <= tok[:, :, None], 0.0, -1e3)).reshape(P, -1)
    p = np.arange(P)
    causal = np.where(p[None, :] <= p[:, None], 0.0, NEG)
    far = np.where(p[None, :] > p[:, None], 0.0, NEG)
    cmp_end = np.arange(NC_) * CMP_STRIDE + 2 * CMP_STRIDE - 1
    c_mask = np.where(cmp_end[None, None, :] <= tok[:, :, None], 0.0, NEG).reshape(P, -1)
    con["masks"] = np.concatenate([causal, far, c_mask], axis=1)
    picks = np.zeros((G, NS, G, S))
    for g in range(G):
        picks[g, :, g, :] = np.arange(S)[None, :] // SEL == j[:, None]
    con["picks"] = picks.reshape(G * NS, G * S)
    return {k: np.ascontiguousarray(v, dtype=f) for k, v in con.items()}


class Kept:

    def __init__(self, m):
        self.v = m.sb("v", [P, NT, 2, KV_W])
        self.gate = m.sb("gate", [P, NT, NH * N_BRANCH])
        self.kT = m.sb("kT", [QR, 2, G, S])
        self.kcT = m.sb("kcT", [QR, G, NC_])
        self.qT = m.sb("qT", [QR, NT * NH, P])
        self.forced = m.sb("forced", [P, NT, NS])
        self.masks = m.sb("masks", [P, 2 * P + NT * NC_], BF16)
        self.picks = m.sb("picks", [G * NS, G * S], BF16)
        self.ident_b = m.sb("ident_b", [P, P], BF16)
        self.v_cmp = m.sb("v_cmp", [P, G, 2 * HD])
        self.selT = m.sb("selT", [G * NS, NT, P], BF16)
        self.o = m.sb("o", [P, NT, NSA_W])


def trunk(nc, a, con, out):
    ctx = ExitStack()
    with ctx:
        def dram(name, shape, dt=F32):
            return nc.dram_tensor(name, shape, dt).ap()

        proj = dram("proj", [S, IN_W])
        mixer = dram("mixer", [S, D])
        stream = [dram(f"stream{j}", [S, D]) for j in range(3)]
        xn = dram("xn", [S, D])
        table = dram("table", [NE * CAP, 2], I32)
        slots = dram("slots", [2 * S, D])

        with Pool_(nc, "all", whole=True) as top:
            cst = Constants(top)
            gates = top.sb("gates", [P, 2 * NT])
            most = top.sb("most", [P, 1], I32)
            with nc.Block() as block:
                constants(nc, cst, block)

            def moe(layer, src):
                with Pool_(nc, f"experts{layer}") as held:
                    data = ExpertData(held, a["moe_w_gate"][layer, :, :, :], a["moe_w_up"][layer, :, :, :],
                                      a["moe_w_down"][layer, :, :, :])
                    with Pool_(nc, f"moe{layer}", clear=False) as m:
                        lg = m.sb("lg", [P, NT, NG + NE])
                        norm_and_logits(nc, f"fn{layer}", src, a["ffn_norm_g"][layer, :], a["moe_wg_group"][layer, :, :],
                                        a["moe_bg_group"][layer, :], a["moe_wg_expert"][layer, :, :],
                                        a["moe_bg_expert"][layer, :], xn, lg, table, data, cst.ident)
                        route(nc, f"rt{layer}", lg, gates, most, data, cst)
                    experts(nc, f"ex{layer}", xn, data, table, slots, most, cst.ident)

            with Pool_(nc, "in") as m:
                xT_hi, xT_lo = m.sb("xT_hi", [P, KT, S], F32R), m.sb("xT_lo", [P, KT, S], F32R)
                ahead = FirstWeights(m, a["ev_w_in"][0, :, :])
                norm_transpose(nc, "mn0", a["x"][0, :, :], cst.ident, xT_hi, xT_lo, gain=a["mix_norm_g"][0, :],
                               ahead=ahead)
                project(nc, "in0", xT_hi, xT_lo, a["ev_w_in"][0, :, :], IN_W, proj, ahead)
            with Pool_(nc, "mix0") as m:
                keep = Kept(m)
                with Pool_(nc, "raw") as raw:
                    keep.kvc2 = raw.sb("kvc2", [P, 2, NT, G, 2, HD])
                    retention_and_rows(nc, "ret", proj, a["ev_ret_norm_g"][0, :], a["ev_q_norm_g"][0, :],
                                       a["ev_k_norm_g"][0, :, :], cst, con, keep, mixer)
                    sparse_prepare(nc, "prep", a["ev_k_norm_g"][0, :, :], a["ev_cmp_pe"][0, :, :, :],
                                   a["ev_w_cmp1"][0, :, :, :], a["ev_w_cmp2"][0, :, :, :], cst, keep)
                sparse_attend(nc, "att", cst, keep, mixer)
            with Pool_(nc, "out") as m:
                xT_hi, xT_lo = m.sb("xT_hi", [P, KT, S], F32R), m.sb("xT_lo", [P, KT, S], F32R)
                ahead = FirstWeights(m, a["ev_w_out"][0, :, :])
                norm_transpose(nc, "tr0", mixer, cst.ident, xT_hi, xT_lo, ahead=ahead)
                project(nc, "out0", xT_hi, xT_lo, a["ev_w_out"][0, :, :], D, stream[0], ahead,
                        residual=a["x"][0, :, :])
            moe(0, stream[0])

            with Pool_(nc, "odd") as m:
                zT_hi, zT_lo = m.sb("zT_hi", [P, KT, S], F32R), m.sb("zT_lo", [P, KT, S], F32R)
                ahead = FirstWeights(m, a["od_w_out"][0, :, :])
                with Pool_(nc, "oddx") as x:
                    xT_hi, xT_lo = x.sb("xT_hi", [P, KT, S], F32R), x.sb("xT_lo", [P, KT, S], F32R)
                    norm_transpose(nc, "mn1", stream[0], cst.ident, xT_hi, xT_lo, gain=a["mix_norm_g"][1, :],
                                   mix=(slots, gates, stream[1]))
                    gated_conv(nc, "conv", xT_hi, xT_lo, a["od_w_in"][0, :, :], a["od_conv_w"][0, :, :],
                               a["od_conv_b"][0, :], zT_hi, zT_lo, ahead)
                project(nc, "out1", zT_hi, zT_lo, a["od_w_out"][0, :, :], D, stream[2], ahead, residual=stream[1])
            moe(1, stream[2])
            finish(nc, "end", stream[2], slots, gates, out)


def finish(nc, name, src, slots, gates, out):
    with Pool_(nc, name) as m:
        rows = m.sb("rows", [P, NT, D])
        ya = m.sb("ya", [P, 2, 2, D])
        loaded, mixed, stored = m.sems("loaded", NT), m.sem("mixed"), m.sem("stored")
        with nc.Block() as block:
            @block.sync
            def _(sp):
                for t in range(NT):
                    sp.dma_start(rows[:, t, :], src[t * P:(t + 1) * P, :]).then_inc(loaded[t], 16)
                    if t >= 2:
                        sp.wait_ge(mixed, t - 1)
                    for c in range(2):
                        at = c * S + t * P
                        sp.dma_start(ya[:, t % 2, c, :], slots[at:at + P, :]).then_inc(loaded[t], 16)

            @block.vector
            def _(dve):
                for t in range(NT):
                    dve.wait_ge(loaded[t], 48)
                    for c in range(2):
                        last = dve.scalar_tensor_tensor(rows[:, t, :], ya[:, t % 2, c, :],
                                                        gates[:, c * NT + t:c * NT + t + 1], rows[:, t, :], ALU.mult, ALU.add)
                        if c == 0:
                            dve.drain()
                    last.then_inc(mixed, 1)

            @block.scalar
            def _(act):
                for t in range(NT):
                    act.wait_ge(mixed, t + 1)
                    act.dma_start(out[t * P:(t + 1) * P, :], rows[:, t, :]).then_inc(stored, 16)
                act.wait_ge(stored, 16 * NT)


class Constants:
    def __init__(self, m):
        self.ident, self.ones, self.before = (m.sb(n, [P, P]) for n in ("ident", "ones", "before"))
        self.iota, self.iota_i = m.sb("iota", [P, 64]), m.sb("iota_i", [P, 64], I32)


INPUTS = ["x", "mix_norm_g", "ffn_norm_g", "ev_w_in", "ev_cmp_pe", "ev_w_cmp1", "ev_w_cmp2", "ev_q_norm_g", "ev_k_norm_g",
          "ev_ret_norm_g", "ev_w_out", "od_w_in", "od_conv_w", "od_conv_b", "od_w_out", "moe_wg_group", "moe_bg_group",
          "moe_wg_expert", "moe_bg_expert", "moe_w_gate", "moe_w_up", "moe_w_down"]


def kernel(**inputs):
    import concourse.bacc as bacc
    from concourse.bass_utils import run_bass_kernel_spmd

    nc = bacc.Bacc("TRN2", target_bir_lowering=False, num_devices=1)
    arrays = {}

    def given(name, array):
        arrays[name] = np.ascontiguousarray(array)
        return nc.dram_tensor(name, array.shape, mybir.dt.from_np(arrays[name].dtype), kind="ExternalInput").ap()

    a = {n: given(f"in_{n}", np.asarray(inputs[n])) for n in INPUTS}
    con = {n: given(f"con_{n}", v) for n, v in sparse_constants(shape_constants()).items()}
    out = nc.dram_tensor("out", (1, S, D), F32, kind="ExternalOutput").ap()
    trunk(nc, a, con, out[0, :, :])
    r = run_bass_kernel_spmd(nc, [arrays], core_ids=[0])
    return np.asarray(r.results[0]["out"])
```
